# Optimizing a Trainium2 kernel written in Bass

```python
import math
import jax, jax.numpy as jnp
from jax import lax
import numpy as np

D_MODEL = 1024
BATCH = 1
SEQ = 256
DEPTH = 2
DEC_BATCH = 8
DEC_SEQ = 8
PAST_LEN = 2048
PAGE_SIZE = 128

CHUNK = 128
D_A = D_MODEL // 2
CH_A = 128
G_A = D_A // CH_A
D_B = D_MODEL // 2
EXPAND_B = 128
H_B = D_B // EXPAND_B
DK_B = EXPAND_B
DV_B = D_B // H_B
HGRN_CHUNK = 64
SPLITS = [D_A, D_A, D_B, D_B, D_B, D_B, D_MODEL, D_MODEL]
IN_COLS = sum(SPLITS)
D_FF = ((8 * D_MODEL // 3 + 127) // 128) * 128
N_EXPERTS = 8
TOP_K = 2
N_DENSE = (DEPTH + 1) // 2
N_MOE = DEPTH // 2
EPS = 1e-6

kernel_name = "gmlp_hgrn2_gated_hybrid_step"

def rms_norm(x, g):
    xf = x.astype(jnp.float32)
    y = xf * lax.rsqrt(jnp.mean(xf * xf, axis=-1, keepdims=True) + EPS)
    return (y * g.astype(jnp.float32)).astype(x.dtype)

def layer_norm(x, g, b):
    xf = x.astype(jnp.float32)
    mu = jnp.mean(xf, axis=-1, keepdims=True)
    xc = xf - mu
    y = xc * lax.rsqrt(jnp.mean(xc * xc, axis=-1, keepdims=True) + EPS)
    return (y * g.astype(jnp.float32) + b.astype(jnp.float32)).astype(x.dtype)

def chunk_spatial_gate(u, v, w_s, b_s):
    bsz, L, _ = v.shape
    n = -(-L // CHUNK)
    pad = n * CHUNK - L
    vp = jnp.pad(v, ((0, 0), (0, pad), (0, 0))).reshape(bsz, n, CHUNK, G_A, CH_A)
    w = w_s * jnp.tril(jnp.ones((CHUNK, CHUNK), w_s.dtype))
    mixed = jnp.einsum('gts,bnsgc->bntgc', w, vp) + b_s.T[None, None, :, :, None]
    mixed = mixed.reshape(bsz, n * CHUNK, D_A)[:, :L]
    return u * mixed

def hgrn2_recurrence(q, logf, k, v, s0):
    bsz, L, H, _ = q.shape
    DV = v.shape[-1]
    C = math.gcd(L, HGRN_CHUNK)
    n = L // C

    def to_chunks(t):
        return t.reshape(bsz, n, C, H, t.shape[-1]).swapaxes(0, 1)

    causal = jnp.tril(jnp.ones((C, C), bool))[None, :, :, None, None]

    def step(S, inp):
        qc, gc, kc, vc = inp
        G = jnp.cumsum(gc, axis=1)
        o_inter = jnp.einsum('bthd,bhdv->bthv', qc * jnp.exp(G), S)
        decay = jnp.exp(jnp.where(causal, G[:, :, None] - G[:, None, :], -jnp.inf))
        scores = jnp.einsum('bthd,bshd,btshd->bhts', qc, kc, decay)
        o_intra = jnp.einsum('bhts,bshv->bthv', scores, vc)
        G_last = G[:, -1]
        k_dec = kc * jnp.exp(G_last[:, None] - G)
        S = jnp.exp(G_last)[..., None] * S + jnp.einsum('bshd,bshv->bhdv', k_dec, vc)
        return S, o_inter + o_intra

    S, o = lax.scan(step, s0, (to_chunks(q), to_chunks(logf), to_chunks(k), to_chunks(v)))
    return o.swapaxes(0, 1).reshape(bsz, L, H, DV), S

def token_mixer(xn, s0, lb, w_in, ln_v_g, ln_v_b, w_spatial, b_spatial, hgrn_norm_g,
                w_branch_a, w_branch_b, w_out):
    bsz, L, _ = xn.shape
    z = xn @ w_in
    cuts = list(np.cumsum(SPLITS)[:-1])
    u, v, q, fz, iz, gz, gate_a, gate_b = jnp.split(z, cuts, axis=-1)
    u = jax.nn.gelu(u, approximate=False)
    v = layer_norm(jax.nn.gelu(v, approximate=False), ln_v_g, ln_v_b)
    a = chunk_spatial_gate(u, v, w_spatial, b_spatial)
    logf = jnp.logaddexp(jnp.log(lb), jnp.log1p(-lb) + jax.nn.log_sigmoid(fz.astype(jnp.float32)))
    kf = -jnp.expm1(logf)
    qf = jax.nn.silu(q.astype(jnp.float32))
    shp = (bsz, L, H_B, DK_B)
    o, s_new = hgrn2_recurrence(qf.reshape(shp), logf.reshape(shp), kf.reshape(shp),
                                iz.astype(jnp.float32).reshape(bsz, L, H_B, DV_B), s0)
    o = o * lax.rsqrt(jnp.mean(o * o, axis=-1, keepdims=True) + EPS)
    o = o * hgrn_norm_g.astype(jnp.float32).reshape(H_B, DV_B)
    b = o.reshape(bsz, L, D_B).astype(xn.dtype) * jax.nn.silu(gz)
    merged = jax.nn.sigmoid(gate_a) * (a @ w_branch_a) + jax.nn.sigmoid(gate_b) * (b @ w_branch_b)
    return merged @ w_out, s_new, v

def swiglu(h, w_gate, w_up, w_down):
    return (jax.nn.silu(h @ w_gate) * (h @ w_up)) @ w_down

def moe_swiglu(h, router_w, w_gate, w_up, w_down):
    logits = (h @ router_w).astype(jnp.float32)
    top_v, top_i = lax.top_k(logits, TOP_K)
    gates = jax.nn.softmax(top_v, axis=-1)
    combine = jnp.sum(jax.nn.one_hot(top_i, N_EXPERTS, dtype=jnp.float32) * gates[..., None], axis=-2)
    combine = combine.astype(h.dtype)
    out = jnp.zeros_like(h)
    for e in range(N_EXPERTS):
        out = out + combine[..., e:e + 1] * swiglu(h, w_gate[e], w_up[e], w_down[e])
    return out

def trunk(x, s_in, collect_rows, params):
    (norm_mix_g, w_in, ln_v_g, ln_v_b, w_spatial, b_spatial, lower_bounds, hgrn_norm_g,
     w_branch_a, w_branch_b, w_out, norm_ffn_g, dense_w_gate, dense_w_up, dense_w_down,
     router_w, moe_w_gate, moe_w_up, moe_w_down, final_norm_g) = params
    lb_cum = jnp.cumsum(jax.nn.softmax(lower_bounds.astype(jnp.float32), axis=0), axis=0)
    lb_all = lb_cum - lb_cum[0:1]
    h = x
    states, rows = [], []
    for l in range(DEPTH):
        mix, s_new, v = token_mixer(rms_norm(h, norm_mix_g[l]), s_in[l], lb_all[l], w_in[l],
                                    ln_v_g[l], ln_v_b[l], w_spatial[l], b_spatial[l],
                                    hgrn_norm_g[l], w_branch_a[l], w_branch_b[l], w_out[l])
        h = h + mix
        hn = rms_norm(h, norm_ffn_g[l])
        if l % 2 == 0:
            i = l // 2
            h = h + swiglu(hn, dense_w_gate[i], dense_w_up[i], dense_w_down[i])
        else:
            i = l // 2
            h = h + moe_swiglu(hn, router_w[i], moe_w_gate[i], moe_w_up[i], moe_w_down[i])
        states.append(s_new)
        if collect_rows:
            rows.append(v)
    y = rms_norm(h, final_norm_g)
    new_rows = jnp.stack(rows) if collect_rows else None
    return y, jnp.stack(states), new_rows

def setup_inputs(seed: int = 0) -> dict:
    key = jax.random.key(seed)
    ks = jax.random.split(key, 24)
    f32 = jnp.float32

    def nrm(k, shape, scale):
        return jax.random.normal(k, shape, f32) * scale

    def gain(k, shape):
        return 1.0 + 0.05 * jax.random.normal(k, shape, f32)

    return {
        "x_prompt": nrm(ks[0], (BATCH, SEQ, D_MODEL), 1.0),
        "x_sample": nrm(ks[1], (DEC_BATCH, DEC_SEQ, D_MODEL), 1.0),
        "state_hgrn": nrm(ks[2], (DEPTH, DEC_BATCH, H_B, DK_B, DV_B), 0.5),
        "norm_mix_g": gain(ks[3], (DEPTH, D_MODEL)),
        "w_in": nrm(ks[4], (DEPTH, D_MODEL, IN_COLS), D_MODEL ** -0.5),
        "ln_v_g": gain(ks[5], (DEPTH, D_A)),
        "ln_v_b": nrm(ks[6], (DEPTH, D_A), 0.02),
        "w_spatial": nrm(ks[7], (DEPTH, G_A, CHUNK, CHUNK), CHUNK ** -0.5),
        "b_spatial": gain(ks[8], (DEPTH, G_A, CHUNK)),
        "lower_bounds": nrm(ks[9], (DEPTH, D_B), 0.5),
        "hgrn_norm_g": gain(ks[10], (DEPTH, D_B)),
        "w_branch_a": nrm(ks[11], (DEPTH, D_A, D_MODEL), D_A ** -0.5),
        "w_branch_b": nrm(ks[12], (DEPTH, D_B, D_MODEL), D_B ** -0.5),
        "w_out": nrm(ks[13], (DEPTH, D_MODEL, D_MODEL), D_MODEL ** -0.5),
        "norm_ffn_g": gain(ks[14], (DEPTH, D_MODEL)),
        "dense_w_gate": nrm(ks[15], (N_DENSE, D_MODEL, D_FF), D_MODEL ** -0.5),
        "dense_w_up": nrm(ks[16], (N_DENSE, D_MODEL, D_FF), D_MODEL ** -0.5),
        "dense_w_down": nrm(ks[17], (N_DENSE, D_FF, D_MODEL), D_FF ** -0.5),
        "router_w": nrm(ks[18], (N_MOE, D_MODEL, N_EXPERTS), D_MODEL ** -0.5),
        "moe_w_gate": nrm(ks[19], (N_MOE, N_EXPERTS, D_MODEL, D_FF), D_MODEL ** -0.5),
        "moe_w_up": nrm(ks[20], (N_MOE, N_EXPERTS, D_MODEL, D_FF), D_MODEL ** -0.5),
        "moe_w_down": nrm(ks[21], (N_MOE, N_EXPERTS, D_FF, D_MODEL), D_FF ** -0.5),
        "final_norm_g": gain(ks[22], (D_MODEL,)),
    }

def reference(x_prompt, x_sample, state_hgrn, norm_mix_g, w_in, ln_v_g, ln_v_b, w_spatial,
              b_spatial, lower_bounds, hgrn_norm_g, w_branch_a, w_branch_b, w_out, norm_ffn_g,
              dense_w_gate, dense_w_up, dense_w_down, router_w, moe_w_gate, moe_w_up,
              moe_w_down, final_norm_g):
    params = (norm_mix_g, w_in, ln_v_g, ln_v_b, w_spatial, b_spatial, lower_bounds, hgrn_norm_g,
              w_branch_a, w_branch_b, w_out, norm_ffn_g, dense_w_gate, dense_w_up, dense_w_down,
              router_w, moe_w_gate, moe_w_up, moe_w_down, final_norm_g)
    s_zero = jnp.zeros((DEPTH, x_prompt.shape[0], H_B, DK_B, DV_B), jnp.float32)
    y_prompt, s_prompt, _ = trunk(x_prompt, s_zero, False, params)
    y_sample, s_sample, v_rows = trunk(x_sample, state_hgrn.astype(jnp.float32), True, params)
    new_state_hgrn_prompt = s_prompt.astype(x_prompt.dtype)
    new_state_hgrn_sample = s_sample.astype(state_hgrn.dtype)
    new_state_chunk_v_sample = v_rows
    return (y_prompt, y_sample, new_state_hgrn_prompt, new_state_hgrn_sample, new_state_chunk_v_sample)


_drawn_inputs = setup_inputs


def setup_inputs(seed=0):
    import zlib

    import numpy as np

    out = dict(_drawn_inputs(seed))
    spreads = {}
    factors = {}
    for name, (base, spread) in spreads.items():
        noise = np.random.default_rng([zlib.crc32(name.encode()), seed]).standard_normal(out[name].shape)
        drawn = base * np.exp(spread * noise) if base else spread * noise
        out[name] = __import__('jax').numpy.asarray(drawn.astype(out[name].dtype))
    for name, factor in factors.items():
        out[name] = (out[name] * factor).astype(out[name].dtype)
    return out
```

```python
import concourse.bass as bass
from concourse import mybir
from contextlib import ExitStack


def hybrid_trunk_program(nc, A, OUT):
    F = mybir.dt.float32
    R = mybir.dt.float32r
    I32 = mybir.dt.int32
    U32 = mybir.dt.uint32
    ALU = mybir.AluOpType
    ACT = mybir.ActivationFunctionType

    D = A["x_prompt"].shape[2]
    TP = A["x_prompt"].shape[1]
    NSEQ, LS = A["x_sample"].shape[0], A["x_sample"].shape[1]
    T = TP + NSEQ * LS
    LAYERS = A["w_in"].shape[0]
    KD = D // 128
    DA = A["ln_v_g"].shape[1]
    H = DA // 128
    FF = A["dense_w_gate"].shape[2]
    KF = FF // 128
    NE = A["router_w"].shape[2]
    TOK = [(0, 128), (128, 128), (256, 64)]
    NT = len(TOK)
    CH = 64
    NPC = TP // CH
    PAIRS = TP // 128
    EPS = 1e-6
    LEVELS = [32, 16, 8, 4, 2, 1]
    COL = {"u": 0, "v": DA, "q": 2 * DA, "forget": 3 * DA, "value": 4 * DA, "out_gate": 5 * DA,
           "gate_a": 6 * DA, "gate_b": 6 * DA + D}

    CHUNK = 2048
    SLOTS = 3
    BANKS = 4
    chunks = []
    mark_after = []
    tile = {}
    first_chunk = {}
    order = []
    marks = 0
    emptied = {"act": 0, "dve": 0}

    def rows(w, k0, kt, c0, cols):
        return w[k0 * 128:(k0 + kt) * 128, c0:c0 + cols].rearrange("(k p) n -> p k n", p=128)

    def add_chunk(key, src, kt, cols, opens, closes, by):
        nonlocal marks
        first_chunk.setdefault(key[:2], len(chunks))
        for t in opens:
            n = len(order)
            order.append((key[0], key[1], t))
            tile[order[-1]] = [n % BANKS, None, by, None, order[n - BANKS] if n >= BANKS else None]
        for t in closes:
            marks += 1
            emptied[by] += 1
            tile[(key[0], key[1], t)][1] = marks
            tile[(key[0], key[1], t)][3] = emptied[by]
        if not closes:
            marks += 1
        chunks.append((src, kt, cols))
        mark_after.append(marks)

    MIX = [("forget", 0), ("forget", 1), ("q", 0), ("q", 1), ("value", 0), ("value", 1), ("v", 0), ("v", 1),
           ("u", 0), ("u", 1)] + [("gate_a", i) for i in range(4)] + [("branch_a", 0), ("branch_a", 1),
           ("out_gate", 0), ("out_gate", 1)] + [("gate_b", i) for i in range(4)] + [
           ("branch_b", 0), ("branch_b", 1)] + [("w_out", i) for i in range(4)]
    KCUT = [(0, 8), (8, 8), (16, KF - 16)]
    FFN = [(s, i) for i in range(KF // 2) for s in ("gate", "up")] + \
          [("down", 3 * i + j) for i in range(4) for j in range(3)]
    for L in range(LAYERS):
        for sec, i in MIX:
            if sec in ("value", "v"):
                add_chunk((L, sec), rows(A["w_in"][L], 4 * i, 4, COL[sec], DA), 4, DA,
                          range(NT) if i == 0 else (), () if i == 0 else range(NT), "act")
            elif sec in ("branch_a", "branch_b"):
                w = A["w_" + sec][L]
                add_chunk((L, sec), rows(w, 0, H, 512 * i, 512), H, 512,
                          range(4 * i, 4 * i + 4), range(4 * i, 4 * i + 4), "dve")
            elif sec == "w_out":
                add_chunk((L, sec), rows(A["w_out"][L], 0, KD, 256 * i, 256), KD, 256,
                          (2 * i, 2 * i + 1), (2 * i, 2 * i + 1), "dve")
            else:
                add_chunk((L, sec), rows(A["w_in"][L], 0, KD, COL[sec] + 256 * i, 256), KD, 256,
                          (2 * i, 2 * i + 1), (2 * i, 2 * i + 1), "act")
        if L % 2 == 0:
            for sec, i in FFN:
                if sec == "down":
                    k0, kt = KCUT[i % 3]
                    ts = (2 * (i // 3), 2 * (i // 3) + 1)
                    add_chunk((L, sec), rows(A["dense_w_down"][L // 2], k0, kt, 256 * (i // 3), 256), kt, 256,
                              ts if i % 3 == 0 else (), ts if i % 3 == 2 else (), "dve")
                else:
                    add_chunk((L, sec), rows(A["dense_w_" + sec][L // 2], 0, KD, 256 * i, 256), KD, 256,
                              (2 * i, 2 * i + 1), (2 * i, 2 * i + 1), "act" if sec == "gate" else "dve")
    NDENSE = len(chunks)
    assert NDENSE % SLOTS == 0

    groups = [(512 * j, min(512, FF - 512 * j)) for j in range(-(-FF // 512))]
    ECH = []
    for j, (c0, cols) in enumerate(groups):
        for s in ("gate", "up"):
            kt = CHUNK // cols
            for part in range(KD // kt):
                ECH.append((s, j, part, part * kt, kt, c0, cols))
    for j in range(KF // 2):
        ECH.append(("down", j, 0, 2 * j, 2, 0, D))
    NEC = len(ECH)
    assert NEC % SLOTS == 0
    NG = len(groups)
    closing = {(s, j): max(i for i, x in enumerate(ECH) if x[0] == s and x[1] == j)
               for s in ("gate", "up") for j in range(NG)}
    CAP = 128

    at = [-(-nc.sbuf_base // 32) * 32]

    def place(name, shape, dt=F, offset=None):
        size = 4
        for s in shape[1:]:
            size *= s
        if offset is None:
            offset = at[0]
            at[0] += -(-size // 32) * 32
        return nc.alloc_sbuf_tensor_at(name, shape, dt, offset=offset)

    raw = place("weights_raw", [128, SLOTS, CHUNK])
    whi = place("weights_high", [128, SLOTS, CHUNK], R)
    wlo = place("weights_low", [128, SLOTS, CHUNK], R)
    h = place("residual", [128, KD, T])
    m_at = at[0]
    xn = place("normed_or_merged", [128, KD, T])
    xh_at = at[0]
    xh = place("moving_high", [128, KD, T], R)
    xl_at = at[0]
    xl = place("moving_low", [128, KD, T], R)
    ident = place("identity", [128, 128])
    ones = place("ones", [128, 128])
    upper = place("upper_ones", [128, 128])
    iota = place("iota_row", [128, 128])
    lmask = place("level_masks", [128, len(LEVELS) + 1, 128], I32)
    smask = place("scan_keep", [128, T])
    bmask = place("sequence_mask", [64, NSEQ])
    r8 = place("row_spread", [LS, NSEQ * LS])
    eps_t = place("eps", [128, 1])
    NROW = 2 * LAYERS * KD + 2 * LAYERS * H
    prow = place("param_rows", [NROW, 128])
    prm = place("param_columns", [128, NROW])
    lbt = place("lower_bound_terms", [128, 5, H])
    wsp = place("spatial_raw", [128, H, 128])
    wst = place("spatial_transposed", [128, H, 128])
    wsd = place("spatial_sample", [64, H, 64])
    bsp = place("spatial_bias", [128, H, 128])
    ln_at = at[0]
    lng = place("ln_gain", [128, DA])
    lnb = place("ln_shift", [128, DA])
    sq = place("squares", [128, 2, T])
    ssum = place("square_sum", [128, T])
    rinv = place("inverse_rms", [128, T])
    el = place("chunk_decay", [128, H, NPC + NSEQ])
    bst = place("ln_stats", [128, NT, 6])
    bag = place("ln_mean_var", [128, NT, 2])
    tmp = place("branch_product", [128, 2, T])
    cmb = place("combine", [128, NT, NE])
    slot = place("slot_of_token", [128, NT, NE])
    cslot = place("slot_now", [128, NT])
    cgate = place("gate_now", [128, NT])
    BLOCKS = -(-T // CAP)
    NMORE = (BLOCKS - 1) * NE
    full = place("more_blocks", [128, NMORE], I32)
    items = place("block_items", [128, NMORE], I32)
    fullf = place("more_blocks_f", [128, 3, NMORE])
    rw = place("router", [128, KD, NE])
    region = at[0]

    def later(name, shape, dt, offset):
        return place(name, shape, dt, offset)

    W5 = 4 * H * T
    ahi = later("a_high", [128, H, T], R, region)
    alo = later("a_low", [128, H, T], R, region + W5)
    gb = later("gate_b", [128, KD, T], F, region)
    o = region + 2 * W5
    u = later("u_or_out_gate", [128, H, T], F, o); o += W5
    V = later("value", [128, NT, DA], F, o); o += 4 * NT * DA
    vn_at = o
    vn = later("v_normed", [128, NT, DA], F, o)
    o += 4 * NT * DA
    sc = later("scores", [128, PAIRS, H, 128], F, o)
    scs = later("scores_sample", [64, H, 64], F, o + 4 * PAIRS * H * 128); o += 4 * PAIRS * H * 128 + 4 * H * 64
    z_at = o
    Z = later("level_product", [128, H, T], F, o); o += W5
    e_at = o
    E = later("level_decay", [128, H, T], F, o); o += W5
    Q = later("query", [128, H, T], F, o); o += W5
    k_at = o
    K = later("key", [128, H, T], F, o); o += W5
    g_at = o
    G = later("log_decay", [128, H, T], F, o); o += W5
    kdt = later("key_decayed_tok", [128, NT, DA], F, o)
    osq = later("out_squares", [128, H, T], F, o); o += 4 * NT * DA
    QE = later("query_decayed", [128, H, T], F, o); o += W5
    assert o <= nc.sbuf_usable_end, (o, nc.sbuf_usable_end)
    S12 = later("state_1_2", [128, 2, H, 128], F, e_at)
    S34 = later("state_3_4", [128, 2, H, 128], F, z_at)
    vex = later("value_by_sequence", [64, NSEQ, 128], F, k_at)
    s0 = [later("state_sample_even", [128, NSEQ, 128], F, g_at), later("state_sample_odd", [128, NSEQ, 128], F, e_at)]
    bhi = later("b_high", [128, H, T], R, k_at)
    blo = later("b_low", [128, H, T], R, g_at)
    xt = later("x_rows", [128, NT, D], F, z_at)
    fh = later("hidden_high", [128, KF, T], R, region)
    fl = later("hidden_low", [128, KF, T], R, region + 4 * KF * T)
    o = region + 8 * KF * T
    sg = later("silu_gate", [128, 2, T], F, o)
    hf = later("hidden", [128, 2, T], F, o + 8 * T)
    assert o + 16 * T <= nc.sbuf_usable_end
    o = region
    acc = later("sum_rows", [128, NT, D], F, o); o += 4 * NT * D
    hn = later("normed_rows", [128, NT, D], F, o); o += 4 * NT * D
    He = later("expert_hidden", [128, FF], F, o); o += 4 * FF
    heh = later("expert_hidden_high", [128, KF, CAP], R, o); o += 4 * KF * CAP
    hel = later("expert_hidden_low", [128, KF, CAP], R, o); o += 4 * KF * CAP
    assert o <= nc.sbuf_usable_end
    xeh = later("expert_in_high", [128, KD, CAP], R, xh_at)
    xel = later("expert_in_low", [128, KD, CAP], R, xl_at)
    sge = later("expert_silu", [128, 2, 512], F, xh_at + 4 * KD * CAP)
    assert 4 * KD * CAP + 4 * 1024 <= 4 * KD * T
    pick = later("pick", [128, NT, CAP], F, m_at)
    pickw = later("pick_weighted", [128, NT, CAP], F, m_at + 4 * NT * CAP)
    pickt = later("pick_weighted_t", [128, T], F, m_at + 8 * NT * CAP)
    Y = later("expert_out", [128, D], F, m_at + 8 * NT * CAP + 4 * T)
    lo_ = xl_at + 4 * KD * CAP
    lg = later("logits", [128, NT, 8], F, lo_)
    top = later("top_values", [128, NT, 8], F, lo_ + 96)
    topi = later("top_indices", [128, NT, 8], U32, lo_ + 192)
    topf = later("top_indices_f", [128, NT, 8], F, lo_ + 288)
    m1 = later("first_mask", [128, NT, 8], F, lo_ + 384)
    m2 = later("second_mask", [128, NT, 8], F, lo_ + 480)
    mk = later("chosen", [128, NT, 8], F, lo_ + 576)
    g1 = later("gate_terms", [128, 4, NT], F, lo_ + 672)
    cf = later("counts_f", [128, NE], F, lo_ + 736)
    gfin = later("final_gain", [128, D], F, ln_at)
    ssf = later("final_square_sum", [128, NT], F, lo_ + 800)
    rf = later("final_inverse_rms", [128, NT], F, lo_ + 832)

    ctx = ExitStack()
    bank = [ctx.enter_context(nc.psum_tensor(f"bank{i}", [128, 512], F)) for i in range(8)]

    def sem(name):
        return ctx.enter_context(nc.semaphore(name))

    raw_full = [sem(f"raw_full_{i}") for i in range(SLOTS)]
    high_done = sem("high_done")
    low_done = sem("low_done")
    pe_mark = sem("pe_mark")
    act_emptied = sem("act_emptied")
    dve_emptied = sem("dve_emptied")
    act_link = sem("act_link")
    dve_link = sem("dve_link")
    pool_link = sem("pool_link")
    consts_ready = sem("consts_ready")
    x_in = [sem("x_prompt_in"), sem("x_sample_in")]
    rows_in = sem("param_rows_in")
    layer_in = sem("layer_params_in")
    router_in = sem("router_in")
    gfin_in = sem("final_gain_in")
    prm_psum = sem("param_columns_psum")
    prm_ready = sem("param_columns_ready")
    lb_exp = sem("lower_bound_exp")
    lb_ready = sem("lower_bound_ready")
    xt_psum = sem("x_transposed_psum")
    h_ready = sem("residual_ready")
    squared = sem("squared")
    summed = sem("square_summed")
    stat_psum = sem("mean_square_psum")
    root_ready = sem("root_ready")
    rinv_ready = sem("inverse_rms_ready")
    xn_ready = sem("normed_ready")
    xh_ready = sem("moving_high_ready")
    xl_ready = sem("moving_low_ready")
    wst_psum = sem("spatial_transposed_psum")
    wst_ready = sem("spatial_transposed_ready")
    wsd_psum = sem("spatial_sample_psum")
    wsd_ready = sem("spatial_sample_ready")
    softplus_a = sem("softplus_forget_ready")
    logsig_ready = sem("key_argument_ready")
    bound_arg = sem("bound_argument_ready")
    softplus_b = sem("softplus_bound_ready")
    key_ready = sem("key_ready")
    cum_ready = sem("log_decay_ready")
    expg_ready = sem("decay_ready")
    qdec_ready = sem("query_decayed_ready")
    gap_ready = sem("gap_ready")
    gap_exp = sem("gap_decay_ready")
    kdec_ready = sem("key_decayed_ready")
    kdt_psum = sem("key_decayed_psum")
    kdt_ready = sem("key_decayed_tok_ready")
    var_ready = sem("ln_var_ready")
    dev_ready = sem("ln_deviation_ready")
    vn_ready = sem("v_normed_ready")
    vrow_out = sem("v_rows_out")
    mix_psum = sem("spatial_mix_psum")
    a_ready = sem("a_ready")
    a_high = sem("a_high_ready")
    a_low = sem("a_low_ready")
    lev_diff = sem("level_difference_ready")
    lev_exp = sem("level_decay_ready")
    lev_prod = sem("level_product_ready")
    score_psum = sem("score_psum")
    score_ready = sem("score_ready")
    upd_psum = sem("state_update_psum")
    state_ready = sem("state_ready")
    o_psum = sem("out_psum")
    o_ready = sem("out_ready")
    pstate_out = sem("prompt_state_out")
    s0_in = [sem("sample_state_in_even"), sem("sample_state_in_odd")]
    s0_out = [sem("sample_state_out_even"), sem("sample_state_out_odd")]
    vex_ready = sem("value_by_sequence_ready")
    so_psum = sem("sample_out_psum")
    su_psum = sem("sample_update_psum")
    s0_ready = sem("sample_state_ready")
    osq_ready = sem("out_squares_ready")
    ostat_psum = sem("out_mean_square_psum")
    oroot_ready = sem("out_root_ready")
    b_ready = sem("b_ready")
    b_high = sem("b_high_ready")
    b_low = sem("b_low_ready")
    merged_ready = sem("merged_ready")
    merged_high = sem("merged_high_ready")
    merged_low = sem("merged_low_ready")
    hid_high = sem("hidden_high_ready")
    hid_low = sem("hidden_low_ready")

    hn_psum = sem("normed_rows_psum")
    logit_psum = sem("logit_psum")
    lg_ready = sem("logits_ready")
    top_ready = sem("top_ready")
    gap_top = sem("top_gap_exp_ready")
    chosen_ready = sem("chosen_ready")
    rank_psum = sem("rank_psum")
    table_ready = sem("slot_table_ready")
    pick_ready = sem("pick_ready")
    pickw_ready = sem("pick_weighted_ready")
    xg_psum = sem("expert_in_psum")
    xg_high = sem("expert_in_high_ready")
    xg_low = sem("expert_in_low_ready")
    gate_emptied = sem("expert_gate_emptied")
    he_ready = sem("expert_hidden_ready")
    het_psum = sem("expert_hidden_t_psum")
    heh_ready = sem("expert_hidden_high_ready")
    hel_ready = sem("expert_hidden_low_ready")
    pickt_psum = sem("pick_weighted_t_psum")
    pickt_ready = sem("pick_weighted_t_ready")
    y_ready = sem("expert_out_ready")
    sum_psum = sem("expert_sum_psum")
    sum_done = sem("expert_sum_done")
    fsq_ready = sem("final_square_sum_ready")
    froot_ready = sem("final_root_ready")
    fout_ready = sem("final_rows_ready")
    y_out = sem("y_out")
    columns_ready = sem("slot_and_gate_columns_ready")
    shift_done = sem("slots_shifted")

    MB = mark_after[-1]
    OUTS = [(t, hf_) for t in range(NT) for hf_ in range(2)]
    SUM_BANK = [2, 3, 6, 7, 4, 5]
    ROW_BANK = [0, 1, 2, 3, 5, 6]
    NO = len(OUTS)

    def expert_source(e, i):
        kind, j, part, k0, kt, c0, cols = ECH[i]
        w = A["moe_w_" + kind][0, e]
        return rows(w, k0, kt, c0, cols)

    def width(i):
        return ECH[i % NEC][4] * ECH[i % NEC][6]

    def group_tiles(j):
        c0, cols = groups[j]
        return range(c0 // 128, (c0 + cols) // 128)

    def extra_blocks(eng, ready, run):
        eng.wait_ge(ready, 1)
        with eng.Fori(0, NMORE) as n:
            more = eng.value_load(full[0:1, bass.ds(n, 1)], min_val=0, max_val=1)
            item = eng.value_load(items[0:1, bass.ds(n, 1)], min_val=NE, max_val=NE + NMORE)
            with eng.If(more > 0):
                run(item, n)

    def emptied_sem(by):
        return act_emptied if by == "act" else dve_emptied

    def base(L):
        return first_chunk[(L, "forget")]

    TV = 64 // NSEQ
    NLEV = len(LEVELS)
    SCORES = PAIRS + 1
    NSCORE = sum(SCORES if lv <= LS // 2 else PAIRS for lv in [0] + LEVELS)

    def score_count(L, li):
        return NSCORE * L + sum(SCORES if lv <= LS // 2 else PAIRS for lv in ([0] + LEVELS)[:li])

    def halves(X, lv, n):
        v = X[:, :, 0:n].rearrange("p h (b c) -> p h b c", c=2 * lv)
        return v[:, :, :, 0:lv], v[:, :, :, lv:2 * lv], v[:, :, :, lv - 1:lv].broadcast_to([128, H, n // (2 * lv), lv])

    def tokens_of(lv):
        return T if lv <= LS // 2 else TP

    P_MIX, P_FFN, P_LB, P_HG = 0, LAYERS * KD, 2 * LAYERS * KD, 2 * LAYERS * KD + LAYERS * H

    block = ctx.enter_context(nc.Block())

    @block.sync
    def _(sp):
        for c, (src, kt, cols) in enumerate(chunks):
            if c >= SLOTS:
                sp.wait_ge(low_done, c - SLOTS + 1)
            sp.dma_start(raw[:, c % SLOTS, 0:kt * cols].rearrange("p (k n) -> p k n", n=cols), src).then_inc(
                raw_full[c % SLOTS], 16)

        def load_expert(item, e):
            for i in range(NEC):
                sp.wait_ge(low_done, NDENSE + NEC * item + i - SLOTS + 1)
                sp.dma_start(raw[:, i % SLOTS, 0:width(i)].rearrange("p (k n) -> p k n", n=ECH[i][6]),
                             expert_source(e, i)).then_inc(raw_full[i % SLOTS], 16)

        with sp.Fori(0, NE) as e:
            load_expert(e, e)
        extra_blocks(sp, table_ready, lambda item, n: load_expert(item, n % NE))

    @block.gpsimd
    def _(pool):
        links = [0]

        def link(ins):
            links[0] += 1
            ins.then_inc(pool_link, 1)
            pool.wait_ge(pool_link, links[0])

        pool.dma_start(xt[:, 0:PAIRS, :], A["x_prompt"][0].rearrange("(t p) d -> p t d", p=128)).then_inc(x_in[0], 16)
        pool.dma_start(xt[0:64, PAIRS, :], A["x_sample"].rearrange("b j d -> (b j) d")).then_inc(x_in[1], 16)
        for n, (name, k) in enumerate((("norm_mix_g", KD), ("norm_ffn_g", KD), ("lower_bounds", H), ("hgrn_norm_g", H))):
            r = (P_MIX, P_FFN, P_LB, P_HG)[n]
            pool.dma_start(prow[r:r + LAYERS * k, :], A[name].rearrange("l (k p) -> (l k) p", p=128)).then_inc(rows_in, 16)

        def layer_params(L):
            pool.dma_start(wsp[:], A["w_spatial"][L].rearrange("g t s -> t g s")).then_inc(layer_in, 16)
            pool.dma_start(bsp[:], A["b_spatial"][L].partition_broadcast(128)).then_inc(layer_in, 16)
            pool.dma_start(lng[:], A["ln_v_g"][L].partition_broadcast(128)).then_inc(layer_in, 16)
            pool.dma_start(lnb[:], A["ln_v_b"][L].partition_broadcast(128)).then_inc(layer_in, 16)

        layer_params(0)
        pool.dma_start(rw[:], A["router_w"][0].rearrange("(k p) e -> p k e", p=128)).then_inc(router_in, 16)
        link(nc.gpsimd.memset(ident[:], 0.0))
        link(nc.gpsimd.affine_select(out=ident[:], in_=ident[:], compare_op=ALU.not_equal, fill=1.0, base=0,
                                     pattern=[[-1, 128]], channel_multiplier=1))
        link(nc.gpsimd.memset(ones[:], 1.0))
        link(nc.gpsimd.affine_select(out=upper[:], in_=ones[:], compare_op=ALU.is_ge, fill=0.0, base=0,
                                     pattern=[[1, 128]], channel_multiplier=-1))
        link(nc.gpsimd.iota(iota[:], pattern=[[1, 128]], base=0, channel_multiplier=0,
                            allow_small_or_imprecise_dtypes=True))
        link(nc.gpsimd.memset(lmask[:], 0))
        link(nc.gpsimd.affine_select(out=lmask[:, 0, :], in_=lmask[:, 0, :], compare_op=ALU.not_equal, fill=1.0, base=0,
                                     pattern=[[-1, 128]], channel_multiplier=1))
        for n, lv in enumerate(LEVELS):
            v = lmask[:, n + 1, :].rearrange("p (b c) -> p b c", c=2 * lv)
            nb = 128 // (2 * lv)
            link(nc.gpsimd.memset(v[:, :, lv:2 * lv], 1))
            link(nc.gpsimd.affine_select(out=v, in_=v, compare_op=ALU.is_ge, fill=0.0, base=0,
                                         pattern=[[-2 * lv, nb], [0, 2 * lv]], channel_multiplier=1))
            link(nc.gpsimd.affine_select(out=v, in_=v, compare_op=ALU.is_ge, fill=0.0, base=lv - 1,
                                         pattern=[[2 * lv, nb], [0, 2 * lv]], channel_multiplier=-1))
        link(nc.gpsimd.memset(smask[:], 1.0))
        link(nc.gpsimd.memset(smask[:, 0:TP:CH], 0.0))
        link(nc.gpsimd.memset(smask[:, TP:T:LS], 0.0))
        link(nc.gpsimd.memset(bmask[:], 1.0))
        link(nc.gpsimd.affine_select(out=bmask[:], in_=bmask[:], compare_op=ALU.is_ge, fill=0.0, base=0,
                                     pattern=[[-LS, NSEQ]], channel_multiplier=1))
        link(nc.gpsimd.affine_select(out=bmask[:], in_=bmask[:], compare_op=ALU.is_ge, fill=0.0, base=LS - 1,
                                     pattern=[[LS, NSEQ]], channel_multiplier=-1))
        for b in range(NSEQ):
            link(nc.gpsimd.tensor_copy(r8[:, LS * b:LS * b + LS], ident[0:LS, 0:LS]))
        nc.gpsimd.memset(eps_t[:], EPS).then_inc(consts_ready, 1)

        def load_s0(L, hd):
            b = hd % 2
            n = 2 * L + hd // 2
            if hd < 2:
                pool.wait_ge(lev_diff, NLEV * (L + 1))
                pool.wait_ge(o_psum, H * (L + 1))
            else:
                pool.wait_ge(s0_out[b], 16 * n)
            pool.dma_start(s0[b][:], A["state_hgrn"][L, :, hd].rearrange("b p v -> p b v")).then_inc(s0_in[b], 16)

        for L in range(LAYERS):
            pool.wait_ge(vn_ready, NT * (L + 1))
            pool.dma_start(OUT["v_rows"][L].rearrange("b j c -> (b j) c"), vn[0:64, PAIRS, :]).then_inc(vrow_out, 16)
            pool.wait_ge(state_ready, NPC * (L + 1))
            pool.dma_start(OUT["prompt_state"][L, 0].rearrange("h p v -> p h v"), S34[:, 1]).then_inc(pstate_out, 16)
            load_s0(L, 0)
            load_s0(L, 1)
            for hd in range(H):
                n = 2 * L + hd // 2
                pool.wait_ge(s0_ready, H * L + hd + 1)
                pool.dma_start(OUT["sample_state"][L, :, hd].rearrange("b p v -> p b v"), s0[hd % 2][:]).then_inc(
                    s0_out[hd % 2], 16)
                if hd + 2 < H:
                    load_s0(L, hd + 2)
            if L + 1 < LAYERS:
                pool.wait_ge(a_ready, H * (L + 1))
                layer_params(L + 1)
        for s in (s0_out[0], s0_out[1]):
            pool.wait_ge(s, 16 * LAYERS * H // 2)
        pool.wait_ge(vrow_out, 16 * LAYERS)
        pool.wait_ge(pstate_out, 16 * LAYERS)
        pool.dma_start(gfin[:], A["final_norm_g"].partition_broadcast(128)).then_inc(gfin_in, 16)
        for t in range(PAIRS):
            pool.wait_ge(fout_ready, t + 1)
            pool.dma_start(OUT["y_prompt"][0, 128 * t:128 * t + 128, :], acc[:, t, :]).then_inc(y_out, 16)
        pool.wait_ge(fout_ready, NT)
        pool.dma_start(OUT["y_sample"].rearrange("b j d -> (b j) d"), acc[0:64, PAIRS, :]).then_inc(y_out, 16)
        pool.wait_ge(y_out, 16 * NT)

    @block.scalar
    def _(act):
        links = [0]
        fn = nc.scalar.activation

        def link(ins):
            links[0] += 1
            ins.then_inc(act_link, 1)
            act.wait_ge(act_link, links[0])

        def split_high(c):
            kt, cols = chunks[c][1:] if c < NDENSE else ECH[c - NDENSE][4::2]
            act.wait_ge(raw_full[c % SLOTS], 16 * (c // SLOTS + 1))
            if c >= SLOTS:
                act.wait_ge(pe_mark, mark_after[c - SLOTS])
            fn(whi[:, c % SLOTS, 0:kt * cols], raw[:, c % SLOTS, 0:kt * cols], ACT.Copy).then_inc(high_done, 1)

        def square(n, j):
            if n == 0:
                act.wait_ge(h_ready, j + 1)
            else:
                L, sec = (n - 1) // 2, ("w_out", "down")[(n - 1) % 2]
                act.wait_ge(dve_emptied, tile[(L, sec, j)][3])
            if 8 * n + j >= 2:
                act.wait_ge(summed, KD * n + j - 1)
            fn(sq[:, j % 2, :], h[:, j, :], ACT.Square).then_inc(squared, 1)

        def norm(n, parts=True):
            act.wait_ge(stat_psum, n + 1)
            if n:
                act.wait_ge(xn_ready, KD * n)
            fn(rinv[:], bank[4][:, 0:T], ACT.Sqrt, bias=eps_t[:], scale=1.0 / D).then_inc(root_ready, 1)
            if parts:
                for j in range(KD):
                    act.wait_ge(xn_ready, KD * n + j + 1)
                    fn(xh[:, j, :], xn[:, j, :], ACT.Copy).then_inc(xh_ready, 1)

        def empties(L, sec, j, out, f, psz=128, cols=T):
            b, mark, by, count, _ = tile[(L, sec, j)]
            act.wait_ge(pe_mark, mark)
            fn(out, bank[b][0:psz, 0:cols], f).then_inc(act_emptied, 1)

        for c in range(SLOTS):
            split_high(c)
        act.wait_ge(consts_ready, 1)
        for j in range(KD):
            square(0, j)
        norm(0)
        act.wait_ge(lb_ready, 1)
        link(fn(lbt[:, 3], lbt[:, 0], ACT.Abs))
        link(fn(lbt[:, 3], lbt[:, 3], ACT.Exp, scale=-1.0))
        fn(lbt[:, 4], lbt[:, 3], ACT.Ln, bias=1.0).then_inc(lb_exp, 1)

        for L in range(LAYERS):
            if L:
                norm(2 * L)
            for i, (sec, part) in enumerate(MIX):
                c = base(L) + i
                if sec == "forget":
                    for j in (2 * part, 2 * part + 1):
                        empties(L, sec, j, G[:, j, :], ACT.Copy)
                elif sec == "q":
                    for j in (2 * part, 2 * part + 1):
                        empties(L, sec, j, Q[:, j, :], ACT.Silu)
                elif sec == "value" and part == 1:
                    for j, (_, sz) in enumerate(TOK):
                        empties(L, sec, j, V[0:sz, j, :], ACT.Copy, sz, DA)
                elif sec == "v" and part == 1:
                    if L:
                        act.wait_ge(vrow_out, 16 * L)
                    for j, (_, sz) in enumerate(TOK):
                        empties(L, sec, j, vn[0:sz, j, :], ACT.Gelu, sz, DA)
                elif sec == "u":
                    for j in (2 * part, 2 * part + 1):
                        empties(L, sec, j, u[:, j, :], ACT.Gelu)
                elif sec == "gate_a":
                    for j in (2 * part, 2 * part + 1):
                        empties(L, sec, j, xn[:, j, :], ACT.Sigmoid)
                elif sec == "out_gate":
                    if part == 0:
                        act.wait_ge(a_ready, H * (L + 1))
                    for j in (2 * part, 2 * part + 1):
                        empties(L, sec, j, u[:, j, :], ACT.Silu)
                elif sec == "gate_b":
                    for j in (2 * part, 2 * part + 1):
                        empties(L, sec, j, gb[:, j, :], ACT.Sigmoid)
                split_high(c + SLOTS)
                if i == 2:
                    act.wait_ge(act_emptied, tile[(L, "forget", H - 1)][3])
                    if L:
                        act.wait_ge(b_low, H * L)
                        act.wait_ge(pstate_out, 16 * L)
                        act.wait_ge(s0_out[0], 32 * L)
                        act.wait_ge(s0_out[1], 32 * L)
                    link(fn(Z[:], G[:], ACT.Abs))
                    link(fn(Z[:], Z[:], ACT.Exp, scale=-1.0))
                    fn(E[:], Z[:], ACT.Ln, bias=1.0).then_inc(softplus_a, 1)
                    act.wait_ge(logsig_ready, L + 1)
                    if L == 0:
                        fn(K[:], E[:], ACT.Exp).then_inc(key_ready, 1)
                    else:
                        act.wait_ge(lb_ready, 2)
                        for j in range(H):
                            ins = fn(K[:, j], E[:, j], ACT.Exp, bias=lbt[:, 2, j:j + 1])
                        ins.then_inc(key_ready, 1)
                        act.wait_ge(bound_arg, L)
                        link(fn(QE[:], Z[:], ACT.Abs))
                        link(fn(QE[:], QE[:], ACT.Exp, scale=-1.0))
                        fn(QE[:], QE[:], ACT.Ln, bias=1.0).then_inc(softplus_b, 1)
                if i == 4:
                    act.wait_ge(cum_ready, H * (L + 1))
                    act.wait_ge(key_ready, L + 1)
                    fn(E[:], G[:], ACT.Exp).then_inc(expg_ready, 1)
                    act.wait_ge(gap_ready, L + 1)
                    fn(Z[:], Z[:], ACT.Exp).then_inc(gap_exp, 1)
                if i == 5:
                    for j, (_, sz) in enumerate(TOK):
                        act.wait_ge(kdt_psum, NT * L + j + 1)
                        fn(kdt[0:sz, j, :], bank[4 + j][0:sz, :], ACT.Copy).then_inc(kdt_ready, 1)
                if i == 7:
                    for j, (_, sz) in enumerate(TOK):
                        act.wait_ge(var_ready, NT * L + j + 1)
                        fn(bag[0:sz, j, 1:2], bag[0:sz, j, 1:2], ACT.Sqrt, bias=eps_t[0:sz]).then_inc(dev_ready, 1)
                if 6 <= i < 6 + NLEV:
                    li = i - 6
                    n = tokens_of(LEVELS[li])
                    act.wait_ge(lev_diff, NLEV * L + li + 1)
                    fn(E[:, :, 0:n], E[:, :, 0:n], ACT.Exp).then_inc(lev_exp, 1)
                if 9 <= i < 9 + H:
                    g = i - 9
                    act.wait_ge(a_ready, H * L + g + 1)
                    fn(ahi[:, g], u[:, g], ACT.Copy).then_inc(a_high, 1)
                if i == 14:
                    for hd in range(H):
                        act.wait_ge(o_psum, H * L + hd + 1)
                        fn(Q[:, hd, :], bank[4 + hd][:, 0:T], ACT.Copy).then_inc(o_ready, 1)
                if i == 19:
                    act.wait_ge(s0_ready, H * (L + 1))
                    fn(osq[:], Q[:], ACT.Square).then_inc(osq_ready, 1)
                    for hd in range(H):
                        act.wait_ge(ostat_psum, H * L + hd + 1)
                        fn(QE[:, hd, :], bank[4 + hd][:, 0:T], ACT.Sqrt, bias=eps_t[:], scale=1.0 / 128).then_inc(
                            oroot_ready, 1)
                if i == 20:
                    for hd in range(H):
                        act.wait_ge(b_ready, H * L + hd + 1)
                        fn(bhi[:, hd], Q[:, hd], ACT.Copy).then_inc(b_high, 1)
                if sec == "branch_b":
                    for j in range(4 * part, 4 * part + 4):
                        act.wait_ge(merged_ready, KD * L + j + 1)
                        fn(xh[:, j, :], xn[:, j, :], ACT.Copy).then_inc(merged_high, 1)
                if sec == "w_out":
                    for j in (2 * part, 2 * part + 1):
                        square(2 * L + 1, j)
            if L % 2 == 0:
                norm(2 * L + 1)
                act.wait_ge(pstate_out, 16 * (L + 1))
                act.wait_ge(vrow_out, 16 * (L + 1))
                act.wait_ge(s0_out[0], 32 * (L + 1))
                act.wait_ge(s0_out[1], 32 * (L + 1))
                for i, (sec, part) in enumerate(FFN):
                    c = first_chunk[(L, "gate")] + i
                    if sec == "gate":
                        if part:
                            act.wait_ge(dve_emptied, tile[(L, "up", 2 * part - 1)][3])
                        for j in (0, 1):
                            empties(L, sec, 2 * part + j, sg[:, j, :], ACT.Silu)
                    split_high(c + SLOTS)
                    if sec == "up":
                        for j in (0, 1):
                            act.wait_ge(dve_emptied, tile[(L, "up", 2 * part + j)][3])
                            fn(fh[:, 2 * part + j, :], hf[:, j, :], ACT.Copy).then_inc(hid_high, 1)
                    if sec == "down" and part % 3 == 2:
                        for j in (0, 1):
                            square(2 * L + 2, 2 * (part // 3) + j)

        norm(2 * LAYERS - 1, parts=False)
        act.wait_ge(pstate_out, 16 * LAYERS)
        act.wait_ge(vrow_out, 16 * LAYERS)
        act.wait_ge(s0_out[0], 32 * LAYERS)
        act.wait_ge(s0_out[1], 32 * LAYERS)
        for n, (t, hf_) in enumerate(OUTS):
            act.wait_ge(hn_psum, n + 1)
            fn(hn[0:TOK[t][1], t, 512 * hf_:512 * hf_ + 512], bank[ROW_BANK[n]][0:TOK[t][1], :], ACT.Copy).then_inc(
                y_ready, 1)
        act.wait_ge(top_ready, 1)
        fn(g1[:, 0], g1[:, 0], ACT.Exp).then_inc(gap_top, 1)

        def expert_in_high(item):
            for hh in range(2):
                act.wait_ge(xg_psum, 2 * item + hh + 1)
                fn(xeh[:, 4 * hh:4 * hh + 4, :], bank[6 + hh][:], ACT.Copy).then_inc(xg_high, 1)

        def hidden_high(item, j):
            ts = group_tiles(j)
            act.wait_ge(het_psum, NG * item + j + 1)
            fn(heh[:, ts[0]:ts[-1] + 1, :], bank[4 + j % 2][:, 0:128 * len(ts)], ACT.Copy).then_inc(heh_ready, 1)

        def high_of(item, i):
            act.wait_ge(raw_full[i % SLOTS], 16 * (NEC // SLOTS) * item + 16 * (NDENSE // SLOTS + i // SLOTS + 1))
            act.wait_ge(pe_mark, NEC * item + (MB + i - SLOTS + 1))
            n = width(i)
            fn(whi[:, i % SLOTS, 0:n], raw[:, i % SLOTS, 0:n], ACT.Copy).then_inc(high_done, 1)

        def expert(item, first, ahead):
            if first:
                for i in range(SLOTS):
                    high_of(item, i)
                expert_in_high(item)
            for i, (kind, j, part, k0, kt, c0, cols) in enumerate(ECH):
                if kind == "gate" and i == closing[(kind, j)]:
                    act.wait_ge(pe_mark, NEC * item + (MB + i + 1))
                    if j >= 2:
                        act.wait_ge(he_ready, NG * item + (j - 1))
                    fn(sge[:, j % 2, 0:cols], bank[2 * (j % 2)][:, 0:cols], ACT.Silu).then_inc(gate_emptied, 1)
                if i + SLOTS < NEC or ahead:
                    high_of(item, i + SLOTS)
                if kind == "up" and i == closing[(kind, j)]:
                    if j:
                        hidden_high(item, j - 1)
                    if j == NG - 1:
                        if ahead:
                            expert_in_high(item + 1)
                        hidden_high(item, j)
                        act.wait_ge(pickt_psum, item + 1)
                        act.wait_ge(sum_psum, NO * item + NO)
                        fn(pickt[:], bank[4][:, 0:T], ACT.Copy).then_inc(pickt_ready, 1)
            act.wait_ge(pe_mark, NEC * item + (MB + NEC))
            act.wait_ge(sum_psum, NO * item + NO)
            for hh in range(2):
                fn(Y[:, 512 * hh:512 * hh + 512], bank[hh][:], ACT.Copy).then_inc(y_ready, 1)

        expert_in_high(0)
        with act.Fori(0, NE - 1) as e:
            expert(e, False, True)
        expert(NE - 1, False, False)
        extra_blocks(act, table_ready, lambda item, n: expert(item, True, False))
        for t, (_, sz) in enumerate(TOK):
            act.wait_ge(fsq_ready, t + 1)
            fn(rf[0:sz, t:t + 1], ssf[0:sz, t:t + 1], ACT.Sqrt, bias=eps_t[0:sz], scale=1.0 / D).then_inc(froot_ready, 1)

    @block.vector
    def _(dve):
        links = [0]
        v = nc.vector

        def link(ins):
            links[0] += 1
            ins.then_inc(dve_link, 1)
            dve.wait_ge(dve_link, links[0])

        def split_low(c):
            kt, cols = chunks[c][1:] if c < NDENSE else ECH[c - NDENSE][4::2]
            dve.wait_ge(high_done, c + 1)
            v.tensor_tensor(wlo[:, c % SLOTS, 0:kt * cols], raw[:, c % SLOTS, 0:kt * cols],
                            whi[:, c % SLOTS, 0:kt * cols].bitcast(F), ALU.subtract).then_inc(low_done, 1)

        def add_square(n, j):
            dve.wait_ge(squared, KD * n + j + 1)
            if j == 0:
                if n:
                    dve.wait_ge(stat_psum, n)
                v.tensor_copy(ssum[:], sq[:, 0, :]).then_inc(summed, 1)
            else:
                dve.wait_ge(summed, KD * n + j)
                v.tensor_tensor(ssum[:], ssum[:], sq[:, j % 2, :], ALU.add).then_inc(summed, 1)

        def norm(n, parts=True):
            col = (P_FFN if n % 2 else P_MIX) + KD * (n // 2)
            dve.wait_ge(root_ready, n + 1)
            v.reciprocal(rinv[:], rinv[:]).then_inc(rinv_ready, 1)
            dve.wait_ge(rinv_ready, n + 1)
            for j in range(KD + 1):
                if j < KD:
                    v.scalar_tensor_tensor(out=xn[:, j, :], in0=h[:, j, :], scalar=prm[:, col + j:col + j + 1],
                                           in1=rinv[:], op0=ALU.mult, op1=ALU.mult).then_inc(xn_ready, 1)
                if j and parts:
                    dve.wait_ge(xh_ready, KD * n + j)
                    v.tensor_tensor(xl[:, j - 1, :], xn[:, j - 1, :], xh[:, j - 1, :].bitcast(F),
                                    ALU.subtract).then_inc(xl_ready, 1)

        def waits_tile(L, sec, j):
            b, mark, _, _, _ = tile[(L, sec, j)]
            dve.wait_ge(pe_mark, mark)
            return bank[b]

        def add_residual(L, sec, j):
            b = waits_tile(L, sec, j)
            v.tensor_tensor(h[:, j, :], h[:, j, :], b[:, 0:T], ALU.add).then_inc(dve_emptied, 1)

        dve.wait_ge(prm_psum, 1)
        v.tensor_copy(prm[:], bank[7][:, 0:NROW]).then_inc(prm_ready, 1)
        for j in range(KD):
            dve.wait_ge(xt_psum, j + 1)
            v.tensor_copy(h[:, j, :], bank[j % 4][:, 0:T]).then_inc(h_ready, 1)
            if j:
                add_square(0, j - 1)
        add_square(0, KD - 1)
        dve.wait_ge(prm_ready, 1)
        v.tensor_tensor(lbt[:, 0], prm[:, P_LB + H:P_LB + 2 * H], prm[:, P_LB:P_LB + H], ALU.subtract).then_inc(lb_ready, 1)
        split_low(0)
        norm(0)
        split_low(1)
        split_low(2)
        dve.wait_ge(lb_exp, 1)
        dve.wait_ge(lb_ready, 1)
        link(v.scalar_tensor_tensor(out=lbt[:, 1], in0=lbt[:, 0], scalar=0.0, in1=lbt[:, 4], op0=ALU.min,
                                    op1=ALU.subtract))
        v.tensor_tensor(lbt[:, 2], lbt[:, 1], lbt[:, 0], ALU.subtract).then_inc(lb_ready, 1)

        for L in range(LAYERS):
            if L:
                add_square(2 * L, KD - 1)
                norm(2 * L)
            for i, (sec, part) in enumerate(MIX):
                c = base(L) + i
                if sec == "branch_a":
                    for j in range(4 * part, 4 * part + 4):
                        b = waits_tile(L, sec, j)
                        dve.wait_ge(act_emptied, tile[(L, "gate_a", j)][3])
                        v.tensor_tensor(xn[:, j, :], b[:, 0:T], xn[:, j, :], ALU.mult).then_inc(dve_emptied, 1)
                if sec == "branch_b":
                    for j in range(4 * part, 4 * part + 4):
                        b = waits_tile(L, sec, j)
                        dve.wait_ge(act_emptied, tile[(L, "gate_b", j)][3])
                        v.tensor_tensor(tmp[:, j % 2, :], b[:, 0:T], gb[:, j, :], ALU.mult).then_inc(dve_emptied, 1)
                        dve.wait_ge(dve_emptied, tile[(L, sec, j)][3])
                        v.tensor_tensor(xn[:, j, :], xn[:, j, :], tmp[:, j % 2, :], ALU.add).then_inc(merged_ready, 1)
                        if j:
                            dve.wait_ge(merged_high, KD * L + j)
                            v.tensor_tensor(xl[:, j - 1, :], xn[:, j - 1, :], xh[:, j - 1, :].bitcast(F),
                                            ALU.subtract).then_inc(merged_low, 1)
                    if part == 1:
                        j = KD
                        dve.wait_ge(merged_high, KD * L + j)
                        v.tensor_tensor(xl[:, j - 1, :], xn[:, j - 1, :], xh[:, j - 1, :].bitcast(F),
                                        ALU.subtract).then_inc(merged_low, 1)
                if sec == "w_out":
                    for j in (2 * part, 2 * part + 1):
                        add_residual(L, sec, j)
                split_low(c + SLOTS)
                if sec == "w_out":
                    for j in (2 * part - 1, 2 * part):
                        if j >= 0:
                            add_square(2 * L + 1, j)
                if i == 0:
                    dve.wait_ge(wst_psum, L + 1)
                    dve.wait_ge(consts_ready, 1)
                    v.tensor_tensor(wst[:], bank[7][:].rearrange("p (g t) -> p g t", g=H),
                                    upper[:].unsqueeze(1).broadcast_to([128, H, 128]), ALU.mult).then_inc(wst_ready, 1)
                if i == 1:
                    dve.wait_ge(wsd_psum, L + 1)
                    for g in range(H):
                        ins = v.tensor_tensor(wsd[:, g].rearrange("p (b t) -> p b t", t=LS),
                                              bank[7][0:64, 64 * g:64 * g + 64].rearrange("p (b t) -> p b t", t=LS),
                                              bmask[:].unsqueeze(2).broadcast_to([64, NSEQ, LS]), ALU.mult)
                        ins.then_inc(wsd_ready, 1)
                if i == 2:
                    dve.wait_ge(softplus_a, L + 1)
                    link(v.scalar_tensor_tensor(out=Z[:], in0=G[:], scalar=0.0, in1=E[:], op0=ALU.min, op1=ALU.subtract))
                    v.tensor_tensor(E[:], Z[:], G[:], ALU.subtract).then_inc(logsig_ready, 1)
                    dve.wait_ge(logsig_ready, L + 1)
                    if L:
                        for j in range(H):
                            ins = v.tensor_scalar(Z[:, j], Z[:, j], lbt[:, 0, j:j + 1], None, ALU.subtract)
                        ins.then_inc(bound_arg, 1)
                        dve.wait_ge(softplus_b, L)
                        dve.wait_ge(bound_arg, L)
                        link(v.scalar_tensor_tensor(out=Z[:], in0=Z[:], scalar=0.0, in1=QE[:], op0=ALU.max, op1=ALU.add))
                        for j in range(H):
                            link(v.tensor_scalar(Z[:, j], Z[:, j], lbt[:, 1, j:j + 1], None, ALU.add))
                    for j in range(H):
                        v.tensor_tensor_scan(G[:, j], smask[:], Z[:, j], 0.0, ALU.mult, ALU.add).then_inc(cum_ready, 1)
                if i == 4:
                    dve.wait_ge(cum_ready, H * (L + 1))
                    link(v.tensor_tensor(Z[:, :, 0:TP].rearrange("p h (c t) -> p h c t", t=CH),
                                         G[:, :, CH - 1:TP:CH].unsqueeze(3).broadcast_to([128, H, NPC, CH]),
                                         G[:, :, 0:TP].rearrange("p h (c t) -> p h c t", t=CH), ALU.subtract))
                    v.tensor_tensor(Z[:, :, TP:T].rearrange("p h (c t) -> p h c t", t=LS),
                                    G[:, :, TP + LS - 1:T:LS].unsqueeze(3).broadcast_to([128, H, NSEQ, LS]),
                                    G[:, :, TP:T].rearrange("p h (c t) -> p h c t", t=LS),
                                    ALU.subtract).then_inc(gap_ready, 1)
                    dve.wait_ge(expg_ready, L + 1)
                    link(v.tensor_copy(el[:, :, 0:NPC], E[:, :, CH - 1:TP:CH]))
                    link(v.tensor_copy(el[:, :, NPC:], E[:, :, TP + LS - 1:T:LS]))
                    dve.wait_ge(act_emptied, tile[(L, "q", H - 1)][3])
                    v.tensor_tensor(QE[:], Q[:], E[:], ALU.mult).then_inc(qdec_ready, 1)
                    dve.wait_ge(gap_exp, L + 1)
                    dve.wait_ge(key_ready, L + 1)
                    v.tensor_tensor(Z[:], Z[:], K[:], ALU.mult).then_inc(kdec_ready, 1)
                    link(v.memset(sc[:], 0.0))
                    link(v.memset(scs[:], 0.0))
                if i == 7:
                    dve.wait_ge(layer_in, 64 * (L + 1))
                    for j, (_, sz) in enumerate(TOK):
                        dve.wait_ge(act_emptied, tile[(L, "v", j)][3])
                        link(v.bn_stats(bst[0:sz, j, :], vn[0:sz, j, :]))
                        v.bn_aggr(bag[0:sz, j, :], bst[0:sz, j, :]).then_inc(var_ready, 1)
                    for j, (_, sz) in enumerate(TOK):
                        dve.wait_ge(dev_ready, NT * L + j + 1)
                        link(v.reciprocal(bag[0:sz, j, 1:2], bag[0:sz, j, 1:2]))
                        link(v.tensor_scalar(vn[0:sz, j, :], vn[0:sz, j, :], bag[0:sz, j, 0:1], bag[0:sz, j, 1:2],
                                             ALU.subtract, ALU.mult))
                        link(v.tensor_tensor(vn[0:sz, j, :], vn[0:sz, j, :], lng[0:sz], ALU.mult))
                        v.tensor_tensor(vn[0:sz, j, :], vn[0:sz, j, :], lnb[0:sz], ALU.add).then_inc(vn_ready, 1)
                if 6 <= i < 6 + NLEV:
                    li = i - 6
                    lv = LEVELS[li]
                    n = tokens_of(lv)
                    ga, gb2, ref = halves(G, lv, n)
                    ea, eb, _ = halves(E, lv, n)
                    za, zb, _ = halves(Z, lv, n)
                    ka, _, _ = halves(K, lv, n)
                    _, qb, _ = halves(Q, lv, n)
                    if li == 0:
                        dve.wait_ge(qdec_ready, L + 1)
                    else:
                        dve.wait_ge(lev_prod, NLEV * L + li)
                    link(v.tensor_tensor(ea, ref, ga, ALU.subtract))
                    v.tensor_tensor(eb, gb2, ref, ALU.subtract).then_inc(lev_diff, 1)
                    dve.wait_ge(lev_exp, NLEV * L + li + 1)
                    if li == 0:
                        dve.wait_ge(kdt_psum, NT * (L + 1))
                    else:
                        dve.wait_ge(score_psum, score_count(L, li + 1))
                    link(v.tensor_tensor(za, ka, ea, ALU.mult))
                    v.tensor_tensor(zb, qb, eb, ALU.mult).then_inc(lev_prod, 1)
                if 6 <= i < 7 + NLEV:
                    li = i - 6
                    k = score_count(L, li)
                    lv = ([0] + LEVELS)[li]
                    for p in range(SCORES if lv <= LS // 2 else PAIRS):
                        dve.wait_ge(score_psum, k + p + 1)
                        if li:
                            dve.wait_ge(score_ready, score_count(L, li))
                        if p < PAIRS:
                            v.copy_predicated(sc[:, p], lmask[:, li, :].unsqueeze(1).broadcast_to([128, H, 128]),
                                              bank[4 + p][:].rearrange("p (h t) -> p h t", h=H)).then_inc(score_ready, 1)
                        else:
                            v.copy_predicated(scs[:], lmask[0:64, li, 0:64].unsqueeze(1).broadcast_to([64, H, 64]),
                                              bank[6][0:64, 0:64 * H].rearrange("p (h t) -> p h t", h=H)).then_inc(
                                                  score_ready, 1)
                if 9 <= i < 9 + H:
                    g = i - 9
                    dve.wait_ge(mix_psum, H * L + g + 1)
                    dve.wait_ge(act_emptied, tile[(L, "u", H - 1)][3])
                    b = bank[7]
                    t1 = tmp[:, g % 2, :]
                    link(v.tensor_tensor(t1[:, 0:TP].rearrange("p (c t) -> p c t", t=128),
                                         b[:, 0:TP].rearrange("p (c t) -> p c t", t=128),
                                         bsp[:, g].unsqueeze(1).broadcast_to([128, PAIRS, 128]), ALU.add))
                    link(v.tensor_tensor(t1[:, TP:T].rearrange("p (c t) -> p c t", t=LS),
                                         b[:, TP:T].rearrange("p (c t) -> p c t", t=LS),
                                         bsp[:, g, 0:LS].unsqueeze(1).broadcast_to([128, NSEQ, LS]), ALU.add))
                    v.tensor_tensor(u[:, g], u[:, g], t1, ALU.mult).then_inc(a_ready, 1)
                    dve.wait_ge(a_high, H * L + g + 1)
                    v.tensor_tensor(alo[:, g], u[:, g], ahi[:, g].bitcast(F), ALU.subtract).then_inc(a_low, 1)
                if i == 13:
                    for n in range(NPC):
                        dve.wait_ge(upd_psum, NPC * L + n + 1)
                        dst = (S12 if n < 2 else S34)[:, n % 2]
                        if n == 0:
                            v.tensor_copy(dst, bank[4][:].rearrange("p (h v) -> p h v", h=H)).then_inc(state_ready, 1)
                            continue
                        dve.wait_ge(state_ready, NPC * L + n)
                        src = (S12 if n - 1 < 2 else S34)[:, (n - 1) % 2]
                        for hd in range(H):
                            ins = v.scalar_tensor_tensor(out=dst[:, hd], in0=src[:, hd], scalar=el[:, hd, n:n + 1],
                                                         in1=bank[4 + n][:, 128 * hd:128 * hd + 128],
                                                         op0=ALU.mult, op1=ALU.add)
                        ins.then_inc(state_ready, 1)
                if 15 <= i < 15 + H:
                    hd = i - 15
                    if hd:
                        dve.wait_ge(su_psum, H * L + hd)
                    dve.wait_ge(act_emptied, tile[(L, "value", NT - 1)][3])
                    v.tensor_tensor(vex[:], V[0:64, PAIRS, 128 * hd:128 * hd + 128].unsqueeze(1).broadcast_to([64, NSEQ, 128]),
                                    bmask[:].unsqueeze(2).broadcast_to([64, NSEQ, 128]), ALU.mult).then_inc(vex_ready, 1)
                    dve.wait_ge(so_psum, H * L + hd + 1)
                    dve.wait_ge(o_ready, H * L + hd + 1)
                    link(v.tensor_tensor(Q[:, hd, TP:T], Q[:, hd, TP:T], bank[6][:, 0:64], ALU.add))
                    dve.wait_ge(su_psum, H * L + hd + 1)
                    st = s0[hd % 2]
                    for b in range(NSEQ):
                        ins = v.scalar_tensor_tensor(out=st[:, b], in0=st[:, b], scalar=el[:, hd, NPC + b:NPC + b + 1],
                                                     in1=bank[4 + b // 4][:, 128 * (b % 4):128 * (b % 4) + 128],
                                                     op0=ALU.mult, op1=ALU.add)
                    ins.then_inc(s0_ready, 1)
                if i == 19:
                    for hd in range(H):
                        dve.wait_ge(oroot_ready, H * L + hd + 1)
                        link(v.reciprocal(QE[:, hd], QE[:, hd]))
                        link(v.tensor_tensor(Q[:, hd], Q[:, hd], QE[:, hd], ALU.mult))
                        dve.wait_ge(act_emptied, tile[(L, "out_gate", hd)][3])
                        v.scalar_tensor_tensor(out=Q[:, hd], in0=Q[:, hd],
                                               scalar=prm[:, P_HG + H * L + hd:P_HG + H * L + hd + 1],
                                               in1=u[:, hd], op0=ALU.mult, op1=ALU.mult).then_inc(b_ready, 1)
                if i == 20:
                    dve.wait_ge(s0_out[0], 32 * (L + 1))
                    for hd in range(H):
                        dve.wait_ge(b_high, H * L + hd + 1)
                        v.tensor_tensor(blo[:, hd], Q[:, hd], bhi[:, hd].bitcast(F), ALU.subtract).then_inc(b_low, 1)
            add_square(2 * L + 1, KD - 1)
            if L % 2 == 0:
                norm(2 * L + 1)
                for i, (sec, part) in enumerate(FFN):
                    c = first_chunk[(L, "gate")] + i
                    if sec == "up":
                        for j in (0, 1):
                            b = waits_tile(L, sec, 2 * part + j)
                            dve.wait_ge(act_emptied, tile[(L, "gate", 2 * part + j)][3])
                            if part:
                                dve.wait_ge(hid_low, 2 * part)
                            v.tensor_tensor(hf[:, j, :], b[:, 0:T], sg[:, j, :], ALU.mult).then_inc(dve_emptied, 1)
                    if sec == "down" and part % 3 == 2:
                        for j in (0, 1):
                            add_residual(L, sec, 2 * (part // 3) + j)
                    split_low(c + SLOTS)
                    if sec == "up":
                        for j in (0, 1):
                            dve.wait_ge(hid_high, 2 * part + j + 1)
                            v.tensor_tensor(fl[:, 2 * part + j, :], hf[:, j, :], fh[:, 2 * part + j, :].bitcast(F),
                                            ALU.subtract).then_inc(hid_low, 1)
                    if sec == "down" and part % 3 == 2:
                        for j in (2 * (part // 3) - 1, 2 * (part // 3)):
                            if j >= 0:
                                add_square(2 * L + 2, j)

        norm(2 * LAYERS - 1, parts=False)
        for n, (t, hf_) in enumerate(OUTS):
            dve.wait_ge(sum_psum, n + 1)
            v.tensor_copy(acc[0:TOK[t][1], t, 512 * hf_:512 * hf_ + 512], bank[ROW_BANK[n]][0:TOK[t][1], :]).then_inc(
                sum_done, 1)
        link(v.memset(lg[:], 0.0))
        dve.wait_ge(logit_psum, 1)
        link(v.tensor_copy(lg[:, 0:PAIRS], bank[7][:, 0:PAIRS * NE].rearrange("p (t e) -> p t e", e=NE)))
        v.tensor_copy(lg[0:64, PAIRS], bank[7][0:64, PAIRS * NE:NT * NE]).then_inc(lg_ready, 1)
        dve.wait_ge(lg_ready, 1)
        for t in range(NT):
            ins = v.max(top[:, t], lg[:, t])
        link(ins)
        for t in range(NT):
            ins = v.max_index(topi[:, t], top[:, t], lg[:, t])
        link(ins)
        link(v.tensor_copy(topf[:], topi[:]))
        v.tensor_tensor(g1[:, 0], top[:, :, 1], top[:, :, 0], ALU.subtract).then_inc(top_ready, 1)
        row = iota[:, 0:NE].unsqueeze(1).broadcast_to([128, NT, NE])
        link(v.tensor_tensor(m1[:], row, topf[:, :, 0:1].broadcast_to([128, NT, NE]), ALU.is_equal))
        link(v.tensor_tensor(m2[:], row, topf[:, :, 1:2].broadcast_to([128, NT, NE]), ALU.is_equal))
        v.tensor_tensor(mk[:], m1[:], m2[:], ALU.add).then_inc(chosen_ready, 1)
        dve.wait_ge(gap_top, 1)
        link(v.tensor_scalar(g1[:, 1], g1[:, 0], 1.0, None, ALU.add))
        link(v.reciprocal(g1[:, 2], g1[:, 1]))
        link(v.tensor_tensor(g1[:, 3], g1[:, 0], g1[:, 2], ALU.mult))
        link(v.tensor_tensor(m1[:], m1[:], g1[:, 2].unsqueeze(2).broadcast_to([128, NT, NE]), ALU.mult))
        link(v.tensor_tensor(m2[:], m2[:], g1[:, 3].unsqueeze(2).broadcast_to([128, NT, NE]), ALU.mult))
        link(v.tensor_tensor(cmb[:], m1[:], m2[:], ALU.add))
        link(v.memset(slot[:], -1.0))
        dve.wait_ge(rank_psum, 1)
        dve.wait_ge(chosen_ready, 1)
        link(v.tensor_tensor(slot[:, 0:PAIRS], bank[7][:, 0:PAIRS * NE].rearrange("p (t e) -> p t e", e=NE),
                             mk[:, 0:PAIRS], ALU.mult))
        link(v.tensor_tensor(slot[0:64, PAIRS], bank[7][0:64, PAIRS * NE:NT * NE], mk[0:64, PAIRS], ALU.mult))
        link(v.tensor_copy(fullf[:, 0, 0:NE], bank[7][:, NT * NE:(NT + 1) * NE]))
        link(v.tensor_scalar(slot[:, 0:PAIRS], slot[:, 0:PAIRS], -1.0, None, ALU.add))
        v.tensor_scalar(slot[0:64, PAIRS], slot[0:64, PAIRS], -1.0, None, ALU.add).then_inc(shift_done, 1)

        def choose(item, e, shifts=1):
            dve.wait_ge(shift_done, shifts)
            v.tensor_copy(cslot[:], slot[:, :, bass.ds(e, 1)]).then_inc(columns_ready, 1)
            v.tensor_copy(cgate[:], cmb[:, :, bass.ds(e, 1)]).then_inc(columns_ready, 1)
            dve.wait_ge(columns_ready, 2 * item + 2)
            dve.wait_ge(xg_psum, 2 * item)
            for t, (_, sz) in enumerate(TOK):
                ins = v.tensor_scalar(pick[0:sz, t], iota[0:sz], cslot[0:sz, t:t + 1], None, ALU.is_equal)
            ins.then_inc(pick_ready, 1)

        def choose_weighted(item):
            dve.wait_ge(pickt_psum, item)
            for t, (_, sz) in enumerate(TOK):
                ins = v.tensor_scalar(pickw[0:sz, t], iota[0:sz], cslot[0:sz, t:t + 1], cgate[0:sz, t:t + 1],
                                      ALU.is_equal, ALU.mult)
            ins.then_inc(pickw_ready, 1)

        def expert_in_low(item):
            for hh in range(2):
                dve.wait_ge(xg_high, 2 * item + hh + 1)
                v.tensor_tensor(xel[:, 4 * hh:4 * hh + 4, :].rearrange("p k s -> p (k s)"), bank[6 + hh][:],
                                xeh[:, 4 * hh:4 * hh + 4, :].rearrange("p k s -> p (k s)").bitcast(F),
                                ALU.subtract).then_inc(xg_low, 1)

        def hidden_low(item, j):
            ts = group_tiles(j)
            dve.wait_ge(heh_ready, NG * item + j + 1)
            v.tensor_tensor(hel[:, ts[0]:ts[-1] + 1, :].rearrange("p k s -> p (k s)"), bank[4 + j % 2][:, 0:128 * len(ts)],
                            heh[:, ts[0]:ts[-1] + 1, :].rearrange("p k s -> p (k s)").bitcast(F),
                            ALU.subtract).then_inc(hel_ready, 1)

        def low_of(item, i):
            dve.wait_ge(high_done, NEC * item + (NDENSE + i + 1))
            n = width(i)
            v.tensor_tensor(wlo[:, i % SLOTS, 0:n], raw[:, i % SLOTS, 0:n], whi[:, i % SLOTS, 0:n].bitcast(F),
                            ALU.subtract).then_inc(low_done, 1)

        def expert(item, e, first, ahead, shifts=1):
            if first:
                choose(item, e, shifts)
                for i in range(SLOTS):
                    low_of(item, i)
                expert_in_low(item)
                choose_weighted(item)
            for i, (kind, j, part, k0, kt, c0, cols) in enumerate(ECH):
                closed = i == closing.get((kind, j))
                if kind == "up" and closed:
                    dve.wait_ge(pe_mark, NEC * item + (MB + i + 1))
                    dve.wait_ge(gate_emptied, NG * item + (j + 1))
                    v.tensor_tensor(He[:, c0:c0 + cols], bank[1 + 2 * (j % 2)][:, 0:cols], sge[:, j % 2, 0:cols],
                                    ALU.mult).then_inc(he_ready, 1)
                if i + SLOTS < NEC or ahead:
                    low_of(item, i + SLOTS)
                if kind == "up" and closed:
                    if j:
                        hidden_low(item, j - 1)
                    if j == NG - 3 and ahead:
                        choose(item + 1, e + 1)
                    if j == NG - 1:
                        if ahead:
                            expert_in_low(item + 1)
                        hidden_low(item, j)
                if kind == "down" and j == 1 and ahead:
                    choose_weighted(item + 1)
            for n, (t, hf_) in enumerate(OUTS):
                sz = TOK[t][1]
                part = acc[0:sz, t, 512 * hf_:512 * hf_ + 512]
                dve.wait_ge(sum_psum, NO * item + (NO + n + 1))
                v.tensor_tensor(part, part, bank[SUM_BANK[n]][0:sz, :], ALU.add).then_inc(sum_done, 1)

        choose(0, 0)
        expert_in_low(0)
        choose_weighted(0)
        for n in range(1, BLOCKS - 1):
            link(v.tensor_scalar(fullf[:, 0, NE * n:NE * n + NE], fullf[:, 0, 0:NE], -float(CAP * n), None, ALU.add))
        link(v.tensor_scalar(fullf[:, 1], fullf[:, 0], float(CAP), None, ALU.is_gt))
        link(v.memset(fullf[:, 0], 1.0))
        link(v.tensor_tensor_scan(fullf[:, 2], fullf[:, 0], fullf[:, 1], float(NE), ALU.mult, ALU.add))
        link(v.tensor_tensor(fullf[:, 2], fullf[:, 2], fullf[:, 1], ALU.subtract))
        link(v.tensor_copy(full[:], fullf[:, 1]))
        v.tensor_copy(items[:], fullf[:, 2]).then_inc(table_ready, 1)
        with dve.Fori(0, NE - 1) as e:
            expert(e, e, False, True)
        expert(NE - 1, NE - 1, False, False)

        dve.wait_ge(table_ready, 1)
        with dve.Fori(1, BLOCKS) as b:
            dve.wait_ge(pick_ready, NE)
            dve.wait_ge(shift_done, b)
            v.tensor_scalar(slot[:], slot[:], -float(CAP), None, ALU.add).then_inc(shift_done, 1)
            with dve.Fori(0, NE) as e:
                n = b * NE + e - NE
                more = dve.value_load(full[0:1, bass.ds(n, 1)], min_val=0, max_val=1)
                item = dve.value_load(items[0:1, bass.ds(n, 1)], min_val=NE, max_val=NE + NMORE)
                with dve.If(more > 0):
                    expert(item, e, True, False, b + 1)
                    dve.wait_ge(sum_done, NO * item + 2 * NO)
                    v.memset(cslot[:], 0.0)
        dve.wait_ge(sum_done, NO * (NE + 1))
        dve.wait_ge(gfin_in, 16)
        for t, (_, sz) in enumerate(TOK):
            v.tensor_tensor_reduce(out=He[0:sz, 0:D], in0=acc[0:sz, t], in1=acc[0:sz, t], scale=1.0, scalar=0.0,
                                   op0=ALU.mult, op1=ALU.add, accum_out=ssf[0:sz, t:t + 1]).then_inc(fsq_ready, 1)
            dve.wait_ge(froot_ready, t + 1)
            link(v.reciprocal(rf[0:sz, t:t + 1], rf[0:sz, t:t + 1]))
            v.scalar_tensor_tensor(out=acc[0:sz, t], in0=acc[0:sz, t], scalar=rf[0:sz, t:t + 1], in1=gfin[0:sz],
                                   op0=ALU.mult, op1=ALU.mult).then_inc(fout_ready, 1)

    @block.tensor
    def _(pe):
        mm = nc.tensor.matmul

        def opens(L, sec, t):
            b, _, _, _, prev = tile[(L, sec, t)]
            if prev:
                pe.wait_ge(emptied_sem(tile[prev][2]), tile[prev][3])
            return bank[b]

        def products(L, sec, c, tiles, first, last, mh, ml, k0=0, ready=None):
            _, kt, cols = chunks[c]
            s = c % SLOTS
            pe.wait_ge(low_done, c + 1)
            for n, t in enumerate(tiles):
                b = opens(L, sec, t) if first else bank[tile[(L, sec, t)][0]]
                for k in range(kt):
                    if ready and n == 0:
                        ready(k)
                    w = slice(k * cols + 128 * n, k * cols + 128 * n + 128)
                    mm(b[:, 0:T], whi[:, s, w], mh[:, k0 + k, :], start=first and k == 0, stop=False)
                    mm(b[:, 0:T], whi[:, s, w], ml[:, k0 + k, :], start=False, stop=False)
                    ins = mm(b[:, 0:T], wlo[:, s, w], mh[:, k0 + k, :], start=False, stop=last and k == kt - 1)
                if last or n == len(tiles) - 1:
                    ins.then_inc(pe_mark, 1)

        def row_products(L, sec, c, part):
            s = c % SLOTS
            pe.wait_ge(low_done, c + 1)
            for t, (t0, sz) in enumerate(TOK):
                b = opens(L, sec, t) if part == 0 else bank[tile[(L, sec, t)][0]]
                for k in range(4):
                    w = slice(k * DA, (k + 1) * DA)
                    kk = 4 * part + k
                    mm(b[0:sz, :], xh[:, kk, t0:t0 + sz], whi[:, s, w], start=kk == 0, stop=False)
                    mm(b[0:sz, :], xh[:, kk, t0:t0 + sz], wlo[:, s, w], start=False, stop=False)
                    ins = mm(b[0:sz, :], xl[:, kk, t0:t0 + sz], whi[:, s, w], start=False, stop=kk == KD - 1)
                if part == 1 or t == NT - 1:
                    ins.then_inc(pe_mark, 1)

        def mean_square(n):
            pe.wait_ge(summed, KD * (n + 1))
            mm(bank[4][:, 0:T], ones[:], ssum[:], start=True, stop=True).then_inc(stat_psum, 1)

        pe.wait_ge(consts_ready, 1)
        pe.wait_ge(rows_in, 64)
        nc.tensor.transpose(bank[7][:, 0:NROW], prow[:], ident[0:NROW, 0:NROW]).then_inc(prm_psum, 1)
        pe.wait_ge(x_in[0], 16)
        pe.wait_ge(x_in[1], 16)
        for j in range(KD):
            if j >= 4:
                pe.wait_ge(h_ready, j - 3)
            for t, (t0, sz) in enumerate(TOK):
                ins = nc.tensor.transpose(bank[j % 4][:, t0:t0 + sz], xt[0:sz, t, 128 * j:128 * j + 128],
                                          ident[0:sz, 0:sz])
            ins.then_inc(xt_psum, 1)
        mean_square(0)
        pe.wait_ge(h_ready, KD)

        for L in range(LAYERS):
            if L:
                mean_square(2 * L)
            ns = 2 * L

            def normed(k, ns=ns):
                pe.wait_ge(xh_ready, KD * ns + k + 1)
                pe.wait_ge(xl_ready, KD * ns + k + 1)

            for i, (sec, part) in enumerate(MIX):
                c = base(L) + i
                if sec in ("value", "v"):
                    row_products(L, sec, c, part)
                elif sec == "branch_a":
                    products(L, sec, c, range(4 * part, 4 * part + 4), True, True, ahi, alo,
                             ready=lambda k: (pe.wait_ge(a_low, H * L + k + 1)))
                elif sec == "branch_b":
                    products(L, sec, c, range(4 * part, 4 * part + 4), True, True, bhi, blo,
                             ready=lambda k: (pe.wait_ge(b_low, H * L + k + 1)))
                elif sec == "w_out":
                    products(L, sec, c, (2 * part, 2 * part + 1), True, True, xh, xl,
                             ready=lambda k: (pe.wait_ge(merged_low, KD * L + k + 1)))
                else:
                    products(L, sec, c, (2 * part, 2 * part + 1), True, True, xh, xl,
                             ready=normed if i == 0 else None)
                if i == 0:
                    pe.wait_ge(layer_in, 64 * (L + 1))
                    pe.wait_ge(prm_ready, 1)
                    if L:
                        pe.wait_ge(ostat_psum, H * L)
                        pe.wait_ge(oroot_ready, H * L)
                    for g in range(H):
                        ins = nc.tensor.transpose(bank[7][:, 128 * g:128 * g + 128], wsp[:, g, :], ident[:])
                    ins.then_inc(wst_psum, 1)
                if i == 1:
                    pe.wait_ge(wst_ready, L + 1)
                    for g in range(H):
                        ins = mm(bank[7][0:64, 64 * g:64 * g + 64], r8[:],
                                 wst[0:LS, g, 0:LS].unsqueeze(1).broadcast_to([LS, NSEQ, LS]), start=True, stop=True)
                    ins.then_inc(wsd_psum, 1)
                if i == 5:
                    pe.wait_ge(kdec_ready, L + 1)
                    for t, (t0, sz) in enumerate(TOK):
                        for hd in range(H):
                            ins = nc.tensor.transpose(bank[4 + t][0:sz, 128 * hd:128 * hd + 128], Z[:, hd, t0:t0 + sz], ident[:])
                        ins.then_inc(kdt_psum, 1)
                if 6 <= i < 7 + NLEV:
                    li = i - 6
                    if li == 0:
                        pe.wait_ge(kdt_ready, NT * (L + 1))
                        lhs, rhs = K, Q
                    else:
                        pe.wait_ge(lev_prod, NLEV * L + li)
                        pe.wait_ge(score_ready, score_count(L, li))
                        lhs, rhs = Z, Z
                    lv = ([0] + LEVELS)[li]
                    for p in range(SCORES if lv <= LS // 2 else PAIRS):
                        t0, sz = TOK[p]
                        for hd in range(H):
                            ins = mm(bank[4 + p][0:sz, sz * hd:sz * hd + sz], lhs[:, hd, t0:t0 + sz],
                                     rhs[:, hd, t0:t0 + sz], start=True, stop=True)
                        ins.then_inc(score_psum, 1)
                if 9 <= i < 9 + H:
                    g = i - 9
                    if g == 0:
                        pe.wait_ge(vn_ready, NT * (L + 1))
                        pe.wait_ge(wsd_ready, H * (L + 1))
                    else:
                        pe.wait_ge(a_ready, H * L + g)
                    for t, (t0, sz) in enumerate(TOK):
                        w = wst[:, g, :] if t < PAIRS else wsd[:, g, :]
                        ins = mm(bank[7][:, t0:t0 + sz], vn[0:sz, t, 128 * g:128 * g + 128], w, start=True, stop=True)
                    ins.then_inc(mix_psum, 1)
                if i == 13:
                    pe.wait_ge(score_ready, NSCORE * (L + 1))
                    pe.wait_ge(a_ready, H * (L + 1))
                    for n in range(NPC):
                        p0 = CH * (n % 2)
                        for hd in range(H):
                            cs = slice(128 * hd, 128 * hd + 128)
                            ins = mm(bank[4 + n][:, cs], kdt[p0:p0 + CH, n // 2, cs], V[p0:p0 + CH, n // 2, cs],
                                     start=True, stop=True)
                        ins.then_inc(upd_psum, 1)
                if i == 14:
                    pe.wait_ge(state_ready, NPC * (L + 1))
                    for hd in range(H):
                        b = bank[4 + hd]
                        cs = slice(128 * hd, 128 * hd + 128)
                        for p in range(PAIRS):
                            mm(b[:, 128 * p:128 * p + 128], V[:, p, cs], sc[:, p, hd, :], start=p == 0, stop=False)
                        for n in range(1, NPC):
                            S = (S12 if n - 1 < 2 else S34)[:, (n - 1) % 2]
                            mm(b[:, CH * n:CH * n + CH], S[:, hd], QE[:, hd, CH * n:CH * n + CH], start=False, stop=False)
                        mm(b[:, TP:T], V[0:64, PAIRS, cs], scs[:, hd, :], start=False, stop=True).then_inc(o_psum, 1)
                if 15 <= i < 15 + H:
                    hd = i - 15
                    cs = slice(128 * hd, 128 * hd + 128)
                    st = s0[hd % 2]
                    pe.wait_ge(s0_in[hd % 2], 16 * (2 * L + hd // 2 + 1))
                    if hd:
                        pe.wait_ge(s0_ready, H * L + hd)
                    else:
                        pe.wait_ge(o_ready, H * (L + 1))
                    for b in range(NSEQ):
                        ins = mm(bank[6][:, LS * b:LS * b + LS], st[:, b, :], QE[:, hd, TP + LS * b:TP + LS * b + LS],
                                 start=b == 0, stop=b == NSEQ - 1, skip_group_check=True)
                    ins.then_inc(so_psum, 1)
                    pe.wait_ge(vex_ready, H * L + hd + 1)
                    for b in (0, 1):
                        ins = mm(bank[4 + b][:], kdt[0:64, PAIRS, cs], vex[:, 4 * b:4 * b + 4, :], start=True, stop=True)
                    ins.then_inc(su_psum, 1)
                if i == 19:
                    pe.wait_ge(osq_ready, L + 1)
                    for hd in range(H):
                        mm(bank[4 + hd][:, 0:T], ones[:], osq[:, hd, :], start=True, stop=True).then_inc(ostat_psum, 1)
            mean_square(2 * L + 1)
            if L % 2 == 0:
                ns = 2 * L + 1

                def normed(k, ns=ns):
                    pe.wait_ge(xh_ready, KD * ns + k + 1)
                    pe.wait_ge(xl_ready, KD * ns + k + 1)

                for i, (sec, part) in enumerate(FFN):
                    c = first_chunk[(L, "gate")] + i
                    if sec == "down":
                        k0, kt = KCUT[part % 3]
                        t = 2 * (part // 3)
                        products(L, sec, c, (t, t + 1), part % 3 == 0, part % 3 == 2, fh, fl, k0=k0,
                                 ready=lambda k, k0=k0: pe.wait_ge(hid_low, k0 + k + 1))
                    else:
                        products(L, sec, c, (2 * part, 2 * part + 1), True, True, xh, xl,
                                 ready=normed if i == 0 else None)

        for src, psum, ready, before in ((h, sum_psum, sum_done, None), (xn, hn_psum, y_ready, sum_done)):
            if before is None:
                pe.wait_ge(dve_emptied, emptied["dve"])
            else:
                pe.wait_ge(xn_ready, KD * 2 * LAYERS)
            for n, (t, hf_) in enumerate(OUTS):
                t0, sz = TOK[t]
                if before is not None:
                    pe.wait_ge(before, n + 1)
                for k in range(4):
                    ins = nc.tensor.transpose(bank[ROW_BANK[n]][0:sz, 128 * k:128 * k + 128],
                                              src[:, 4 * hf_ + k, t0:t0 + sz], ident[:])
                ins.then_inc(psum, 1)
        pe.wait_ge(router_in, 16)
        for t, (t0, sz) in enumerate(TOK):
            for k in range(KD):
                ins = mm(bank[7][0:sz, NE * t:NE * t + NE], xn[:, k, t0:t0 + sz], rw[:, k, :], start=k == 0, stop=k == KD - 1)
        ins.then_inc(logit_psum, 1)
        pe.wait_ge(chosen_ready, 1)
        for t, (_, sz) in enumerate(TOK):
            for q in range(t):
                mm(bank[7][0:sz, NE * t:NE * t + NE], ones[:, 0:sz], mk[:, q, :], start=q == 0, stop=False)
            mm(bank[7][0:sz, NE * t:NE * t + NE], upper[0:sz, 0:sz], mk[0:sz, t, :], start=t == 0, stop=True)
        for t, (_, sz) in enumerate(TOK):
            ins = mm(bank[7][:, NE * NT:NE * NT + NE], ones[0:sz, :], mk[0:sz, t, :], start=t == 0, stop=t == NT - 1)
        ins.then_inc(rank_psum, 1)

        def gather(item):
            pe.wait_ge(pick_ready, item + 1)
            for hh in range(2):
                for k in range(4):
                    for t, (_, sz) in enumerate(TOK):
                        kk = 4 * hh + k
                        ins = mm(bank[6 + hh][:, 128 * k:128 * k + 128], hn[0:sz, t, 128 * kk:128 * kk + 128],
                                 pick[0:sz, t, :], start=t == 0, stop=t == NT - 1)
                ins.then_inc(xg_psum, 1)

        def hidden_rows_turned(item, j):
            pe.wait_ge(he_ready, NG * item + (j + 1))
            if j >= 2:
                pe.wait_ge(hel_ready, NG * item + (j - 1))
            for n, t in enumerate(group_tiles(j)):
                ins = nc.tensor.transpose(bank[4 + j % 2][:, 128 * n:128 * n + 128], He[:, 128 * t:128 * t + 128], ident[:])
            ins.then_inc(het_psum, 1)

        def expert(item, first, ahead):
            if first:
                pe.wait_ge(sum_done, NO * item + NO)
                gather(item)
            for i, (kind, j, part, k0, kt, c0, cols) in enumerate(ECH):
                s = i % SLOTS
                pe.wait_ge(low_done, NEC * item + (NDENSE + i + 1))
                if kind != "down":
                    b = bank[(kind == "up") + 2 * (j % 2)]
                    if part == 0:
                        if j == 0:
                            pe.wait_ge(y_ready, 2 * item + NO)
                        elif j == 1:
                            pe.wait_ge(sum_done, NO * item + NO)
                        else:
                            pe.wait_ge(gate_emptied if kind == "gate" else he_ready, NG * item + (j - 1))
                    for k in range(kt):
                        kk = k0 + k
                        if j == 0 and kk % 4 == 0:
                            pe.wait_ge(xg_low, 2 * item + (kk // 4 + 1))
                        w = slice(k * cols, (k + 1) * cols)
                        mm(b[:, 0:cols], xeh[:, kk, :], whi[:, s, w], start=kk == 0, stop=False)
                        mm(b[:, 0:cols], xeh[:, kk, :], wlo[:, s, w], start=False, stop=False)
                        ins = mm(b[:, 0:cols], xel[:, kk, :], whi[:, s, w], start=False, stop=kk == KD - 1)
                    ins.then_inc(pe_mark, 1)
                    if kind == "up" and i == closing[(kind, j)]:
                        if j == 1:
                            pe.wait_ge(sum_done, NO * item + NO)
                        if j:
                            hidden_rows_turned(item, j - 1)
                        if j == NG - 1:
                            if ahead:
                                gather(item + 1)
                            hidden_rows_turned(item, j)
                            pe.wait_ge(hel_ready, NG * item + (NG - 1))
                            pe.wait_ge(pickw_ready, item + 1)
                            for t, (t0, sz) in enumerate(TOK):
                                ins = nc.tensor.transpose(bank[4][:, t0:t0 + sz], pickw[0:sz, t, :], ident[0:sz, 0:sz])
                            ins.then_inc(pickt_psum, 1)
                    continue
                if j == 0:
                    pe.wait_ge(he_ready, NG * item + (NG - 1))
                for k in range(kt):
                    kk = k0 + k
                    if kk % 4 == 0:
                        pe.wait_ge(hel_ready, NG * item + (kk // 4 + 1))
                    for hh in range(2):
                        w = slice(k * cols + 512 * hh, k * cols + 512 * hh + 512)
                        mm(bank[hh][:], heh[:, kk, :], whi[:, s, w], start=kk == 0, stop=False)
                        mm(bank[hh][:], heh[:, kk, :], wlo[:, s, w], start=False, stop=False)
                        ins = mm(bank[hh][:], hel[:, kk, :], whi[:, s, w], start=False, stop=kk == KF - 1)
                ins.then_inc(pe_mark, 1)
            pe.wait_ge(pickt_ready, item + 1)
            pe.wait_ge(y_ready, 2 * item + (NO + 2))
            pe.wait_ge(he_ready, NG * item + NG)
            pe.wait_ge(hel_ready, NG * item + NG)
            if ahead:
                pe.wait_ge(xg_low, 2 * item + 4)
            for n, (t, hf_) in enumerate(OUTS):
                t0, sz = TOK[t]
                mm(bank[SUM_BANK[n]][0:sz, :], pickt[:, t0:t0 + sz], Y[:, 512 * hf_:512 * hf_ + 512],
                   start=True, stop=True).then_inc(sum_psum, 1)

        pe.wait_ge(y_ready, NO)
        pe.wait_ge(sum_done, NO)
        gather(0)
        pe.wait_ge(table_ready, 1)
        with pe.Fori(0, NE - 1) as e:
            expert(e, False, True)
        expert(NE - 1, False, False)
        extra_blocks(pe, table_ready, lambda item, n: expert(item, True, False))

    ctx.close()


_OUTS = {"y_prompt": (1, 256, 1024), "y_sample": (8, 8, 1024), "prompt_state": (2, 1, 4, 128, 128),
         "sample_state": (2, 8, 4, 128, 128), "v_rows": (2, 8, 8, 512)}


def kernel(**inputs):
    import numpy as np
    import concourse.bacc as bacc
    from concourse.bass_utils import run_bass_kernel_spmd

    nc = bacc.Bacc("TRN2", target_bir_lowering=False, num_devices=1)
    arrays, ins, outs = {}, {}, {}
    for name, a in inputs.items():
        arrays["in_" + name] = np.ascontiguousarray(a)
        ins[name] = nc.dram_tensor("in_" + name, a.shape, mybir.dt.float32, kind="ExternalInput").ap()
    for name, shape in _OUTS.items():
        outs[name] = nc.dram_tensor("out_" + name, shape, mybir.dt.float32, kind="ExternalOutput").ap()
    hybrid_trunk_program(nc, ins, outs)
    r = run_bass_kernel_spmd(nc, [arrays], core_ids=[0])
    return tuple(r.results[0]["out_" + name] for name in _OUTS)
```

```python
import concourse.bass as bass
from concourse import mybir
from contextlib import ExitStack


def hybrid_trunk_program(nc, A, OUT):
    F = mybir.dt.float32
    R = mybir.dt.float32r
    I32 = mybir.dt.int32
    U32 = mybir.dt.uint32
    ALU = mybir.AluOpType
    ACT = mybir.ActivationFunctionType

    D = A["x_prompt"].shape[2]
    TP = A["x_prompt"].shape[1]
    NSEQ, LS = A["x_sample"].shape[0], A["x_sample"].shape[1]
    T = TP + NSEQ * LS
    LAYERS = A["w_in"].shape[0]
    KD = D // 128
    DA = A["ln_v_g"].shape[1]
    H = DA // 128
    FF = A["dense_w_gate"].shape[2]
    KF = FF // 128
    NE = A["router_w"].shape[2]
    TOK = [(0, 128), (128, 128), (256, 64)]
    NT = len(TOK)
    CH = 64
    NPC = TP // CH
    PAIRS = TP // 128
    EPS = 1e-6
    LEVELS = [32, 16, 8, 4, 2, 1]
    COL = {"u": 0, "v": DA, "q": 2 * DA, "forget": 3 * DA, "value": 4 * DA, "out_gate": 5 * DA,
           "gate_a": 6 * DA, "gate_b": 6 * DA + D}

    CHUNK = 2048
    SLOTS = 3
    PIECE = CHUNK // 2
    RING = 6
    BANKS = 4
    chunks = []
    mark_after = []
    tile = {}
    first_chunk = {}
    order = []
    marks = 0
    emptied = {"act": 0, "dve": 0}

    def rows(w, k0, kt, c0, cols):
        return w[k0 * 128:(k0 + kt) * 128, c0:c0 + cols].rearrange("(k p) n -> p k n", p=128)

    def add_chunk(key, src, kt, cols, opens, closes, by):
        nonlocal marks
        first_chunk.setdefault(key[:2], len(chunks))
        for t in opens:
            n = len(order)
            order.append((key[0], key[1], t))
            tile[order[-1]] = [n % BANKS, None, by, None, order[n - BANKS] if n >= BANKS else None]
        marks += 1
        mark_after.append(marks)
        for t in closes:
            marks += 1
            emptied[by] += 1
            tile[(key[0], key[1], t)][1] = marks
            tile[(key[0], key[1], t)][3] = emptied[by]
        if not closes:
            marks += 1
        chunks.append((src, kt, cols))
        mark_after.append(marks)

    MIX = [("forget", 0), ("forget", 1), ("q", 0), ("q", 1), ("value", 0), ("value", 1), ("v", 0), ("v", 1),
           ("u", 0), ("u", 1)] + [("gate_a", i) for i in range(4)] + [("branch_a", 0), ("branch_a", 1),
           ("out_gate", 0), ("out_gate", 1)] + [("gate_b", i) for i in range(4)] + [
           ("branch_b", 0), ("branch_b", 1)] + [("w_out", i) for i in range(4)]
    KCUT = [(0, 8), (8, 8), (16, KF - 16)]
    FFN = [(s, i) for i in range(KF // 2) for s in ("gate", "up")] + \
          [("down", 3 * i + j) for i in range(4) for j in range(3)]
    for L in range(LAYERS):
        for sec, i in MIX:
            if sec in ("value", "v"):
                add_chunk((L, sec), rows(A["w_in"][L], 4 * i, 4, COL[sec], DA), 4, DA,
                          range(NT) if i == 0 else (), () if i == 0 else range(NT), "act")
            elif sec in ("branch_a", "branch_b"):
                w = A["w_" + sec][L]
                add_chunk((L, sec), rows(w, 0, H, 512 * i, 512), H, 512,
                          range(4 * i, 4 * i + 4), range(4 * i, 4 * i + 4), "dve")
            elif sec == "w_out":
                add_chunk((L, sec), rows(A["w_out"][L], 0, KD, 256 * i, 256), KD, 256,
                          (2 * i, 2 * i + 1), (2 * i, 2 * i + 1), "dve")
            else:
                add_chunk((L, sec), rows(A["w_in"][L], 0, KD, COL[sec] + 256 * i, 256), KD, 256,
                          (2 * i, 2 * i + 1), (2 * i, 2 * i + 1), "act")
        if L % 2 == 0:
            for sec, i in FFN:
                if sec == "down":
                    k0, kt = KCUT[i % 3]
                    ts = (2 * (i // 3), 2 * (i // 3) + 1)
                    add_chunk((L, sec), rows(A["dense_w_down"][L // 2], k0, kt, 256 * (i // 3), 256), kt, 256,
                              ts if i % 3 == 0 else (), ts if i % 3 == 2 else (), "dve")
                else:
                    add_chunk((L, sec), rows(A["dense_w_" + sec][L // 2], 0, KD, 256 * i, 256), KD, 256,
                              (2 * i, 2 * i + 1), (2 * i, 2 * i + 1), "act" if sec == "gate" else "dve")
    NDENSE = len(chunks)
    assert NDENSE % SLOTS == 0 and 2 * SLOTS == RING

    groups = [(512 * j, min(512, FF - 512 * j)) for j in range(-(-FF // 512))]
    ECH = []
    for j, (c0, cols) in enumerate(groups):
        for s in ("gate", "up"):
            kt = CHUNK // cols
            for part in range(KD // kt):
                ECH.append((s, j, part, part * kt, kt, c0, cols))
    for j in range(KF // 2):
        ECH.append(("down", j, 0, 2 * j, 2, 0, D))
    NEC = len(ECH)
    assert NEC % SLOTS == 0
    NG = len(groups)
    closing = {(s, j): max(i for i, x in enumerate(ECH) if x[0] == s and x[1] == j)
               for s in ("gate", "up") for j in range(NG)}
    CAP = 128

    at = [-(-nc.sbuf_base // 32) * 32]

    def place(name, shape, dt=F, offset=None):
        size = 4
        for s in shape[1:]:
            size *= s
        if offset is None:
            offset = at[0]
            at[0] += -(-size // 32) * 32
        return nc.alloc_sbuf_tensor_at(name, shape, dt, offset=offset)

    raw = place("weights_raw", [128, SLOTS, CHUNK])
    whi = place("weights_high", [128, RING, PIECE], R)
    wlo = place("weights_low", [128, RING, PIECE], R)
    h = place("residual", [128, KD, T])
    m_at = at[0]
    xn = place("normed_or_merged", [128, KD, T])
    xh_at = at[0]
    xh = place("moving_high", [128, KD, T], R)
    xl_at = at[0]
    xl = place("moving_low", [128, KD, T], R)
    ident = place("identity", [128, 128])
    ones = place("ones", [128, 128])
    upper = place("upper_ones", [128, 128])
    iota = place("iota_row", [128, 128])
    lmask = place("level_masks", [128, len(LEVELS) + 1, 128], I32)
    smask = place("scan_keep", [128, T])
    bmask = place("sequence_mask", [64, NSEQ])
    r8 = place("row_spread", [LS, NSEQ * LS])
    eps_t = place("eps", [128, 1])
    NROW = 2 * LAYERS * KD + 2 * LAYERS * H
    prow = place("param_rows", [NROW, 128])
    prm = place("param_columns", [128, NROW])
    lbt = place("lower_bound_terms", [128, 5, H])
    wsp = place("spatial_raw", [128, H, 128])
    wst = place("spatial_transposed", [128, H, 128])
    wsd = place("spatial_sample", [64, H, 64])
    bsp = place("spatial_bias", [128, H, 128])
    ln_at = at[0]
    lng = place("ln_gain", [128, DA])
    lnb = place("ln_shift", [128, DA])
    sq = place("squares", [128, 2, T])
    ssum = place("square_sum", [128, T])
    rinv = place("inverse_rms", [128, T])
    el = place("chunk_decay", [128, H, NPC + NSEQ])
    bst = place("ln_stats", [128, NT, 6])
    bag = place("ln_mean_var", [128, NT, 2])
    tmp = place("branch_product", [128, 2, T])
    cmb = place("combine", [128, NT, NE])
    slot = place("slot_of_token", [128, NT, NE])
    cslot = place("slot_now", [128, NT])
    cgate = place("gate_now", [128, NT])
    BLOCKS = -(-T // CAP)
    NMORE = (BLOCKS - 1) * NE
    full = place("more_blocks", [128, NMORE + 1], I32)
    items = place("block_items", [128, NMORE], I32)
    fullf = place("more_blocks_f", [128, 3, NMORE])
    rw = place("router", [128, KD, NE])
    region = at[0]

    def later(name, shape, dt, offset):
        return place(name, shape, dt, offset)

    W5 = 4 * H * T
    ahi = later("a_high", [128, H, T], R, region)
    alo = later("a_low", [128, H, T], R, region + W5)
    gb = later("gate_b", [128, KD, T], F, region)
    o = region + 2 * W5
    u = later("u_or_out_gate", [128, H, T], F, o); o += W5
    V = later("value", [128, NT, DA], F, o); o += 4 * NT * DA
    vn_at = o
    vn = later("v_normed", [128, NT, DA], F, o)
    o += 4 * NT * DA
    sc = later("scores", [128, PAIRS, H, 128], F, o)
    scs = later("scores_sample", [64, H, 64], F, o + 4 * PAIRS * H * 128); o += 4 * PAIRS * H * 128 + 4 * H * 64
    z_at = o
    Z = later("level_product", [128, H, T], F, o); o += W5
    e_at = o
    E = later("level_decay", [128, H, T], F, o); o += W5
    Q = later("query", [128, H, T], F, o); o += W5
    k_at = o
    K = later("key", [128, H, T], F, o); o += W5
    g_at = o
    G = later("log_decay", [128, H, T], F, o); o += W5
    kdt = later("key_decayed_tok", [128, NT, DA], F, o)
    osq = later("out_squares", [128, H, T], F, o); o += 4 * NT * DA
    QE = later("query_decayed", [128, H, T], F, o); o += W5
    assert o <= nc.sbuf_usable_end, (o, nc.sbuf_usable_end)
    S12 = later("state_1_2", [128, 2, H, 128], F, e_at)
    S34 = later("state_3_4", [128, 2, H, 128], F, z_at)
    vex = later("value_by_sequence", [64, NSEQ, 128], F, k_at)
    s0 = [later("state_sample_even", [128, NSEQ, 128], F, g_at), later("state_sample_odd", [128, NSEQ, 128], F, e_at)]
    bhi = later("b_high", [128, H, T], R, k_at)
    blo = later("b_low", [128, H, T], R, g_at)
    xt = later("x_rows", [128, NT, D], F, z_at)
    fh = later("hidden_high", [128, KF, T], R, region)
    fl = later("hidden_low", [128, KF, T], R, region + 4 * KF * T)
    o = region + 8 * KF * T
    sg = later("silu_gate", [128, 2, T], F, o)
    hf = later("hidden", [128, 2, T], F, o + 8 * T)
    assert o + 16 * T <= nc.sbuf_usable_end
    o = region
    acc = later("sum_rows", [128, NT, D], F, o); o += 4 * NT * D
    hn = later("normed_rows", [128, NT, D], F, o); o += 4 * NT * D
    He = later("expert_hidden", [128, FF], F, o); o += 4 * FF
    heh = later("expert_hidden_high", [128, KF, CAP], R, o); o += 4 * KF * CAP
    hel = later("expert_hidden_low", [128, KF, CAP], R, o); o += 4 * KF * CAP
    assert o <= nc.sbuf_usable_end
    xeh = later("expert_in_high", [128, KD, CAP], R, xh_at)
    xel = later("expert_in_low", [128, KD, CAP], R, xl_at)
    sge = later("expert_silu", [128, 2, 512], F, xh_at + 4 * KD * CAP)
    assert 8 * KD * CAP + 4 * NT * CAP <= 4 * KD * T and 4 * T + 8 * D <= 4 * KD * T
    pick = later("pick", [128, NT, CAP], F, xh_at + 8 * KD * CAP)
    pickt = later("pick_t", [128, T], R, m_at)
    Yh = later("expert_out_high", [128, D], R, m_at + 4 * T)
    Yl = later("expert_out_low", [128, D], R, m_at + 4 * T + 4 * D)
    lo_ = xl_at + 4 * KD * CAP
    lg = later("logits", [128, NT, 8], F, lo_)
    top = later("top_values", [128, NT, 8], F, lo_ + 96)
    topi = later("top_indices", [128, NT, 8], U32, lo_ + 192)
    topf = later("top_indices_f", [128, NT, 8], F, lo_ + 288)
    m1 = later("first_mask", [128, NT, 8], F, lo_ + 384)
    m2 = later("second_mask", [128, NT, 8], F, lo_ + 480)
    mk = later("chosen", [128, NT, 8], F, lo_ + 576)
    g1 = later("gate_terms", [128, 4, NT], F, lo_ + 672)
    cf = later("counts_f", [128, NE], F, lo_ + 736)
    gfin = later("final_gain", [128, D], F, ln_at)
    ssf = later("final_square_sum", [128, NT], F, lo_ + 800)
    rf = later("final_inverse_rms", [128, NT], F, lo_ + 832)

    ctx = ExitStack()
    bank = [ctx.enter_context(nc.psum_tensor(f"bank{i}", [128, 512], F)) for i in range(8)]

    def sem(name):
        return ctx.enter_context(nc.semaphore(name))

    raw_full = [sem(f"raw_full_{i}") for i in range(SLOTS)]
    high_done = sem("high_done")
    low_done = sem("low_done")
    pe_mark = sem("pe_mark")
    act_emptied = sem("act_emptied")
    dve_emptied = sem("dve_emptied")
    act_link = sem("act_link")
    dve_link = sem("dve_link")
    pool_link = sem("pool_link")
    first_ready = sem("eps_ones_identity_ready")
    consts_ready = sem("other_constants_ready")
    x_in = [sem("x_prompt_in"), sem("x_sample_in")]
    rows_in = sem("param_rows_in")
    layer_in = sem("layer_params_in")
    router_in = sem("router_in")
    gfin_in = sem("final_gain_in")
    prm_psum = sem("param_columns_psum")
    prm_ready = sem("param_columns_ready")
    lb_exp = sem("lower_bound_exp")
    lb_ready = sem("lower_bound_ready")
    xt_psum = sem("x_transposed_psum")
    h_ready = sem("residual_ready")
    squared = sem("squared")
    summed = sem("square_summed")
    stat_psum = sem("mean_square_psum")
    root_ready = sem("root_ready")
    rinv_ready = sem("inverse_rms_ready")
    xn_ready = sem("normed_ready")
    xh_ready = sem("moving_high_ready")
    xl_ready = sem("moving_low_ready")
    wst_psum = sem("spatial_transposed_psum")
    wst_ready = sem("spatial_transposed_ready")
    wsd_psum = sem("spatial_sample_psum")
    wsd_ready = sem("spatial_sample_ready")
    softplus_a = sem("softplus_forget_ready")
    logsig_ready = sem("key_argument_ready")
    bound_arg = sem("bound_argument_ready")
    softplus_b = sem("softplus_bound_ready")
    key_ready = sem("key_ready")
    cum_ready = sem("log_decay_ready")
    expg_ready = sem("decay_ready")
    qdec_ready = sem("query_decayed_ready")
    gap_ready = sem("gap_ready")
    gap_exp = sem("gap_decay_ready")
    kdec_ready = sem("key_decayed_ready")
    kdt_psum = sem("key_decayed_psum")
    kdt_ready = sem("key_decayed_tok_ready")
    var_ready = sem("ln_var_ready")
    dev_ready = sem("ln_deviation_ready")
    vn_ready = sem("v_normed_ready")
    vrow_out = sem("v_rows_out")
    mix_psum = sem("spatial_mix_psum")
    a_ready = sem("a_ready")
    a_high = sem("a_high_ready")
    a_low = sem("a_low_ready")
    lev_diff = sem("level_difference_ready")
    lev_exp = sem("level_decay_ready")
    lev_prod = sem("level_product_ready")
    score_psum = sem("score_psum")
    score_ready = sem("score_ready")
    upd_psum = sem("state_update_psum")
    state_ready = sem("state_ready")
    o_psum = sem("out_psum")
    o_ready = sem("out_ready")
    pstate_out = sem("prompt_state_out")
    s0_in = [sem("sample_state_in_even"), sem("sample_state_in_odd")]
    s0_out = [sem("sample_state_out_even"), sem("sample_state_out_odd")]
    vex_ready = sem("value_by_sequence_ready")
    so_psum = sem("sample_out_psum")
    su_psum = sem("sample_update_psum")
    s0_ready = sem("sample_state_ready")
    osq_ready = sem("out_squares_ready")
    ostat_psum = sem("out_mean_square_psum")
    oroot_ready = sem("out_root_ready")
    b_ready = sem("b_ready")
    b_high = sem("b_high_ready")
    b_low = sem("b_low_ready")
    merged_ready = sem("merged_ready")
    merged_high = sem("merged_high_ready")
    merged_low = sem("merged_low_ready")
    hid_high = sem("hidden_high_ready")
    hid_low = sem("hidden_low_ready")

    hn_psum = sem("normed_rows_psum")
    logit_psum = sem("logit_psum")
    lg_ready = sem("logits_ready")
    top_ready = sem("top_ready")
    gap_top = sem("top_gap_exp_ready")
    chosen_ready = sem("chosen_ready")
    rank_psum = sem("rank_psum")
    table_ready = sem("slot_table_ready")
    pick_ready = sem("pick_ready")
    xg_psum = sem("expert_in_psum")
    xg_high = sem("expert_in_high_ready")
    xg_low = sem("expert_in_low_ready")
    gate_emptied = sem("expert_gate_emptied")
    he_ready = sem("expert_hidden_ready")
    het_psum = sem("expert_hidden_t_psum")
    heh_ready = sem("expert_hidden_high_ready")
    hel_ready = sem("expert_hidden_low_ready")
    pickt_psum = sem("pick_t_psum")
    pickt_ready = sem("pick_t_ready")
    y_ready = sem("expert_out_high_ready")
    y_low = sem("expert_out_low_ready")
    sum_psum = sem("expert_sum_psum")
    sum_done = sem("expert_sum_done")
    fsq_ready = sem("final_square_sum_ready")
    froot_ready = sem("final_root_ready")
    fout_ready = sem("final_rows_ready")
    y_out = sem("y_out")
    columns_ready = sem("slot_column_ready")
    gates_ready = sem("gate_column_ready")
    shift_done = sem("slots_shifted")

    MB = mark_after[-1]
    OUTS = [(t, hf_) for t in range(NT) for hf_ in range(2)]
    SUM_BANK = [6, 7, 4, 5, 2, 3]
    ROW_BANK = [0, 1, 2, 3, 5, 6]
    NO = len(OUTS)

    def expert_source(e, i):
        kind, j, part, k0, kt, c0, cols = ECH[i]
        w = A["moe_w_" + kind][0, e]
        return rows(w, k0, kt, c0, cols)

    def width(i):
        return ECH[i % NEC][4] * ECH[i % NEC][6]

    def group_tiles(j):
        c0, cols = groups[j]
        return range(c0 // 128, (c0 + cols) // 128)

    HEAD = closing[("gate", 0)] + 1

    def any_extra(eng):
        eng.wait_ge(table_ready, 1)
        return eng.value_load(full[0:1, NMORE:NMORE + 1], min_val=0, max_val=1) > 0

    def extra_block(eng, n):
        more = eng.value_load(full[0:1, bass.ds(n, 1)], min_val=0, max_val=1)
        item = eng.value_load(items[0:1, bass.ds(n, 1)], min_val=NE, max_val=NE + NMORE)
        return more > 0, item

    def extra_blocks(eng, run):
        with eng.If(any_extra(eng)):
            with eng.Fori(0, NMORE) as n:
                more, item = extra_block(eng, n)
                with eng.If(more):
                    run(item, n)

    def piece_width(c):
        return (chunks[c][1] * chunks[c][2] if c < NDENSE else width(c - NDENSE)) // 2

    def emptied_sem(by):
        return act_emptied if by == "act" else dve_emptied

    def base(L):
        return first_chunk[(L, "forget")]

    TV = 64 // NSEQ
    NLEV = len(LEVELS)
    SCORES = PAIRS + 1
    NSCORE = sum(SCORES if lv <= LS // 2 else PAIRS for lv in [0] + LEVELS)

    def score_count(L, li):
        return NSCORE * L + sum(SCORES if lv <= LS // 2 else PAIRS for lv in ([0] + LEVELS)[:li])

    def halves(X, lv, n):
        v = X[:, :, 0:n].rearrange("p h (b c) -> p h b c", c=2 * lv)
        return v[:, :, :, 0:lv], v[:, :, :, lv:2 * lv], v[:, :, :, lv - 1:lv].broadcast_to([128, H, n // (2 * lv), lv])

    def tokens_of(lv):
        return T if lv <= LS // 2 else TP

    P_MIX, P_FFN, P_LB, P_HG = 0, LAYERS * KD, 2 * LAYERS * KD, 2 * LAYERS * KD + LAYERS * H

    block = ctx.enter_context(nc.Block())

    @block.sync
    def _(sp):
        for c, (src, kt, cols) in enumerate(chunks):
            if c >= SLOTS:
                sp.wait_ge(low_done, 2 * (c - SLOTS + 1))
            sp.dma_start(raw[:, c % SLOTS, 0:kt * cols].rearrange("p (k n) -> p k n", n=cols), src).then_inc(
                raw_full[c % SLOTS], 16)

        def load_expert(item, e):
            for i in range(NEC):
                sp.wait_ge(low_done, 2 * NEC * item + 2 * (NDENSE + i - SLOTS + 1))
                sp.dma_start(raw[:, i % SLOTS, 0:width(i)].rearrange("p (k n) -> p k n", n=ECH[i][6]),
                             expert_source(e, i)).then_inc(raw_full[i % SLOTS], 16)

        with sp.Fori(0, NE) as e:
            load_expert(e, e)
        extra_blocks(sp, lambda item, n: load_expert(item, n % NE))
        for t in range(NT):
            sp.wait_ge(fout_ready, t + 1)
            if t < PAIRS:
                sp.dma_start(OUT["y_prompt"][0, 128 * t:128 * t + 128, :], acc[:, t, :]).then_inc(y_out, 16)
            else:
                sp.dma_start(OUT["y_sample"].rearrange("b j d -> (b j) d"), acc[0:64, t, :]).then_inc(y_out, 16)
        sp.wait_ge(y_out, 16 * NT)

    @block.gpsimd
    def _(pool):
        links = [0]

        def link(ins):
            links[0] += 1
            ins.then_inc(pool_link, 1)
            pool.wait_ge(pool_link, links[0])

        pool.dma_start(xt[:, 0:PAIRS, :], A["x_prompt"][0].rearrange("(t p) d -> p t d", p=128)).then_inc(x_in[0], 16)
        pool.dma_start(xt[0:64, PAIRS, :], A["x_sample"].rearrange("b j d -> (b j) d")).then_inc(x_in[1], 16)
        for n, (name, k) in enumerate((("norm_mix_g", KD), ("norm_ffn_g", KD), ("lower_bounds", H), ("hgrn_norm_g", H))):
            r = (P_MIX, P_FFN, P_LB, P_HG)[n]
            pool.dma_start(prow[r:r + LAYERS * k, :], A[name].rearrange("l (k p) -> (l k) p", p=128)).then_inc(rows_in, 16)

        def layer_params(L):
            pool.dma_start(wsp[:], A["w_spatial"][L].rearrange("g t s -> t g s")).then_inc(layer_in, 16)
            pool.dma_start(bsp[:], A["b_spatial"][L].partition_broadcast(128)).then_inc(layer_in, 16)
            pool.dma_start(lng[:], A["ln_v_g"][L].partition_broadcast(128)).then_inc(layer_in, 16)
            pool.dma_start(lnb[:], A["ln_v_b"][L].partition_broadcast(128)).then_inc(layer_in, 16)

        layer_params(0)
        pool.dma_start(rw[:], A["router_w"][0].rearrange("(k p) e -> p k e", p=128)).then_inc(router_in, 16)
        nc.gpsimd.memset(eps_t[:], EPS).then_inc(first_ready, 1)
        nc.gpsimd.memset(ones[:], 1.0).then_inc(first_ready, 1)
        link(nc.gpsimd.memset(ident[:], 0.0))
        nc.gpsimd.affine_select(out=ident[:], in_=ident[:], compare_op=ALU.not_equal, fill=1.0, base=0,
                                pattern=[[-1, 128]], channel_multiplier=1).then_inc(first_ready, 1)
        pool.wait_ge(first_ready, 3)
        link(nc.gpsimd.affine_select(out=upper[:], in_=ones[:], compare_op=ALU.is_ge, fill=0.0, base=0,
                                     pattern=[[1, 128]], channel_multiplier=-1))
        link(nc.gpsimd.iota(iota[:], pattern=[[1, 128]], base=0, channel_multiplier=0,
                            allow_small_or_imprecise_dtypes=True))
        link(nc.gpsimd.memset(lmask[:], 0))
        link(nc.gpsimd.affine_select(out=lmask[:, 0, :], in_=lmask[:, 0, :], compare_op=ALU.not_equal, fill=1.0, base=0,
                                     pattern=[[-1, 128]], channel_multiplier=1))
        for n, lv in enumerate(LEVELS):
            v = lmask[:, n + 1, :].rearrange("p (b c) -> p b c", c=2 * lv)
            nb = 128 // (2 * lv)
            link(nc.gpsimd.memset(v[:, :, lv:2 * lv], 1))
            link(nc.gpsimd.affine_select(out=v, in_=v, compare_op=ALU.is_ge, fill=0.0, base=0,
                                         pattern=[[-2 * lv, nb], [0, 2 * lv]], channel_multiplier=1))
            link(nc.gpsimd.affine_select(out=v, in_=v, compare_op=ALU.is_ge, fill=0.0, base=lv - 1,
                                         pattern=[[2 * lv, nb], [0, 2 * lv]], channel_multiplier=-1))
        link(nc.gpsimd.memset(smask[:], 1.0))
        link(nc.gpsimd.memset(smask[:, 0:TP:CH], 0.0))
        link(nc.gpsimd.memset(smask[:, TP:T:LS], 0.0))
        link(nc.gpsimd.memset(bmask[:], 1.0))
        link(nc.gpsimd.affine_select(out=bmask[:], in_=bmask[:], compare_op=ALU.is_ge, fill=0.0, base=0,
                                     pattern=[[-LS, NSEQ]], channel_multiplier=1))
        link(nc.gpsimd.affine_select(out=bmask[:], in_=bmask[:], compare_op=ALU.is_ge, fill=0.0, base=LS - 1,
                                     pattern=[[LS, NSEQ]], channel_multiplier=-1))
        nc.gpsimd.tensor_copy(r8[:].rearrange("p (b t) -> p b t", t=LS),
                              ident[0:LS, 0:LS].unsqueeze(1).broadcast_to([LS, NSEQ, LS])).then_inc(consts_ready, 1)

        def load_s0(L, hd):
            b = hd % 2
            n = 2 * L + hd // 2
            if hd < 2:
                pool.wait_ge(lev_diff, NLEV * (L + 1))
                pool.wait_ge(o_psum, H * (L + 1))
            else:
                pool.wait_ge(s0_out[b], 16 * n)
            pool.dma_start(s0[b][:], A["state_hgrn"][L, :, hd].rearrange("b p v -> p b v")).then_inc(s0_in[b], 16)

        for L in range(LAYERS):
            pool.wait_ge(vn_ready, NT * (L + 1))
            pool.dma_start(OUT["v_rows"][L].rearrange("b j c -> (b j) c"), vn[0:64, PAIRS, :]).then_inc(vrow_out, 16)
            pool.wait_ge(state_ready, NPC * (L + 1))
            pool.dma_start(OUT["prompt_state"][L, 0].rearrange("h p v -> p h v"), S34[:, 1]).then_inc(pstate_out, 16)
            load_s0(L, 0)
            load_s0(L, 1)
            for hd in range(H):
                n = 2 * L + hd // 2
                pool.wait_ge(s0_ready, H * L + hd + 1)
                pool.dma_start(OUT["sample_state"][L, :, hd].rearrange("b p v -> p b v"), s0[hd % 2][:]).then_inc(
                    s0_out[hd % 2], 16)
                if hd + 2 < H:
                    load_s0(L, hd + 2)
            if L + 1 < LAYERS:
                pool.wait_ge(a_ready, H * (L + 1))
                layer_params(L + 1)
        for s in (s0_out[0], s0_out[1]):
            pool.wait_ge(s, 16 * LAYERS * H // 2)
        pool.wait_ge(vrow_out, 16 * LAYERS)
        pool.wait_ge(pstate_out, 16 * LAYERS)
        pool.dma_start(gfin[:], A["final_norm_g"].partition_broadcast(128)).then_inc(gfin_in, 16)

    @block.scalar
    def _(act):
        links = [0]
        fn = nc.scalar.activation

        def link(ins):
            links[0] += 1
            ins.then_inc(act_link, 1)
            act.wait_ge(act_link, links[0])

        def split_high(c, half):
            n = piece_width(c)
            p = 2 * c + half
            if half == 0:
                act.wait_ge(raw_full[c % SLOTS], 16 * (c // SLOTS + 1))
            if p >= RING:
                act.wait_ge(pe_mark, mark_after[p - RING])
            fn(whi[:, p % RING, 0:n], raw[:, c % SLOTS, half * n:half * n + n], ACT.Copy).then_inc(high_done, 1)

        def square(n, j):
            if n == 0:
                act.wait_ge(h_ready, j + 1)
            else:
                L, sec = (n - 1) // 2, ("w_out", "down")[(n - 1) % 2]
                act.wait_ge(dve_emptied, tile[(L, sec, j)][3])
            if 8 * n + j >= 2:
                act.wait_ge(summed, KD * n + j - 1)
            fn(sq[:, j % 2, :], h[:, j, :], ACT.Square).then_inc(squared, 1)

        def norm(n, parts=True):
            act.wait_ge(stat_psum, n + 1)
            if n:
                act.wait_ge(xn_ready, KD * n)
            fn(rinv[:], bank[4][:, 0:T], ACT.Sqrt, bias=eps_t[:], scale=1.0 / D).then_inc(root_ready, 1)
            if parts:
                for j in range(KD):
                    act.wait_ge(xn_ready, KD * n + j + 1)
                    fn(xh[:, j, :], xn[:, j, :], ACT.Copy).then_inc(xh_ready, 1)

        def empties(L, sec, j, out, f, psz=128, cols=T):
            b, mark, by, count, _ = tile[(L, sec, j)]
            act.wait_ge(pe_mark, mark)
            fn(out, bank[b][0:psz, 0:cols], f).then_inc(act_emptied, 1)

        for c in range(SLOTS):
            split_high(c, 0)
            split_high(c, 1)
        act.wait_ge(first_ready, 3)
        for j in range(KD):
            square(0, j)
        norm(0)
        act.wait_ge(lb_ready, 1)
        link(fn(lbt[:, 3], lbt[:, 0], ACT.Abs))
        link(fn(lbt[:, 3], lbt[:, 3], ACT.Exp, scale=-1.0))
        fn(lbt[:, 4], lbt[:, 3], ACT.Ln, bias=1.0).then_inc(lb_exp, 1)

        for L in range(LAYERS):
            if L:
                norm(2 * L)
            for i, (sec, part) in enumerate(MIX):
                c = base(L) + i
                split_high(c + SLOTS, 0)
                if sec == "forget":
                    for j in (2 * part, 2 * part + 1):
                        empties(L, sec, j, G[:, j, :], ACT.Copy)
                elif sec == "q":
                    for j in (2 * part, 2 * part + 1):
                        empties(L, sec, j, Q[:, j, :], ACT.Silu)
                elif sec == "value" and part == 1:
                    for j, (_, sz) in enumerate(TOK):
                        empties(L, sec, j, V[0:sz, j, :], ACT.Copy, sz, DA)
                elif sec == "v" and part == 1:
                    if L:
                        act.wait_ge(vrow_out, 16 * L)
                    for j, (_, sz) in enumerate(TOK):
                        empties(L, sec, j, vn[0:sz, j, :], ACT.Gelu, sz, DA)
                elif sec == "u":
                    for j in (2 * part, 2 * part + 1):
                        empties(L, sec, j, u[:, j, :], ACT.Gelu)
                elif sec == "gate_a":
                    for j in (2 * part, 2 * part + 1):
                        empties(L, sec, j, xn[:, j, :], ACT.Sigmoid)
                elif sec == "out_gate":
                    if part == 0:
                        act.wait_ge(a_ready, H * (L + 1))
                    for j in (2 * part, 2 * part + 1):
                        empties(L, sec, j, u[:, j, :], ACT.Silu)
                elif sec == "gate_b":
                    for j in (2 * part, 2 * part + 1):
                        empties(L, sec, j, gb[:, j, :], ACT.Sigmoid)
                split_high(c + SLOTS, 1)
                if i == 2:
                    act.wait_ge(act_emptied, tile[(L, "forget", H - 1)][3])
                    if L:
                        act.wait_ge(b_low, H * L)
                        act.wait_ge(pstate_out, 16 * L)
                        act.wait_ge(s0_out[0], 32 * L)
                        act.wait_ge(s0_out[1], 32 * L)
                    link(fn(Z[:], G[:], ACT.Abs))
                    link(fn(Z[:], Z[:], ACT.Exp, scale=-1.0))
                    fn(E[:], Z[:], ACT.Ln, bias=1.0).then_inc(softplus_a, 1)
                    act.wait_ge(logsig_ready, L + 1)
                    if L == 0:
                        fn(K[:], E[:], ACT.Exp).then_inc(key_ready, 1)
                    else:
                        act.wait_ge(lb_ready, 2)
                        for j in range(H):
                            ins = fn(K[:, j], E[:, j], ACT.Exp, bias=lbt[:, 2, j:j + 1])
                        ins.then_inc(key_ready, 1)
                        act.wait_ge(bound_arg, L)
                        link(fn(QE[:], Z[:], ACT.Abs))
                        link(fn(QE[:], QE[:], ACT.Exp, scale=-1.0))
                        fn(QE[:], QE[:], ACT.Ln, bias=1.0).then_inc(softplus_b, 1)
                if i == 4:
                    act.wait_ge(cum_ready, H * (L + 1))
                    act.wait_ge(key_ready, L + 1)
                    fn(E[:], G[:], ACT.Exp).then_inc(expg_ready, 1)
                    act.wait_ge(gap_ready, L + 1)
                    fn(Z[:], Z[:], ACT.Exp).then_inc(gap_exp, 1)
                if i == 5:
                    for j, (_, sz) in enumerate(TOK):
                        act.wait_ge(kdt_psum, NT * L + j + 1)
                        fn(kdt[0:sz, j, :], bank[4 + j][0:sz, :], ACT.Copy).then_inc(kdt_ready, 1)
                if i == 7:
                    for j, (_, sz) in enumerate(TOK):
                        act.wait_ge(var_ready, NT * L + j + 1)
                        fn(bag[0:sz, j, 1:2], bag[0:sz, j, 1:2], ACT.Sqrt, bias=eps_t[0:sz]).then_inc(dev_ready, 1)
                if 6 <= i < 6 + NLEV:
                    li = i - 6
                    n = tokens_of(LEVELS[li])
                    act.wait_ge(lev_diff, NLEV * L + li + 1)
                    fn(E[:, :, 0:n], E[:, :, 0:n], ACT.Exp).then_inc(lev_exp, 1)
                if 9 <= i < 9 + H:
                    g = i - 9
                    act.wait_ge(a_ready, H * L + g + 1)
                    fn(ahi[:, g], u[:, g], ACT.Copy).then_inc(a_high, 1)
                if i == 14:
                    for hd in range(H):
                        act.wait_ge(o_psum, H * L + hd + 1)
                        fn(Q[:, hd, :], bank[4 + hd][:, 0:T], ACT.Copy).then_inc(o_ready, 1)
                if i == 19:
                    act.wait_ge(s0_ready, H * (L + 1))
                    fn(osq[:], Q[:], ACT.Square).then_inc(osq_ready, 1)
                    for hd in range(H):
                        act.wait_ge(ostat_psum, H * L + hd + 1)
                        fn(QE[:, hd, :], bank[4 + hd][:, 0:T], ACT.Sqrt, bias=eps_t[:], scale=1.0 / 128).then_inc(
                            oroot_ready, 1)
                if i == 20:
                    for hd in range(H):
                        act.wait_ge(b_ready, H * L + hd + 1)
                        fn(bhi[:, hd], Q[:, hd], ACT.Copy).then_inc(b_high, 1)
                if sec == "branch_b":
                    for j in range(4 * part, 4 * part + 4):
                        act.wait_ge(merged_ready, KD * L + j + 1)
                        fn(xh[:, j, :], xn[:, j, :], ACT.Copy).then_inc(merged_high, 1)
                if sec == "w_out":
                    for j in (2 * part, 2 * part + 1):
                        square(2 * L + 1, j)
            if L % 2 == 0:
                norm(2 * L + 1)
                act.wait_ge(pstate_out, 16 * (L + 1))
                act.wait_ge(vrow_out, 16 * (L + 1))
                act.wait_ge(s0_out[0], 32 * (L + 1))
                act.wait_ge(s0_out[1], 32 * (L + 1))
                for i, (sec, part) in enumerate(FFN):
                    c = first_chunk[(L, "gate")] + i
                    split_high(c + SLOTS, 0)
                    if sec == "gate":
                        if part:
                            act.wait_ge(dve_emptied, tile[(L, "up", 2 * part - 1)][3])
                        for j in (0, 1):
                            empties(L, sec, 2 * part + j, sg[:, j, :], ACT.Silu)
                    split_high(c + SLOTS, 1)
                    if sec == "up":
                        for j in (0, 1):
                            act.wait_ge(dve_emptied, tile[(L, "up", 2 * part + j)][3])
                            fn(fh[:, 2 * part + j, :], hf[:, j, :], ACT.Copy).then_inc(hid_high, 1)
                    if sec == "down" and part % 3 == 2:
                        for j in (0, 1):
                            square(2 * L + 2, 2 * (part // 3) + j)

        norm(2 * LAYERS - 1, parts=False)
        act.wait_ge(pstate_out, 16 * LAYERS)
        act.wait_ge(vrow_out, 16 * LAYERS)
        act.wait_ge(s0_out[0], 32 * LAYERS)
        act.wait_ge(s0_out[1], 32 * LAYERS)
        for n, (t, hf_) in enumerate(OUTS):
            act.wait_ge(hn_psum, n + 1)
            fn(hn[0:TOK[t][1], t, 512 * hf_:512 * hf_ + 512], bank[ROW_BANK[n]][0:TOK[t][1], :], ACT.Copy).then_inc(
                y_ready, 1)
        act.wait_ge(top_ready, 1)
        fn(g1[:, 0], g1[:, 0], ACT.Exp).then_inc(gap_top, 1)

        def expert_in_high(item):
            for hh in range(2):
                act.wait_ge(xg_psum, 2 * item + hh + 1)
                fn(xeh[:, 4 * hh:4 * hh + 4, :], bank[6 + hh][:], ACT.Copy).then_inc(xg_high, 1)

        def hidden_high(item, j):
            ts = group_tiles(j)
            act.wait_ge(het_psum, NG * item + j + 1)
            fn(heh[:, ts[0]:ts[-1] + 1, :], bank[4 + j % 2][:, 0:128 * len(ts)], ACT.Copy).then_inc(heh_ready, 1)

        def high_of(item, i, half):
            n = piece_width(NDENSE + i % NEC)
            p = 2 * i + half
            if half == 0:
                act.wait_ge(raw_full[i % SLOTS], 16 * (NEC // SLOTS) * item + 16 * (NDENSE // SLOTS + i // SLOTS + 1))
            act.wait_ge(pe_mark, 2 * NEC * item + (MB + p - RING + 1))
            fn(whi[:, p % RING, 0:n], raw[:, i % SLOTS, half * n:half * n + n], ACT.Copy).then_inc(high_done, 1)

        def chunk(item, i, last, ahead):
            if i + SLOTS < last:
                high_of(item, i + SLOTS, 0)
            if i >= NEC:
                item, i, last = item + 1, i - NEC, last - NEC
            kind, j, cols = ECH[i][0], ECH[i][1], ECH[i][6]
            closed = i == closing.get((kind, j))
            if kind == "gate" and closed:
                act.wait_ge(pe_mark, 2 * NEC * item + (MB + 2 * i + 2))
                if j >= 2:
                    act.wait_ge(he_ready, NG * item + (j - 1))
                fn(sge[:, j % 2, 0:cols], bank[2 * (j % 2)][:, 0:cols], ACT.Silu).then_inc(gate_emptied, 1)
            if i + SLOTS < last:
                high_of(item, i + SLOTS, 1)
            if kind == "up" and closed:
                if j == 1:
                    act.wait_ge(pickt_psum, item + 1)
                    act.wait_ge(sum_psum, NO * item + NO)
                    fn(pickt[:], bank[5][:, 0:T], ACT.Copy).then_inc(pickt_ready, 1)
                if j:
                    hidden_high(item, j - 1)
                if j == NG - 1:
                    if ahead:
                        expert_in_high(item + 1)
                    hidden_high(item, j)
            if i == NEC - 1:
                act.wait_ge(pe_mark, 2 * NEC * item + (MB + 2 * NEC))
                act.wait_ge(sum_psum, NO * item + NO)
                for hh in range(2):
                    fn(Yh[:, 512 * hh:512 * hh + 512], bank[2 + hh][:], ACT.Copy).then_inc(y_ready, 1)

        def extra(item, n):
            for i in range(SLOTS):
                for half in range(2):
                    high_of(item, i, half)
            expert_in_high(item)
            for i in range(NEC):
                chunk(item, i, NEC, False)

        expert_in_high(0)
        for i in range(HEAD):
            chunk(0, i, 2 * NEC, True)
        with act.Fori(0, NE - 1) as e:
            for i in range(HEAD, HEAD + NEC):
                chunk(e, i, 2 * NEC, True)
        for i in range(HEAD, NEC):
            chunk(NE - 1, i, NEC, False)
        extra_blocks(act, extra)
        for t, (_, sz) in enumerate(TOK):
            act.wait_ge(fsq_ready, t + 1)
            fn(rf[0:sz, t:t + 1], ssf[0:sz, t:t + 1], ACT.Sqrt, bias=eps_t[0:sz], scale=1.0 / D).then_inc(froot_ready, 1)

    @block.vector
    def _(dve):
        links = [0]
        v = nc.vector

        def link(ins):
            links[0] += 1
            ins.then_inc(dve_link, 1)
            dve.wait_ge(dve_link, links[0])

        def split_low(c, half):
            n = piece_width(c)
            p = 2 * c + half
            dve.wait_ge(high_done, p + 1)
            v.tensor_tensor(wlo[:, p % RING, 0:n], raw[:, c % SLOTS, half * n:half * n + n],
                            whi[:, p % RING, 0:n].bitcast(F), ALU.subtract).then_inc(low_done, 1)

        def add_square(n, j):
            dve.wait_ge(squared, KD * n + j + 1)
            if j == 0:
                if n:
                    dve.wait_ge(stat_psum, n)
                v.tensor_copy(ssum[:], sq[:, 0, :]).then_inc(summed, 1)
            else:
                dve.wait_ge(summed, KD * n + j)
                v.tensor_tensor(ssum[:], ssum[:], sq[:, j % 2, :], ALU.add).then_inc(summed, 1)

        def norm(n, parts=True):
            col = (P_FFN if n % 2 else P_MIX) + KD * (n // 2)
            dve.wait_ge(root_ready, n + 1)
            v.reciprocal(rinv[:], rinv[:]).then_inc(rinv_ready, 1)
            dve.wait_ge(rinv_ready, n + 1)
            for j in range(KD + 1):
                if j < KD:
                    v.scalar_tensor_tensor(out=xn[:, j, :], in0=h[:, j, :], scalar=prm[:, col + j:col + j + 1],
                                           in1=rinv[:], op0=ALU.mult, op1=ALU.mult).then_inc(xn_ready, 1)
                if j and parts:
                    dve.wait_ge(xh_ready, KD * n + j)
                    v.tensor_tensor(xl[:, j - 1, :], xn[:, j - 1, :], xh[:, j - 1, :].bitcast(F),
                                    ALU.subtract).then_inc(xl_ready, 1)

        def waits_tile(L, sec, j):
            b, mark, _, _, _ = tile[(L, sec, j)]
            dve.wait_ge(pe_mark, mark)
            return bank[b]

        def add_residual(L, sec, j):
            b = waits_tile(L, sec, j)
            v.tensor_tensor(h[:, j, :], h[:, j, :], b[:, 0:T], ALU.add).then_inc(dve_emptied, 1)

        for c in range(SLOTS):
            split_low(c, 0)
            split_low(c, 1)
        dve.wait_ge(prm_psum, 1)
        v.tensor_copy(prm[:], bank[7][:, 0:NROW]).then_inc(prm_ready, 1)
        for j in range(KD):
            dve.wait_ge(xt_psum, j + 1)
            v.tensor_copy(h[:, j, :], bank[j % 4][:, 0:T]).then_inc(h_ready, 1)
            if j:
                add_square(0, j - 1)
        add_square(0, KD - 1)
        dve.wait_ge(prm_ready, 1)
        v.tensor_tensor(lbt[:, 0], prm[:, P_LB + H:P_LB + 2 * H], prm[:, P_LB:P_LB + H], ALU.subtract).then_inc(lb_ready, 1)
        norm(0)
        dve.wait_ge(lb_exp, 1)
        dve.wait_ge(lb_ready, 1)
        link(v.scalar_tensor_tensor(out=lbt[:, 1], in0=lbt[:, 0], scalar=0.0, in1=lbt[:, 4], op0=ALU.min,
                                    op1=ALU.subtract))
        v.tensor_tensor(lbt[:, 2], lbt[:, 1], lbt[:, 0], ALU.subtract).then_inc(lb_ready, 1)

        for L in range(LAYERS):
            if L:
                add_square(2 * L, KD - 1)
                norm(2 * L)
            for i, (sec, part) in enumerate(MIX):
                c = base(L) + i
                split_low(c + SLOTS, 0)
                if sec == "branch_a":
                    for j in range(4 * part, 4 * part + 4):
                        b = waits_tile(L, sec, j)
                        dve.wait_ge(act_emptied, tile[(L, "gate_a", j)][3])
                        v.tensor_tensor(xn[:, j, :], b[:, 0:T], xn[:, j, :], ALU.mult).then_inc(dve_emptied, 1)
                if sec == "branch_b":
                    for j in range(4 * part, 4 * part + 4):
                        b = waits_tile(L, sec, j)
                        dve.wait_ge(act_emptied, tile[(L, "gate_b", j)][3])
                        v.tensor_tensor(tmp[:, j % 2, :], b[:, 0:T], gb[:, j, :], ALU.mult).then_inc(dve_emptied, 1)
                        dve.wait_ge(dve_emptied, tile[(L, sec, j)][3])
                        v.tensor_tensor(xn[:, j, :], xn[:, j, :], tmp[:, j % 2, :], ALU.add).then_inc(merged_ready, 1)
                        if j:
                            dve.wait_ge(merged_high, KD * L + j)
                            v.tensor_tensor(xl[:, j - 1, :], xn[:, j - 1, :], xh[:, j - 1, :].bitcast(F),
                                            ALU.subtract).then_inc(merged_low, 1)
                    if part == 1:
                        j = KD
                        dve.wait_ge(merged_high, KD * L + j)
                        v.tensor_tensor(xl[:, j - 1, :], xn[:, j - 1, :], xh[:, j - 1, :].bitcast(F),
                                        ALU.subtract).then_inc(merged_low, 1)
                if sec == "w_out":
                    for j in (2 * part, 2 * part + 1):
                        add_residual(L, sec, j)
                split_low(c + SLOTS, 1)
                if sec == "w_out":
                    for j in (2 * part - 1, 2 * part):
                        if j >= 0:
                            add_square(2 * L + 1, j)
                if i == 0:
                    dve.wait_ge(wst_psum, L + 1)
                    dve.wait_ge(consts_ready, 1)
                    v.tensor_tensor(wst[:], bank[7][:].rearrange("p (g t) -> p g t", g=H),
                                    upper[:].unsqueeze(1).broadcast_to([128, H, 128]), ALU.mult).then_inc(wst_ready, 1)
                if i == 1:
                    dve.wait_ge(wsd_psum, L + 1)
                    for g in range(H):
                        ins = v.tensor_tensor(wsd[:, g].rearrange("p (b t) -> p b t", t=LS),
                                              bank[7][0:64, 64 * g:64 * g + 64].rearrange("p (b t) -> p b t", t=LS),
                                              bmask[:].unsqueeze(2).broadcast_to([64, NSEQ, LS]), ALU.mult)
                        ins.then_inc(wsd_ready, 1)
                if i == 2:
                    dve.wait_ge(softplus_a, L + 1)
                    link(v.scalar_tensor_tensor(out=Z[:], in0=G[:], scalar=0.0, in1=E[:], op0=ALU.min, op1=ALU.subtract))
                    v.tensor_tensor(E[:], Z[:], G[:], ALU.subtract).then_inc(logsig_ready, 1)
                    dve.wait_ge(logsig_ready, L + 1)
                    if L:
                        for j in range(H):
                            ins = v.tensor_scalar(Z[:, j], Z[:, j], lbt[:, 0, j:j + 1], None, ALU.subtract)
                        ins.then_inc(bound_arg, 1)
                        dve.wait_ge(softplus_b, L)
                        dve.wait_ge(bound_arg, L)
                        link(v.scalar_tensor_tensor(out=Z[:], in0=Z[:], scalar=0.0, in1=QE[:], op0=ALU.max, op1=ALU.add))
                        for j in range(H):
                            link(v.tensor_scalar(Z[:, j], Z[:, j], lbt[:, 1, j:j + 1], None, ALU.add))
                    for j in range(H):
                        v.tensor_tensor_scan(G[:, j], smask[:], Z[:, j], 0.0, ALU.mult, ALU.add).then_inc(cum_ready, 1)
                if i == 4:
                    dve.wait_ge(cum_ready, H * (L + 1))
                    link(v.tensor_tensor(Z[:, :, 0:TP].rearrange("p h (c t) -> p h c t", t=CH),
                                         G[:, :, CH - 1:TP:CH].unsqueeze(3).broadcast_to([128, H, NPC, CH]),
                                         G[:, :, 0:TP].rearrange("p h (c t) -> p h c t", t=CH), ALU.subtract))
                    v.tensor_tensor(Z[:, :, TP:T].rearrange("p h (c t) -> p h c t", t=LS),
                                    G[:, :, TP + LS - 1:T:LS].unsqueeze(3).broadcast_to([128, H, NSEQ, LS]),
                                    G[:, :, TP:T].rearrange("p h (c t) -> p h c t", t=LS),
                                    ALU.subtract).then_inc(gap_ready, 1)
                    dve.wait_ge(expg_ready, L + 1)
                    link(v.tensor_copy(el[:, :, 0:NPC], E[:, :, CH - 1:TP:CH]))
                    link(v.tensor_copy(el[:, :, NPC:], E[:, :, TP + LS - 1:T:LS]))
                    dve.wait_ge(act_emptied, tile[(L, "q", H - 1)][3])
                    v.tensor_tensor(QE[:], Q[:], E[:], ALU.mult).then_inc(qdec_ready, 1)
                    dve.wait_ge(gap_exp, L + 1)
                    dve.wait_ge(key_ready, L + 1)
                    v.tensor_tensor(Z[:], Z[:], K[:], ALU.mult).then_inc(kdec_ready, 1)
                    link(v.memset(sc[:], 0.0))
                    link(v.memset(scs[:], 0.0))
                if i == 7:
                    dve.wait_ge(layer_in, 64 * (L + 1))
                    for j, (_, sz) in enumerate(TOK):
                        dve.wait_ge(act_emptied, tile[(L, "v", j)][3])
                        link(v.bn_stats(bst[0:sz, j, :], vn[0:sz, j, :]))
                        v.bn_aggr(bag[0:sz, j, :], bst[0:sz, j, :]).then_inc(var_ready, 1)
                    for j, (_, sz) in enumerate(TOK):
                        dve.wait_ge(dev_ready, NT * L + j + 1)
                        link(v.reciprocal(bag[0:sz, j, 1:2], bag[0:sz, j, 1:2]))
                        link(v.tensor_scalar(vn[0:sz, j, :], vn[0:sz, j, :], bag[0:sz, j, 0:1], bag[0:sz, j, 1:2],
                                             ALU.subtract, ALU.mult))
                        link(v.tensor_tensor(vn[0:sz, j, :], vn[0:sz, j, :], lng[0:sz], ALU.mult))
                        v.tensor_tensor(vn[0:sz, j, :], vn[0:sz, j, :], lnb[0:sz], ALU.add).then_inc(vn_ready, 1)
                if 6 <= i < 6 + NLEV:
                    li = i - 6
                    lv = LEVELS[li]
                    n = tokens_of(lv)
                    ga, gb2, ref = halves(G, lv, n)
                    ea, eb, _ = halves(E, lv, n)
                    za, zb, _ = halves(Z, lv, n)
                    ka, _, _ = halves(K, lv, n)
                    _, qb, _ = halves(Q, lv, n)
                    if li == 0:
                        dve.wait_ge(qdec_ready, L + 1)
                    else:
                        dve.wait_ge(lev_prod, NLEV * L + li)
                    link(v.tensor_tensor(ea, ref, ga, ALU.subtract))
                    v.tensor_tensor(eb, gb2, ref, ALU.subtract).then_inc(lev_diff, 1)
                    dve.wait_ge(lev_exp, NLEV * L + li + 1)
                    if li == 0:
                        dve.wait_ge(kdt_psum, NT * (L + 1))
                    else:
                        dve.wait_ge(score_psum, score_count(L, li + 1))
                    link(v.tensor_tensor(za, ka, ea, ALU.mult))
                    v.tensor_tensor(zb, qb, eb, ALU.mult).then_inc(lev_prod, 1)
                if 6 <= i < 7 + NLEV:
                    li = i - 6
                    k = score_count(L, li)
                    lv = ([0] + LEVELS)[li]
                    for p in range(SCORES if lv <= LS // 2 else PAIRS):
                        dve.wait_ge(score_psum, k + p + 1)
                        if li:
                            dve.wait_ge(score_ready, score_count(L, li))
                        if p < PAIRS:
                            v.copy_predicated(sc[:, p], lmask[:, li, :].unsqueeze(1).broadcast_to([128, H, 128]),
                                              bank[4 + p][:].rearrange("p (h t) -> p h t", h=H)).then_inc(score_ready, 1)
                        else:
                            v.copy_predicated(scs[:], lmask[0:64, li, 0:64].unsqueeze(1).broadcast_to([64, H, 64]),
                                              bank[6][0:64, 0:64 * H].rearrange("p (h t) -> p h t", h=H)).then_inc(
                                                  score_ready, 1)
                if 9 <= i < 9 + H:
                    g = i - 9
                    dve.wait_ge(mix_psum, H * L + g + 1)
                    dve.wait_ge(act_emptied, tile[(L, "u", H - 1)][3])
                    b = bank[7]
                    t1 = tmp[:, g % 2, :]
                    link(v.tensor_tensor(t1[:, 0:TP].rearrange("p (c t) -> p c t", t=128),
                                         b[:, 0:TP].rearrange("p (c t) -> p c t", t=128),
                                         bsp[:, g].unsqueeze(1).broadcast_to([128, PAIRS, 128]), ALU.add))
                    link(v.tensor_tensor(t1[:, TP:T].rearrange("p (c t) -> p c t", t=LS),
                                         b[:, TP:T].rearrange("p (c t) -> p c t", t=LS),
                                         bsp[:, g, 0:LS].unsqueeze(1).broadcast_to([128, NSEQ, LS]), ALU.add))
                    v.tensor_tensor(u[:, g], u[:, g], t1, ALU.mult).then_inc(a_ready, 1)
                    dve.wait_ge(a_high, H * L + g + 1)
                    v.tensor_tensor(alo[:, g], u[:, g], ahi[:, g].bitcast(F), ALU.subtract).then_inc(a_low, 1)
                if i == 13:
                    for n in range(NPC):
                        dve.wait_ge(upd_psum, NPC * L + n + 1)
                        dst = (S12 if n < 2 else S34)[:, n % 2]
                        if n == 0:
                            v.tensor_copy(dst, bank[4][:].rearrange("p (h v) -> p h v", h=H)).then_inc(state_ready, 1)
                            continue
                        dve.wait_ge(state_ready, NPC * L + n)
                        src = (S12 if n - 1 < 2 else S34)[:, (n - 1) % 2]
                        for hd in range(H):
                            ins = v.scalar_tensor_tensor(out=dst[:, hd], in0=src[:, hd], scalar=el[:, hd, n:n + 1],
                                                         in1=bank[4 + n][:, 128 * hd:128 * hd + 128],
                                                         op0=ALU.mult, op1=ALU.add)
                        ins.then_inc(state_ready, 1)
                if 15 <= i < 15 + H:
                    hd = i - 15
                    if hd:
                        dve.wait_ge(su_psum, H * L + hd)
                    dve.wait_ge(act_emptied, tile[(L, "value", NT - 1)][3])
                    v.tensor_tensor(vex[:], V[0:64, PAIRS, 128 * hd:128 * hd + 128].unsqueeze(1).broadcast_to([64, NSEQ, 128]),
                                    bmask[:].unsqueeze(2).broadcast_to([64, NSEQ, 128]), ALU.mult).then_inc(vex_ready, 1)
                    dve.wait_ge(so_psum, H * L + hd + 1)
                    dve.wait_ge(o_ready, H * L + hd + 1)
                    link(v.tensor_tensor(Q[:, hd, TP:T], Q[:, hd, TP:T], bank[6][:, 0:64], ALU.add))
                    dve.wait_ge(su_psum, H * L + hd + 1)
                    st = s0[hd % 2]
                    for b in range(NSEQ):
                        ins = v.scalar_tensor_tensor(out=st[:, b], in0=st[:, b], scalar=el[:, hd, NPC + b:NPC + b + 1],
                                                     in1=bank[4 + b // 4][:, 128 * (b % 4):128 * (b % 4) + 128],
                                                     op0=ALU.mult, op1=ALU.add)
                    ins.then_inc(s0_ready, 1)
                if i == 19:
                    for hd in range(H):
                        dve.wait_ge(oroot_ready, H * L + hd + 1)
                        link(v.reciprocal(QE[:, hd], QE[:, hd]))
                        link(v.tensor_tensor(Q[:, hd], Q[:, hd], QE[:, hd], ALU.mult))
                        dve.wait_ge(act_emptied, tile[(L, "out_gate", hd)][3])
                        v.scalar_tensor_tensor(out=Q[:, hd], in0=Q[:, hd],
                                               scalar=prm[:, P_HG + H * L + hd:P_HG + H * L + hd + 1],
                                               in1=u[:, hd], op0=ALU.mult, op1=ALU.mult).then_inc(b_ready, 1)
                if i == 20:
                    dve.wait_ge(s0_out[0], 32 * (L + 1))
                    for hd in range(H):
                        dve.wait_ge(b_high, H * L + hd + 1)
                        v.tensor_tensor(blo[:, hd], Q[:, hd], bhi[:, hd].bitcast(F), ALU.subtract).then_inc(b_low, 1)
            add_square(2 * L + 1, KD - 1)
            if L % 2 == 0:
                norm(2 * L + 1)
                for i, (sec, part) in enumerate(FFN):
                    c = first_chunk[(L, "gate")] + i
                    split_low(c + SLOTS, 0)
                    if sec == "up":
                        for j in (0, 1):
                            b = waits_tile(L, sec, 2 * part + j)
                            dve.wait_ge(act_emptied, tile[(L, "gate", 2 * part + j)][3])
                            if part:
                                dve.wait_ge(hid_low, 2 * part)
                            v.tensor_tensor(hf[:, j, :], b[:, 0:T], sg[:, j, :], ALU.mult).then_inc(dve_emptied, 1)
                    if sec == "down" and part % 3 == 2:
                        for j in (0, 1):
                            add_residual(L, sec, 2 * (part // 3) + j)
                    split_low(c + SLOTS, 1)
                    if sec == "up":
                        for j in (0, 1):
                            dve.wait_ge(hid_high, 2 * part + j + 1)
                            v.tensor_tensor(fl[:, 2 * part + j, :], hf[:, j, :], fh[:, 2 * part + j, :].bitcast(F),
                                            ALU.subtract).then_inc(hid_low, 1)
                    if sec == "down" and part % 3 == 2:
                        for j in (2 * (part // 3) - 1, 2 * (part // 3)):
                            if j >= 0:
                                add_square(2 * L + 2, j)

        norm(2 * LAYERS - 1, parts=False)
        for n, (t, hf_) in enumerate(OUTS):
            dve.wait_ge(sum_psum, n + 1)
            v.tensor_copy(acc[0:TOK[t][1], t, 512 * hf_:512 * hf_ + 512], bank[ROW_BANK[n]][0:TOK[t][1], :]).then_inc(
                sum_done, 1)
        link(v.memset(lg[:], 0.0))
        dve.wait_ge(logit_psum, 1)
        link(v.tensor_copy(lg[:, 0:PAIRS], bank[7][:, 0:PAIRS * NE].rearrange("p (t e) -> p t e", e=NE)))
        v.tensor_copy(lg[0:64, PAIRS], bank[7][0:64, PAIRS * NE:NT * NE]).then_inc(lg_ready, 1)
        dve.wait_ge(lg_ready, 1)
        for t in range(NT):
            ins = v.max(top[:, t], lg[:, t])
        link(ins)
        for t in range(NT):
            ins = v.max_index(topi[:, t], top[:, t], lg[:, t])
        link(ins)
        link(v.tensor_copy(topf[:], topi[:]))
        v.tensor_tensor(g1[:, 0], top[:, :, 1], top[:, :, 0], ALU.subtract).then_inc(top_ready, 1)
        row = iota[:, 0:NE].unsqueeze(1).broadcast_to([128, NT, NE])
        link(v.tensor_tensor(m1[:], row, topf[:, :, 0:1].broadcast_to([128, NT, NE]), ALU.is_equal))
        link(v.tensor_tensor(m2[:], row, topf[:, :, 1:2].broadcast_to([128, NT, NE]), ALU.is_equal))
        v.tensor_tensor(mk[:], m1[:], m2[:], ALU.add).then_inc(chosen_ready, 1)
        dve.wait_ge(gap_top, 1)
        link(v.tensor_scalar(g1[:, 1], g1[:, 0], 1.0, None, ALU.add))
        link(v.reciprocal(g1[:, 2], g1[:, 1]))
        link(v.tensor_tensor(g1[:, 3], g1[:, 0], g1[:, 2], ALU.mult))
        link(v.tensor_tensor(m1[:], m1[:], g1[:, 2].unsqueeze(2).broadcast_to([128, NT, NE]), ALU.mult))
        link(v.tensor_tensor(m2[:], m2[:], g1[:, 3].unsqueeze(2).broadcast_to([128, NT, NE]), ALU.mult))
        link(v.tensor_tensor(cmb[:], m1[:], m2[:], ALU.add))
        link(v.memset(slot[:], -1.0))
        dve.wait_ge(rank_psum, 1)
        dve.wait_ge(chosen_ready, 1)
        link(v.tensor_tensor(slot[:, 0:PAIRS], bank[7][:, 0:PAIRS * NE].rearrange("p (t e) -> p t e", e=NE),
                             mk[:, 0:PAIRS], ALU.mult))
        link(v.tensor_tensor(slot[0:64, PAIRS], bank[7][0:64, PAIRS * NE:NT * NE], mk[0:64, PAIRS], ALU.mult))
        link(v.tensor_copy(fullf[:, 0, 0:NE], bank[7][:, NT * NE:(NT + 1) * NE]))
        link(v.tensor_scalar(slot[:, 0:PAIRS], slot[:, 0:PAIRS], -1.0, None, ALU.add))
        v.tensor_scalar(slot[0:64, PAIRS], slot[0:64, PAIRS], -1.0, None, ALU.add).then_inc(shift_done, 1)

        def choose(item, e, shifts=1):
            dve.wait_ge(shift_done, shifts)
            v.tensor_copy(cslot[:], slot[:, :, bass.ds(e, 1)]).then_inc(columns_ready, 1)
            dve.wait_ge(columns_ready, item + 1)
            if not isinstance(item, int) or item:
                dve.wait_ge(xg_psum, 2 * item)
                dve.wait_ge(pickt_psum, item)
            for t, (_, sz) in enumerate(TOK):
                ins = v.tensor_scalar(pick[0:sz, t], iota[0:sz], cslot[0:sz, t:t + 1], None, ALU.is_equal)
            ins.then_inc(pick_ready, 1)

        def expert_in_low(item):
            for hh in range(2):
                dve.wait_ge(xg_high, 2 * item + hh + 1)
                v.tensor_tensor(xel[:, 4 * hh:4 * hh + 4, :].rearrange("p k s -> p (k s)"), bank[6 + hh][:],
                                xeh[:, 4 * hh:4 * hh + 4, :].rearrange("p k s -> p (k s)").bitcast(F),
                                ALU.subtract).then_inc(xg_low, 1)

        def hidden_low(item, j):
            ts = group_tiles(j)
            dve.wait_ge(heh_ready, NG * item + j + 1)
            v.tensor_tensor(hel[:, ts[0]:ts[-1] + 1, :].rearrange("p k s -> p (k s)"), bank[4 + j % 2][:, 0:128 * len(ts)],
                            heh[:, ts[0]:ts[-1] + 1, :].rearrange("p k s -> p (k s)").bitcast(F),
                            ALU.subtract).then_inc(hel_ready, 1)

        def low_of(item, i, half):
            n = piece_width(NDENSE + i % NEC)
            p = 2 * i + half
            dve.wait_ge(high_done, 2 * NEC * item + (2 * NDENSE + p + 1))
            v.tensor_tensor(wlo[:, p % RING, 0:n], raw[:, i % SLOTS, half * n:half * n + n],
                            whi[:, p % RING, 0:n].bitcast(F), ALU.subtract).then_inc(low_done, 1)

        def chunk(item, i, last, ahead, e=None):
            if i + SLOTS < last:
                low_of(item, i + SLOTS, 0)
            if i >= NEC:
                item, i, last = item + 1, i - NEC, last - NEC
            kind, j, c0, cols = ECH[i][0], ECH[i][1], ECH[i][5], ECH[i][6]
            closed = i == closing.get((kind, j))
            if kind == "up" and closed:
                dve.wait_ge(pe_mark, 2 * NEC * item + (MB + 2 * i + 2))
                dve.wait_ge(gate_emptied, NG * item + (j + 1))
                v.tensor_tensor(He[:, c0:c0 + cols], bank[1 + 2 * (j % 2)][:, 0:cols], sge[:, j % 2, 0:cols],
                                ALU.mult).then_inc(he_ready, 1)
            if i + SLOTS < last:
                low_of(item, i + SLOTS, 1)
            if kind == "up" and closed:
                if j:
                    hidden_low(item, j - 1)
                if j == NG - 3 and ahead:
                    choose(item + 1, item + 1)
                if j == NG - 1:
                    if ahead:
                        expert_in_low(item + 1)
                    hidden_low(item, j)
            if i == NEC - 1:
                dve.wait_ge(sum_psum, NO * item + NO)
                for hh in range(2):
                    dve.wait_ge(y_ready, 2 * item + (NO + hh + 1))
                    v.tensor_tensor(Yl[:, 512 * hh:512 * hh + 512], bank[2 + hh][:],
                                    Yh[:, 512 * hh:512 * hh + 512].bitcast(F), ALU.subtract).then_inc(y_low, 1)

        def add_sums(item, e):
            dve.wait_ge(sum_done, NO * item + NO)
            v.tensor_copy(cgate[:], cmb[:, :, bass.ds(e, 1)]).then_inc(gates_ready, 1)
            dve.wait_ge(gates_ready, item + 1)
            for n, (t, hf_) in enumerate(OUTS):
                sz = TOK[t][1]
                part = acc[0:sz, t, 512 * hf_:512 * hf_ + 512]
                dve.wait_ge(sum_psum, NO * item + (NO + n + 1))
                v.scalar_tensor_tensor(out=part, in0=bank[SUM_BANK[n]][0:sz, :], scalar=cgate[0:sz, t:t + 1], in1=part,
                                       op0=ALU.mult, op1=ALU.add).then_inc(sum_done, 1)

        choose(0, 0)
        expert_in_low(0)
        for n in range(1, BLOCKS - 1):
            link(v.tensor_scalar(fullf[:, 0, NE * n:NE * n + NE], fullf[:, 0, 0:NE], -float(CAP * n), None, ALU.add))
        link(v.tensor_scalar(fullf[:, 1], fullf[:, 0], float(CAP), None, ALU.is_gt))
        link(v.memset(fullf[:, 0], 1.0))
        link(v.tensor_tensor_scan(fullf[:, 2], fullf[:, 0], fullf[:, 1], float(NE), ALU.mult, ALU.add))
        link(v.tensor_tensor(fullf[:, 2], fullf[:, 2], fullf[:, 1], ALU.subtract))
        link(v.tensor_copy(full[:, 0:NMORE], fullf[:, 1]))
        link(v.tensor_copy(items[:], fullf[:, 2]))
        v.tensor_reduce(full[:, NMORE:NMORE + 1], fullf[:, 1], mybir.AxisListType.X, ALU.max).then_inc(table_ready, 1)
        for i in range(HEAD):
            chunk(0, i, 2 * NEC, True)
        with dve.Fori(0, NE - 1) as e:
            for i in range(HEAD, HEAD + NEC):
                chunk(e, i, 2 * NEC, True)
            add_sums(e, e)
        for i in range(HEAD, NEC):
            chunk(NE - 1, i, NEC, False)
        add_sums(NE - 1, NE - 1)

        with dve.If(any_extra(dve)):
            with dve.Fori(1, BLOCKS) as b:
                dve.wait_ge(pick_ready, NE)
                dve.wait_ge(shift_done, b)
                v.tensor_scalar(slot[:], slot[:], -float(CAP), None, ALU.add).then_inc(shift_done, 1)
                with dve.Fori(0, NE) as e:
                    more, item = extra_block(dve, b * NE + e - NE)
                    with dve.If(more):
                        choose(item, e, b + 1)
                        for i in range(SLOTS):
                            for half in range(2):
                                low_of(item, i, half)
                        expert_in_low(item)
                        for i in range(NEC):
                            chunk(item, i, NEC, False)
                        add_sums(item, e)
                        dve.wait_ge(sum_done, NO * item + 2 * NO)
                        v.memset(cgate[:], 0.0)
        dve.wait_ge(sum_done, NO * (NE + 1))
        dve.wait_ge(gfin_in, 16)
        def square_rows(t, sz):
            v.tensor_tensor_reduce(out=He[0:sz, 0:D], in0=acc[0:sz, t], in1=acc[0:sz, t], scale=1.0, scalar=0.0,
                                   op0=ALU.mult, op1=ALU.add, accum_out=ssf[0:sz, t:t + 1]).then_inc(fsq_ready, 1)

        square_rows(0, TOK[0][1])
        for t, (_, sz) in enumerate(TOK):
            if t + 1 < NT:
                dve.wait_ge(fsq_ready, t + 1)
                square_rows(t + 1, TOK[t + 1][1])
            dve.wait_ge(froot_ready, t + 1)
            link(v.reciprocal(rf[0:sz, t:t + 1], rf[0:sz, t:t + 1]))
            v.scalar_tensor_tensor(out=acc[0:sz, t], in0=acc[0:sz, t], scalar=rf[0:sz, t:t + 1], in1=gfin[0:sz],
                                   op0=ALU.mult, op1=ALU.mult).then_inc(fout_ready, 1)

    @block.tensor
    def _(pe):
        mm = nc.tensor.matmul

        def opens(L, sec, t):
            b, _, _, _, prev = tile[(L, sec, t)]
            if prev:
                pe.wait_ge(emptied_sem(tile[prev][2]), tile[prev][3])
            return bank[b]

        def products(L, sec, c, tiles, first, last, mh, ml, k0=0, ready=None):
            _, kt, cols = chunks[c]
            for half in range(2):
                p = 2 * c + half
                pe.wait_ge(low_done, p + 1)
                for n, t in enumerate(tiles):
                    b = opens(L, sec, t) if first and half == 0 else bank[tile[(L, sec, t)][0]]
                    for q in range(kt // 2):
                        k = half * (kt // 2) + q
                        if ready and n == 0:
                            ready(k)
                        w = slice(q * cols + 128 * n, q * cols + 128 * n + 128)
                        ends = half == 1 and q == kt // 2 - 1
                        mm(b[:, 0:T], whi[:, p % RING, w], mh[:, k0 + k, :], start=first and k == 0, stop=False)
                        mm(b[:, 0:T], whi[:, p % RING, w], ml[:, k0 + k, :], start=False, stop=False)
                        ins = mm(b[:, 0:T], wlo[:, p % RING, w], mh[:, k0 + k, :], start=False, stop=last and ends)
                    if last and half or n == len(tiles) - 1:
                        ins.then_inc(pe_mark, 1)

        def row_products(L, sec, c, part):
            for half in range(2):
                p = 2 * c + half
                pe.wait_ge(low_done, p + 1)
                for t, (t0, sz) in enumerate(TOK):
                    b = opens(L, sec, t) if part == 0 and half == 0 else bank[tile[(L, sec, t)][0]]
                    for q in range(2):
                        w = slice(q * DA, (q + 1) * DA)
                        kk = 4 * part + 2 * half + q
                        mm(b[0:sz, :], xh[:, kk, t0:t0 + sz], whi[:, p % RING, w], start=kk == 0, stop=False)
                        mm(b[0:sz, :], xh[:, kk, t0:t0 + sz], wlo[:, p % RING, w], start=False, stop=False)
                        ins = mm(b[0:sz, :], xl[:, kk, t0:t0 + sz], whi[:, p % RING, w], start=False, stop=kk == KD - 1)
                    if part == 1 and half or t == NT - 1:
                        ins.then_inc(pe_mark, 1)

        def mean_square(n):
            pe.wait_ge(summed, KD * (n + 1))
            mm(bank[4][:, 0:T], ones[:], ssum[:], start=True, stop=True).then_inc(stat_psum, 1)

        pe.wait_ge(first_ready, 3)
        pe.wait_ge(rows_in, 64)
        nc.tensor.transpose(bank[7][:, 0:NROW], prow[:], ident[0:NROW, 0:NROW]).then_inc(prm_psum, 1)
        pe.wait_ge(x_in[0], 16)
        pe.wait_ge(x_in[1], 16)
        for j in range(KD):
            if j >= 4:
                pe.wait_ge(h_ready, j - 3)
            for t, (t0, sz) in enumerate(TOK):
                ins = nc.tensor.transpose(bank[j % 4][:, t0:t0 + sz], xt[0:sz, t, 128 * j:128 * j + 128],
                                          ident[0:sz, 0:sz])
            ins.then_inc(xt_psum, 1)
        mean_square(0)
        pe.wait_ge(h_ready, KD)

        for L in range(LAYERS):
            if L:
                mean_square(2 * L)
            ns = 2 * L

            def normed(k, ns=ns):
                pe.wait_ge(xh_ready, KD * ns + k + 1)
                pe.wait_ge(xl_ready, KD * ns + k + 1)

            for i, (sec, part) in enumerate(MIX):
                c = base(L) + i
                if sec in ("value", "v"):
                    row_products(L, sec, c, part)
                elif sec == "branch_a":
                    products(L, sec, c, range(4 * part, 4 * part + 4), True, True, ahi, alo,
                             ready=lambda k: (pe.wait_ge(a_low, H * L + k + 1)))
                elif sec == "branch_b":
                    products(L, sec, c, range(4 * part, 4 * part + 4), True, True, bhi, blo,
                             ready=lambda k: (pe.wait_ge(b_low, H * L + k + 1)))
                elif sec == "w_out":
                    products(L, sec, c, (2 * part, 2 * part + 1), True, True, xh, xl,
                             ready=lambda k: (pe.wait_ge(merged_low, KD * L + k + 1)))
                else:
                    products(L, sec, c, (2 * part, 2 * part + 1), True, True, xh, xl,
                             ready=normed if i == 0 else None)
                if i == 0:
                    pe.wait_ge(layer_in, 64 * (L + 1))
                    pe.wait_ge(prm_ready, 1)
                    if L:
                        pe.wait_ge(ostat_psum, H * L)
                        pe.wait_ge(oroot_ready, H * L)
                    for g in range(H):
                        ins = nc.tensor.transpose(bank[7][:, 128 * g:128 * g + 128], wsp[:, g, :], ident[:])
                    ins.then_inc(wst_psum, 1)
                if i == 1:
                    pe.wait_ge(wst_ready, L + 1)
                    pe.wait_ge(consts_ready, 1)
                    for g in range(H):
                        ins = mm(bank[7][0:64, 64 * g:64 * g + 64], r8[:],
                                 wst[0:LS, g, 0:LS].unsqueeze(1).broadcast_to([LS, NSEQ, LS]), start=True, stop=True)
                    ins.then_inc(wsd_psum, 1)
                if i == 5:
                    pe.wait_ge(kdec_ready, L + 1)
                    for t, (t0, sz) in enumerate(TOK):
                        for hd in range(H):
                            ins = nc.tensor.transpose(bank[4 + t][0:sz, 128 * hd:128 * hd + 128], Z[:, hd, t0:t0 + sz], ident[:])
                        ins.then_inc(kdt_psum, 1)
                if 6 <= i < 7 + NLEV:
                    li = i - 6
                    if li == 0:
                        pe.wait_ge(kdt_ready, NT * (L + 1))
                        lhs, rhs = K, Q
                    else:
                        pe.wait_ge(lev_prod, NLEV * L + li)
                        pe.wait_ge(score_ready, score_count(L, li))
                        lhs, rhs = Z, Z
                    lv = ([0] + LEVELS)[li]
                    for p in range(SCORES if lv <= LS // 2 else PAIRS):
                        t0, sz = TOK[p]
                        for hd in range(H):
                            ins = mm(bank[4 + p][0:sz, sz * hd:sz * hd + sz], lhs[:, hd, t0:t0 + sz],
                                     rhs[:, hd, t0:t0 + sz], start=True, stop=True)
                        ins.then_inc(score_psum, 1)
                if 9 <= i < 9 + H:
                    g = i - 9
                    if g == 0:
                        pe.wait_ge(vn_ready, NT * (L + 1))
                        pe.wait_ge(wsd_ready, H * (L + 1))
                    else:
                        pe.wait_ge(a_ready, H * L + g)
                    for t, (t0, sz) in enumerate(TOK):
                        w = wst[:, g, :] if t < PAIRS else wsd[:, g, :]
                        ins = mm(bank[7][:, t0:t0 + sz], vn[0:sz, t, 128 * g:128 * g + 128], w, start=True, stop=True)
                    ins.then_inc(mix_psum, 1)
                if i == 13:
                    pe.wait_ge(score_ready, NSCORE * (L + 1))
                    pe.wait_ge(a_ready, H * (L + 1))
                    for n in range(NPC):
                        p0 = CH * (n % 2)
                        for hd in range(H):
                            cs = slice(128 * hd, 128 * hd + 128)
                            ins = mm(bank[4 + n][:, cs], kdt[p0:p0 + CH, n // 2, cs], V[p0:p0 + CH, n // 2, cs],
                                     start=True, stop=True)
                        ins.then_inc(upd_psum, 1)
                if i == 14:
                    pe.wait_ge(state_ready, NPC * (L + 1))
                    for hd in range(H):
                        b = bank[4 + hd]
                        cs = slice(128 * hd, 128 * hd + 128)
                        for p in range(PAIRS):
                            mm(b[:, 128 * p:128 * p + 128], V[:, p, cs], sc[:, p, hd, :], start=p == 0, stop=False)
                        for n in range(1, NPC):
                            S = (S12 if n - 1 < 2 else S34)[:, (n - 1) % 2]
                            mm(b[:, CH * n:CH * n + CH], S[:, hd], QE[:, hd, CH * n:CH * n + CH], start=False, stop=False)
                        mm(b[:, TP:T], V[0:64, PAIRS, cs], scs[:, hd, :], start=False, stop=True).then_inc(o_psum, 1)
                if 15 <= i < 15 + H:
                    hd = i - 15
                    cs = slice(128 * hd, 128 * hd + 128)
                    st = s0[hd % 2]
                    pe.wait_ge(s0_in[hd % 2], 16 * (2 * L + hd // 2 + 1))
                    if hd:
                        pe.wait_ge(s0_ready, H * L + hd)
                    else:
                        pe.wait_ge(o_ready, H * (L + 1))
                    for b in range(NSEQ):
                        ins = mm(bank[6][:, LS * b:LS * b + LS], st[:, b, :], QE[:, hd, TP + LS * b:TP + LS * b + LS],
                                 start=b == 0, stop=b == NSEQ - 1, skip_group_check=True)
                    ins.then_inc(so_psum, 1)
                    pe.wait_ge(vex_ready, H * L + hd + 1)
                    for b in (0, 1):
                        ins = mm(bank[4 + b][:], kdt[0:64, PAIRS, cs], vex[:, 4 * b:4 * b + 4, :], start=True, stop=True)
                    ins.then_inc(su_psum, 1)
                if i == 19:
                    pe.wait_ge(osq_ready, L + 1)
                    for hd in range(H):
                        mm(bank[4 + hd][:, 0:T], ones[:], osq[:, hd, :], start=True, stop=True).then_inc(ostat_psum, 1)
            mean_square(2 * L + 1)
            if L % 2 == 0:
                ns = 2 * L + 1

                def normed(k, ns=ns):
                    pe.wait_ge(xh_ready, KD * ns + k + 1)
                    pe.wait_ge(xl_ready, KD * ns + k + 1)

                for i, (sec, part) in enumerate(FFN):
                    c = first_chunk[(L, "gate")] + i
                    if sec == "down":
                        k0, kt = KCUT[part % 3]
                        t = 2 * (part // 3)
                        products(L, sec, c, (t, t + 1), part % 3 == 0, part % 3 == 2, fh, fl, k0=k0,
                                 ready=lambda k, k0=k0: pe.wait_ge(hid_low, k0 + k + 1))
                    else:
                        products(L, sec, c, (2 * part, 2 * part + 1), True, True, xh, xl,
                                 ready=normed if i == 0 else None)

        for src, psum, ready, before in ((h, sum_psum, sum_done, None), (xn, hn_psum, y_ready, sum_done)):
            if before is None:
                pe.wait_ge(dve_emptied, emptied["dve"])
            else:
                pe.wait_ge(xn_ready, KD * 2 * LAYERS)
            for n, (t, hf_) in enumerate(OUTS):
                t0, sz = TOK[t]
                if before is not None:
                    pe.wait_ge(before, n + 1)
                for k in range(4):
                    ins = nc.tensor.transpose(bank[ROW_BANK[n]][0:sz, 128 * k:128 * k + 128],
                                              src[:, 4 * hf_ + k, t0:t0 + sz], ident[:])
                ins.then_inc(psum, 1)
        pe.wait_ge(router_in, 16)
        for t, (t0, sz) in enumerate(TOK):
            for k in range(KD):
                ins = mm(bank[7][0:sz, NE * t:NE * t + NE], xn[:, k, t0:t0 + sz], rw[:, k, :], start=k == 0, stop=k == KD - 1)
        ins.then_inc(logit_psum, 1)
        pe.wait_ge(chosen_ready, 1)
        for t, (_, sz) in enumerate(TOK):
            for q in range(t):
                mm(bank[7][0:sz, NE * t:NE * t + NE], ones[:, 0:sz], mk[:, q, :], start=q == 0, stop=False)
            mm(bank[7][0:sz, NE * t:NE * t + NE], upper[0:sz, 0:sz], mk[0:sz, t, :], start=t == 0, stop=True)
        for t, (_, sz) in enumerate(TOK):
            ins = mm(bank[7][:, NE * NT:NE * NT + NE], ones[0:sz, :], mk[0:sz, t, :], start=t == 0, stop=t == NT - 1)
        ins.then_inc(rank_psum, 1)

        def gather(item):
            pe.wait_ge(pick_ready, item + 1)
            for hh in range(2):
                for k in range(4):
                    for t, (_, sz) in enumerate(TOK):
                        kk = 4 * hh + k
                        ins = mm(bank[6 + hh][:, 128 * k:128 * k + 128], hn[0:sz, t, 128 * kk:128 * kk + 128],
                                 pick[0:sz, t, :], start=t == 0, stop=t == NT - 1)
                ins.then_inc(xg_psum, 1)

        def hidden_rows_turned(item, j):
            pe.wait_ge(he_ready, NG * item + (j + 1))
            if j == 1:
                pe.wait_ge(pickt_ready, item + 1)
            if j >= 2:
                pe.wait_ge(hel_ready, NG * item + (j - 1))
            for n, t in enumerate(group_tiles(j)):
                ins = nc.tensor.transpose(bank[4 + j % 2][:, 128 * n:128 * n + 128], He[:, 128 * t:128 * t + 128], ident[:])
            ins.then_inc(het_psum, 1)

        def chunk(item, i, ahead):
            if i >= NEC:
                item, i = item + 1, i - NEC
            kind, j, part, k0, kt, c0, cols = ECH[i]
            if kind == "down" and j == 0:
                pe.wait_ge(he_ready, NG * item + NG)
            for half in range(2):
                p = 2 * i + half
                pe.wait_ge(low_done, 2 * NEC * item + (2 * NDENSE + p + 1))
                if kind != "down" and part == 0 and half == 0:
                    if j == 1:
                        pe.wait_ge(sum_done, NO * item + NO)
                    elif j > 1:
                        pe.wait_ge(gate_emptied if kind == "gate" else he_ready, NG * item + (j - 1))
                for q in range(kt // 2):
                    kk = k0 + half * (kt // 2) + q
                    if kind == "down":
                        if kk % 4 == 0:
                            pe.wait_ge(hel_ready, NG * item + (kk // 4 + 1))
                        for hh in range(2):
                            w = slice(q * cols + 512 * hh, q * cols + 512 * hh + 512)
                            mm(bank[2 + hh][:], heh[:, kk, :], whi[:, p % RING, w], start=kk == 0, stop=False)
                            mm(bank[2 + hh][:], heh[:, kk, :], wlo[:, p % RING, w], start=False, stop=False)
                            ins = mm(bank[2 + hh][:], hel[:, kk, :], whi[:, p % RING, w], start=False, stop=kk == KF - 1)
                    else:
                        if j == 0 and kk % 4 == 0:
                            pe.wait_ge(xg_low, 2 * item + (kk // 4 + 1))
                        b = bank[(kind == "up") + 2 * (j % 2)]
                        w = slice(q * cols, (q + 1) * cols)
                        mm(b[:, 0:cols], xeh[:, kk, :], whi[:, p % RING, w], start=kk == 0, stop=False)
                        mm(b[:, 0:cols], xeh[:, kk, :], wlo[:, p % RING, w], start=False, stop=False)
                        ins = mm(b[:, 0:cols], xel[:, kk, :], whi[:, p % RING, w], start=False, stop=kk == KD - 1)
                ins.then_inc(pe_mark, 1)
            if kind == "up" and i == closing[(kind, j)]:
                if j == 1:
                    for t, (t0, sz) in enumerate(TOK):
                        ins = nc.tensor.transpose(bank[5][:, t0:t0 + sz], pick[0:sz, t, :], ident[0:sz, 0:sz])
                    ins.then_inc(pickt_psum, 1)
                if j:
                    hidden_rows_turned(item, j - 1)
                if j == NG - 1:
                    if ahead:
                        gather(item + 1)
                    hidden_rows_turned(item, j)

        def scatter(item, ahead):
            pe.wait_ge(pickt_ready, item + 1)
            pe.wait_ge(y_low, 2 * item + 2)
            pe.wait_ge(hel_ready, NG * item + NG)
            if ahead:
                pe.wait_ge(xg_low, 2 * item + 4)
            for n, (t, hf_) in enumerate(OUTS):
                t0, sz = TOK[t]
                w = slice(512 * hf_, 512 * hf_ + 512)
                mm(bank[SUM_BANK[n]][0:sz, :], pickt[:, t0:t0 + sz], Yh[:, w], start=True, stop=False)
                mm(bank[SUM_BANK[n]][0:sz, :], pickt[:, t0:t0 + sz], Yl[:, w], start=False, stop=True).then_inc(
                    sum_psum, 1)

        def extra(item, n):
            pe.wait_ge(sum_done, NO * item + NO)
            gather(item)
            for i in range(NEC):
                chunk(item, i, False)
            scatter(item, False)

        pe.wait_ge(y_ready, NO)
        pe.wait_ge(sum_done, NO)
        gather(0)
        for i in range(HEAD):
            chunk(0, i, True)
        with pe.Fori(0, NE - 1) as e:
            for i in range(HEAD, HEAD + NEC):
                chunk(e, i, True)
            scatter(e, True)
        for i in range(HEAD, NEC):
            chunk(NE - 1, i, False)
        scatter(NE - 1, False)
        extra_blocks(pe, extra)

    ctx.close()


_OUTS = {"y_prompt": (1, 256, 1024), "y_sample": (8, 8, 1024), "prompt_state": (2, 1, 4, 128, 128),
         "sample_state": (2, 8, 4, 128, 128), "v_rows": (2, 8, 8, 512)}


def kernel(**inputs):
    import numpy as np
    import concourse.bacc as bacc
    from concourse.bass_utils import run_bass_kernel_spmd

    nc = bacc.Bacc("TRN2", target_bir_lowering=False, num_devices=1)
    arrays, ins, outs = {}, {}, {}
    for name, a in inputs.items():
        arrays["in_" + name] = np.ascontiguousarray(a)
        ins[name] = nc.dram_tensor("in_" + name, a.shape, mybir.dt.float32, kind="ExternalInput").ap()
    for name, shape in _OUTS.items():
        outs[name] = nc.dram_tensor("out_" + name, shape, mybir.dt.float32, kind="ExternalOutput").ap()
    hybrid_trunk_program(nc, ins, outs)
    r = run_bass_kernel_spmd(nc, [arrays], core_ids=[0])
    return tuple(r.results[0]["out_" + name] for name in _OUTS)
```

```python
import concourse.bass as bass
from concourse import mybir
from contextlib import ExitStack


def hybrid_trunk_program(nc, A, OUT):
    F = mybir.dt.float32
    R = mybir.dt.float32r
    I32 = mybir.dt.int32
    U32 = mybir.dt.uint32
    ALU = mybir.AluOpType
    ACT = mybir.ActivationFunctionType

    D = A["x_prompt"].shape[2]
    TP = A["x_prompt"].shape[1]
    NSEQ, LS = A["x_sample"].shape[0], A["x_sample"].shape[1]
    T = TP + NSEQ * LS
    LAYERS = A["w_in"].shape[0]
    KD = D // 128
    DA = A["ln_v_g"].shape[1]
    H = DA // 128
    FF = A["dense_w_gate"].shape[2]
    KF = FF // 128
    NE = A["router_w"].shape[2]
    TOK = [(0, 128), (128, 128), (256, 64)]
    NT = len(TOK)
    STAT = [(t0, 0) if sz == 128 else (t0 + sz - 128, 128 - sz) for t0, sz in TOK]
    CH = 64
    NPC = TP // CH
    PAIRS = TP // 128
    EPS = 1e-6
    LEVELS = [32, 16, 8, 4, 2, 1]
    COL = {"u": 0, "v": DA, "q": 2 * DA, "forget": 3 * DA, "value": 4 * DA, "out_gate": 5 * DA,
           "gate_a": 6 * DA, "gate_b": 6 * DA + D}

    CHUNK = 2048
    AHEAD = 3
    PIECE = CHUNK // 2
    RING = 2 * AHEAD
    BANKS = 4
    chunks = []
    mark_after = []
    tile = {}
    first_chunk = {}
    order = []
    marks = 0
    emptied = {"act": 0, "dve": 0}

    def rows(w, k0, kt, c0, cols):
        return w[k0 * 128:(k0 + kt) * 128, c0:c0 + cols].rearrange("(k p) n -> p k n", p=128)

    def add_chunk(key, src, kt, cols, opens, closes, by):
        nonlocal marks
        first_chunk.setdefault(key[:2], len(chunks))
        for t in opens:
            n = len(order)
            order.append((key[0], key[1], t))
            tile[order[-1]] = [n % BANKS, None, by, None, order[n - BANKS] if n >= BANKS else None]
        marks += 1
        mark_after.append(marks)
        for t in closes:
            marks += 1
            emptied[by] += 1
            tile[(key[0], key[1], t)][1] = marks
            tile[(key[0], key[1], t)][3] = emptied[by]
        if not closes:
            marks += 1
        chunks.append((src, kt, cols))
        mark_after.append(marks)

    MIX = [("forget", 0), ("forget", 1), ("q", 0), ("q", 1), ("value", 0), ("value", 1), ("v", 0), ("v", 1),
           ("u", 0), ("u", 1)] + [("gate_a", i) for i in range(4)] + [("branch_a", 0), ("branch_a", 1),
           ("out_gate", 0), ("out_gate", 1)] + [("gate_b", i) for i in range(4)] + [
           ("branch_b", 0), ("branch_b", 1)] + [("w_out", i) for i in range(4)]
    KCUT = [(0, 8), (8, 8), (16, KF - 16)]
    FFN = [(s, i) for i in range(KF // 2) for s in ("gate", "up")] + \
          [("down", 3 * i + j) for i in range(4) for j in range(3)]
    for L in range(LAYERS):
        for sec, i in MIX:
            if sec in ("value", "v"):
                add_chunk((L, sec), rows(A["w_in"][L], 4 * i, 4, COL[sec], DA), 4, DA,
                          range(NT) if i == 0 else (), () if i == 0 else range(NT), "act")
            elif sec in ("branch_a", "branch_b"):
                w = A["w_" + sec][L]
                add_chunk((L, sec), rows(w, 0, H, 512 * i, 512), H, 512,
                          range(4 * i, 4 * i + 4), range(4 * i, 4 * i + 4), "dve")
            elif sec == "w_out":
                add_chunk((L, sec), rows(A["w_out"][L], 0, KD, 256 * i, 256), KD, 256,
                          (2 * i, 2 * i + 1), (2 * i, 2 * i + 1), "dve")
            else:
                add_chunk((L, sec), rows(A["w_in"][L], 0, KD, COL[sec] + 256 * i, 256), KD, 256,
                          (2 * i, 2 * i + 1), (2 * i, 2 * i + 1), "act")
        if L % 2 == 0:
            for sec, i in FFN:
                if sec == "down":
                    k0, kt = KCUT[i % 3]
                    ts = (2 * (i // 3), 2 * (i // 3) + 1)
                    add_chunk((L, sec), rows(A["dense_w_down"][L // 2], k0, kt, 256 * (i // 3), 256), kt, 256,
                              ts if i % 3 == 0 else (), ts if i % 3 == 2 else (), "dve")
                else:
                    add_chunk((L, sec), rows(A["dense_w_" + sec][L // 2], 0, KD, 256 * i, 256), KD, 256,
                              (2 * i, 2 * i + 1), (2 * i, 2 * i + 1), "act" if sec == "gate" else "dve")
    NDENSE = len(chunks)
    assert NDENSE % AHEAD == 0

    groups = [(512 * j, min(512, FF - 512 * j)) for j in range(-(-FF // 512))]
    ECH = []
    for j, (c0, cols) in enumerate(groups):
        for s in ("gate", "up"):
            kt = CHUNK // cols
            for part in range(KD // kt):
                ECH.append((s, j, part, part * kt, kt, c0, cols))
    for j in range(KF // 2):
        ECH.append(("down", j, 0, 2 * j, 2, 0, D))
    NEC = len(ECH)
    assert NEC % AHEAD == 0
    NG = len(groups)
    closing = {(s, j): max(i for i, x in enumerate(ECH) if x[0] == s and x[1] == j)
               for s in ("gate", "up") for j in range(NG)}
    CAP = 128

    at = [-(-nc.sbuf_base // 32) * 32]

    def place(name, shape, dt=F, offset=None):
        size = 4
        for s in shape[1:]:
            size *= s
        if offset is None:
            offset = at[0]
            at[0] += -(-size // 32) * 32
        return nc.alloc_sbuf_tensor_at(name, shape, dt, offset=offset)

    raw = place("weights_raw", [128, RING, PIECE])
    whi = place("weights_high", [128, RING, PIECE], R)
    wlo = place("weights_low", [128, RING, PIECE], R)
    h = place("residual", [128, KD, T])
    m_at = at[0]
    xn = place("normed_or_merged", [128, KD, T])
    xh_at = at[0]
    xh = place("moving_high", [128, KD, T], R)
    xl_at = at[0]
    xl = place("moving_low", [128, KD, T], R)
    ident = place("identity", [128, 128])
    ones = place("ones", [128, 128])
    upper = place("upper_ones", [128, 128])
    iota = place("iota_row", [128, 128])
    lmask = place("level_masks", [128, len(LEVELS) + 1, 128], I32)
    smask = place("scan_keep", [128, T])
    bmask = place("sequence_mask", [64, NSEQ])
    r8 = place("row_spread", [LS, NSEQ * LS])
    eps_t = place("eps", [128, 1])
    NROW = 2 * LAYERS * KD + 2 * LAYERS * H
    prow = place("param_rows", [NROW, 128])
    prm = place("param_columns", [128, NROW])
    lbt = place("lower_bound_terms", [128, 5, H])
    wsp = place("spatial_raw", [128, H, 128])
    wst = place("spatial_transposed", [128, H, 128])
    wsd = place("spatial_sample", [64, H, 64])
    bsp = place("spatial_bias", [128, H, 128])
    ln_at = at[0]
    lng = place("ln_gain", [128, DA])
    lnb = place("ln_shift", [128, DA])
    sq = place("squares", [128, 2, T])
    ssum = place("square_sum", [128, T])
    rcol = place("inverse_rms", [128, NT])
    orc = place("out_inverse_rms", [128, H, NT])
    el = place("chunk_decay", [128, H, NPC + NSEQ])
    bst = place("ln_stats", [128, NT, 6])
    bag = place("ln_mean_var", [128, NT, 2])
    tmp = place("branch_product", [128, 2, T])
    cmb = place("combine", [128, NT, NE])
    slot = place("slot_of_token", [128, NT, NE])
    cslot = place("slot_now", [128, NT])
    cgate = place("gate_now", [128, NT])
    BLOCKS = -(-T // CAP)
    NMORE = (BLOCKS - 1) * NE
    full = place("more_blocks", [128, NMORE + 1], I32)
    items = place("block_items", [128, NMORE], I32)
    fullf = place("more_blocks_f", [128, 3, NMORE])
    rw = place("router", [128, KD, NE])
    region = at[0]

    def later(name, shape, dt, offset):
        return place(name, shape, dt, offset)

    W5 = 4 * H * T
    ahi = later("a_high", [128, H, T], R, region)
    alo = later("a_low", [128, H, T], R, region + W5)
    gb = later("gate_b", [128, KD, T], F, region)
    o = region + 2 * W5
    u = later("u_or_out_gate", [128, H, T], F, o); o += W5
    V = later("value", [128, NT, DA], F, o); o += 4 * NT * DA
    vn_at = o
    vn = later("v_normed", [128, NT, DA], F, o)
    o += 4 * NT * DA
    sc = later("scores", [128, PAIRS, H, 128], F, o)
    scs = later("scores_sample", [64, H, 64], F, o + 4 * PAIRS * H * 128); o += 4 * PAIRS * H * 128 + 4 * H * 64
    z_at = o
    Z = later("level_product", [128, H, T], F, o); o += W5
    e_at = o
    E = later("level_decay", [128, H, T], F, o); o += W5
    Q = later("query", [128, H, T], F, o); o += W5
    k_at = o
    K = later("key", [128, H, T], F, o); o += W5
    g_at = o
    G = later("log_decay", [128, H, T], F, o); o += W5
    kdt = later("key_decayed_tok", [128, NT, DA], F, o)
    o += 4 * NT * DA
    QE = later("query_decayed", [128, H, T], F, o); o += W5
    assert o <= nc.sbuf_usable_end, (o, nc.sbuf_usable_end)
    S12 = later("state_1_2", [128, 2, H, 128], F, e_at)
    S34 = later("state_3_4", [128, 2, H, 128], F, z_at)
    vex = later("value_by_sequence", [64, NSEQ, 128], F, k_at)
    s0 = [later(f"state_sample_{n}", [128, NSEQ, 128], F, q)
          for n, q in enumerate((g_at, vn_at, e_at, vn_at + 4 * NT * DA))]
    bhi = later("b_high", [128, H, T], R, k_at)
    blo = later("b_low", [128, H, T], R, g_at)
    xt = later("x_rows", [128, NT, D], F, z_at)
    fh = later("hidden_high", [128, KF, T], R, region)
    fl = later("hidden_low", [128, KF, T], R, region + 4 * KF * T)
    o = region + 8 * KF * T
    sg = later("silu_gate", [128, 2, T], F, o)
    hf = later("hidden", [128, 2, T], F, o + 8 * T)
    assert o + 16 * T <= nc.sbuf_usable_end
    o = region
    acc = later("sum_rows", [128, NT, D], F, o); o += 4 * NT * D
    hn = later("normed_rows", [128, NT, D], F, o); o += 4 * NT * D
    He = later("expert_hidden", [128, FF], F, o); o += 4 * FF
    heh = later("expert_hidden_high", [128, KF, CAP], R, o); o += 4 * KF * CAP
    hel = later("expert_hidden_low", [128, KF, CAP], R, o); o += 4 * KF * CAP
    assert o <= nc.sbuf_usable_end
    xeh = later("expert_in_high", [128, KD, CAP], R, xh_at)
    xel = later("expert_in_low", [128, KD, CAP], R, xl_at)
    sge = later("expert_silu", [128, 2, 512], F, xh_at + 4 * KD * CAP)
    assert 8 * KD * CAP + 4 * NT * CAP <= 4 * KD * T and 4 * T + 8 * D <= 4 * KD * T
    pick = later("pick", [128, NT, CAP], F, xh_at + 8 * KD * CAP)
    pickt = later("pick_t", [128, T], R, m_at)
    Yh = later("expert_out_high", [128, D], R, m_at + 4 * T)
    Yl = later("expert_out_low", [128, D], R, m_at + 4 * T + 4 * D)
    lo_ = xl_at + 4 * KD * CAP
    lg = later("logits", [128, NT, 8], F, lo_)
    top = later("top_values", [128, NT, 8], F, lo_ + 96)
    topi = later("top_indices", [128, NT, 8], U32, lo_ + 192)
    topf = later("top_indices_f", [128, NT, 8], F, lo_ + 288)
    m1 = later("first_mask", [128, NT, 8], F, lo_ + 384)
    m2 = later("second_mask", [128, NT, 8], F, lo_ + 480)
    mk = later("chosen", [128, NT, 8], F, lo_ + 576)
    g1 = later("gate_terms", [128, 4, NT], F, lo_ + 672)
    lgt = later("logits_by_expert", [NE, T], F, lo_ + 1024)
    gfin = later("final_gain", [128, D], F, ln_at)
    ssf = later("final_square_sum", [128, NT], F, lo_ + 800)
    rf = later("final_inverse_rms", [128, NT], F, lo_ + 832)

    ctx = ExitStack()
    bank = [ctx.enter_context(nc.psum_tensor(f"bank{i}", [128, 512], F)) for i in range(8)]

    def sem(name):
        return ctx.enter_context(nc.semaphore(name))

    raw_full = [sem(f"raw_full_{i}") for i in range(RING)]
    high_done = sem("high_done")
    low_done = sem("low_done")
    pe_mark = sem("pe_mark")
    act_emptied = sem("act_emptied")
    dve_emptied = sem("dve_emptied")
    act_link = sem("act_link")
    dve_link = sem("dve_link")
    pool_link = sem("pool_link")
    first_ready = sem("eps_ones_identity_ready")
    consts_ready = sem("other_constants_ready")
    x_in = [sem("x_prompt_in"), sem("x_sample_in")]
    rows_in = sem("param_rows_in")
    layer_in = sem("layer_params_in")
    router_in = sem("router_in")
    gfin_in = sem("final_gain_in")
    prm_psum = sem("param_columns_psum")
    prm_ready = sem("param_columns_ready")
    lb_exp = sem("lower_bound_exp")
    lb_ready = sem("lower_bound_ready")
    xt_psum = sem("x_transposed_psum")
    h_ready = sem("residual_ready")
    squared = sem("squared")
    summed = sem("square_summed")
    stat_psum = sem("mean_square_psum")
    root_ready = sem("root_ready")
    rinv_ready = sem("inverse_rms_ready")
    spread_psum = sem("inverse_rms_spread")
    xn_ready = sem("normed_ready")
    xh_ready = sem("moving_high_ready")
    xl_ready = sem("moving_low_ready")
    wst_psum = sem("spatial_transposed_psum")
    wst_ready = sem("spatial_transposed_ready")
    wsd_psum = sem("spatial_sample_psum")
    wsd_ready = sem("spatial_sample_ready")
    softplus_a = sem("softplus_forget_ready")
    logsig_ready = sem("key_argument_ready")
    bound_arg = sem("bound_argument_ready")
    softplus_b = sem("softplus_bound_ready")
    key_ready = sem("key_ready")
    cum_ready = sem("log_decay_ready")
    expg_ready = sem("decay_ready")
    qdec_ready = sem("query_decayed_ready")
    gap_ready = sem("gap_ready")
    gap_exp = sem("gap_decay_ready")
    kdec_ready = sem("key_decayed_ready")
    kdt_psum = sem("key_decayed_psum")
    kdt_ready = sem("key_decayed_tok_ready")
    var_ready = sem("ln_var_ready")
    dev_ready = sem("ln_deviation_ready")
    vn_scaled = sem("v_scaled_ready")
    vn_ready = sem("v_normed_ready")
    vrow_out = sem("v_rows_out")
    mix_psum = sem("spatial_mix_psum")
    a_ready = sem("a_ready")
    a_high = sem("a_high_ready")
    a_low = sem("a_low_ready")
    lev_diff = sem("level_difference_ready")
    lev_exp = sem("level_decay_ready")
    lev_prod = sem("level_product_ready")
    score_psum = sem("score_psum")
    score_ready = sem("score_ready")
    upd_psum = sem("state_update_psum")
    state_ready = sem("state_ready")
    o_psum = sem("out_psum")
    o_ready = sem("out_ready")
    pstate_out = sem("prompt_state_out")
    s0_in = [sem(f"sample_state_in_{hd}") for hd in range(H)]
    s0_out = [sem(f"sample_state_out_{hd}") for hd in range(H)]
    vex_ready = sem("value_by_sequence_ready")
    so_psum = sem("sample_out_psum")
    su_psum = sem("sample_update_psum")
    s0_ready = sem("sample_state_ready")
    osq_ready = sem("out_squares_ready")
    ostat_psum = sem("out_mean_square_psum")
    oroot_ready = sem("out_root_ready")
    orinv_ready = sem("out_inverse_rms_ready")
    ospread_psum = sem("out_inverse_rms_spread")
    b_ready = sem("b_ready")
    b_high = sem("b_high_ready")
    b_low = sem("b_low_ready")
    merged_ready = sem("merged_ready")
    merged_high = sem("merged_high_ready")
    merged_low = sem("merged_low_ready")
    hid_high = sem("hidden_high_ready")
    hid_low = sem("hidden_low_ready")

    hn_psum = sem("normed_rows_psum")
    logit_psum = sem("logit_psum")
    lgt_psum = sem("logits_by_expert_psum")
    lgt_ready = sem("logits_by_expert_ready")
    lg_ready = sem("logits_ready")
    top_ready = sem("top_ready")
    gap_top = sem("top_gap_exp_ready")
    chosen_ready = sem("chosen_ready")
    rank_psum = sem("rank_psum")
    table_ready = sem("slot_table_ready")
    pick_ready = sem("pick_ready")
    xg_psum = sem("expert_in_psum")
    xg_high = sem("expert_in_high_ready")
    xg_low = sem("expert_in_low_ready")
    gate_emptied = sem("expert_gate_emptied")
    he_ready = sem("expert_hidden_ready")
    het_psum = sem("expert_hidden_t_psum")
    heh_ready = sem("expert_hidden_high_ready")
    hel_ready = sem("expert_hidden_low_ready")
    pickt_psum = sem("pick_t_psum")
    pickt_ready = sem("pick_t_ready")
    y_ready = sem("expert_out_high_ready")
    y_low = sem("expert_out_low_ready")
    sum_psum = sem("expert_sum_psum")
    sum_done = sem("expert_sum_done")
    fsq_ready = sem("final_square_sum_ready")
    froot_ready = sem("final_root_ready")
    fout_ready = sem("final_rows_ready")
    y_out = sem("y_out")
    columns_ready = sem("slot_column_ready")
    gates_ready = sem("gate_column_ready")
    shift_done = sem("slots_shifted")

    MB = mark_after[-1]
    OUTS = [(t, hf_) for t in range(NT) for hf_ in range(2)]
    SUM_BANK = [2, 3, 6, 7, 4, 5]
    ROW_BANK = [0, 1, 2, 3, 5, 6]
    NO = len(OUTS)

    def down_bank(ahead):
        return 2 if ahead else 0

    def width(i):
        return ECH[i % NEC][4] * ECH[i % NEC][6]

    def group_tiles(j):
        c0, cols = groups[j]
        return range(c0 // 128, (c0 + cols) // 128)

    HEAD = 3

    def any_extra(eng):
        eng.wait_ge(table_ready, 1)
        return eng.value_load(full[0:1, NMORE:NMORE + 1], min_val=0, max_val=1) > 0

    def extra_block(eng, n):
        more = eng.value_load(full[0:1, bass.ds(n, 1)], min_val=0, max_val=1)
        item = eng.value_load(items[0:1, bass.ds(n, 1)], min_val=0, max_val=NMORE) + NE
        return more > 0, item

    def extra_blocks(eng, run):
        with eng.If(any_extra(eng)):
            with eng.Fori(0, NMORE) as n:
                more, item = extra_block(eng, n)
                with eng.If(more):
                    run(item, n)

    def piece_width(c):
        return (chunks[c][1] * chunks[c][2] if c < NDENSE else width(c - NDENSE)) // 2

    def emptied_sem(by):
        return act_emptied if by == "act" else dve_emptied

    def base(L):
        return first_chunk[(L, "forget")]

    NLEV = len(LEVELS)
    GATES_AT, KEYS_AT, SUMS_AT, DECAYS_AT, DIAGONAL_AT, TURN_AT, SCORES_AT, LN_AT, MIX_AT = 2, 3, 4, 5, 6, 7, 7, 8, 10
    STATES_AT, OUT_AT, SAMPLE_AT, ONORM_AT, B_AT = 14, 15, 16, 20, 21
    SCORES = PAIRS + 1
    NSCORE = sum(SCORES if lv <= LS // 2 else PAIRS for lv in [0] + LEVELS)

    def score_count(L, li):
        return NSCORE * L + sum(SCORES if lv <= LS // 2 else PAIRS for lv in ([0] + LEVELS)[:li])

    def halves(X, lv, n):
        v = X[:, :, 0:n].rearrange("p h (b c) -> p h b c", c=2 * lv)
        return v[:, :, :, 0:lv], v[:, :, :, lv:2 * lv], v[:, :, :, lv - 1:lv].broadcast_to([128, H, n // (2 * lv), lv])

    def tokens_of(lv):
        return T if lv <= LS // 2 else TP

    P_MIX, P_FFN, P_LB, P_HG = 0, LAYERS * KD, 2 * LAYERS * KD, 2 * LAYERS * KD + LAYERS * H

    block = ctx.enter_context(nc.Block())

    @block.sync
    def _(sp):
        sp.dma_start(xt[:, 0:PAIRS, :], A["x_prompt"][0].rearrange("(t p) d -> p t d", p=128)).then_inc(x_in[0], 16)
        sp.dma_start(xt[0:64, PAIRS, :], A["x_sample"].rearrange("b j d -> (b j) d")).then_inc(x_in[1], 16)
        for n, (name, k) in enumerate((("norm_mix_g", KD), ("norm_ffn_g", KD), ("lower_bounds", H), ("hgrn_norm_g", H))):
            r = (P_MIX, P_FFN, P_LB, P_HG)[n]
            sp.dma_start(prow[r:r + LAYERS * k, :], A[name].rearrange("l (k p) -> (l k) p", p=128)).then_inc(rows_in, 16)

        for c, (src, kt, cols) in enumerate(chunks):
            for half in range(2):
                p = 2 * c + half
                ks = slice(half * (kt // 2), (half + 1) * (kt // 2))
                if p >= RING:
                    sp.wait_ge(low_done, p - RING + 1)
                sp.dma_start(raw[:, p % RING, 0:kt // 2 * cols].rearrange("p (k n) -> p k n", n=cols),
                             src[:, ks]).then_inc(raw_full[p % RING], 16)

        def load_expert(item, e):
            for i, (kind, j, part, k0, kt, c0, cols) in enumerate(ECH):
                for half in range(2):
                    p = 2 * i + half
                    sp.wait_ge(low_done, 2 * NEC * item + (2 * NDENSE + p - RING + 1))
                    sp.dma_start(raw[:, p % RING, 0:kt // 2 * cols].rearrange("p (k n) -> p k n", n=cols),
                                 rows(A["moe_w_" + kind][0, e], k0 + half * (kt // 2), kt // 2, c0, cols)).then_inc(
                                     raw_full[p % RING], 16)

        with sp.Fori(0, NE) as e:
            load_expert(e, e)
        extra_blocks(sp, lambda item, n: load_expert(item, n % NE))
        for t in range(NT):
            sp.wait_ge(fout_ready, t + 1)
            if t < PAIRS:
                sp.dma_start(OUT["y_prompt"][0, 128 * t:128 * t + 128, :], acc[:, t, :]).then_inc(y_out, 16)
            else:
                sp.dma_start(OUT["y_sample"].rearrange("b j d -> (b j) d"), acc[0:64, t, :]).then_inc(y_out, 16)
        sp.wait_ge(y_out, 16 * NT)

    @block.gpsimd
    def _(pool):
        links = [0]

        def link(ins):
            links[0] += 1
            ins.then_inc(pool_link, 1)
            pool.wait_ge(pool_link, links[0])

        def layer_params(L):
            pool.dma_start(wsp[:], A["w_spatial"][L].rearrange("g t s -> t g s")).then_inc(layer_in, 16)
            pool.dma_start(bsp[:], A["b_spatial"][L].partition_broadcast(128)).then_inc(layer_in, 16)
            pool.dma_start(lng[:], A["ln_v_g"][L].partition_broadcast(128)).then_inc(layer_in, 16)
            pool.dma_start(lnb[:], A["ln_v_b"][L].partition_broadcast(128)).then_inc(layer_in, 16)

        nc.gpsimd.memset(eps_t[:], EPS).then_inc(first_ready, 1)
        nc.gpsimd.memset(ones[:], 1.0).then_inc(first_ready, 1)
        link(nc.gpsimd.memset(ident[:], 0.0))
        nc.gpsimd.affine_select(out=ident[:], in_=ident[:], compare_op=ALU.not_equal, fill=1.0, base=0,
                                pattern=[[-1, 128]], channel_multiplier=1).then_inc(first_ready, 1)
        pool.wait_ge(first_ready, 3)
        link(nc.gpsimd.affine_select(out=upper[:], in_=ones[:], compare_op=ALU.is_ge, fill=0.0, base=0,
                                     pattern=[[1, 128]], channel_multiplier=-1))
        link(nc.gpsimd.iota(iota[:], pattern=[[1, 128]], base=0, channel_multiplier=0,
                            allow_small_or_imprecise_dtypes=True))
        link(nc.gpsimd.memset(lmask[:], 0))
        link(nc.gpsimd.affine_select(out=lmask[:, 0, :], in_=lmask[:, 0, :], compare_op=ALU.not_equal, fill=1.0, base=0,
                                     pattern=[[-1, 128]], channel_multiplier=1))
        for n, lv in enumerate(LEVELS):
            v = lmask[:, n + 1, :].rearrange("p (b c) -> p b c", c=2 * lv)
            nb = 128 // (2 * lv)
            link(nc.gpsimd.memset(v[:, :, lv:2 * lv], 1))
            link(nc.gpsimd.affine_select(out=v, in_=v, compare_op=ALU.is_ge, fill=0.0, base=0,
                                         pattern=[[-2 * lv, nb], [0, 2 * lv]], channel_multiplier=1))
            link(nc.gpsimd.affine_select(out=v, in_=v, compare_op=ALU.is_ge, fill=0.0, base=lv - 1,
                                         pattern=[[2 * lv, nb], [0, 2 * lv]], channel_multiplier=-1))
        link(nc.gpsimd.memset(smask[:], 1.0))
        link(nc.gpsimd.memset(smask[:, 0:TP:CH], 0.0))
        link(nc.gpsimd.memset(smask[:, TP:T:LS], 0.0))
        link(nc.gpsimd.memset(bmask[:], 1.0))
        link(nc.gpsimd.affine_select(out=bmask[:], in_=bmask[:], compare_op=ALU.is_ge, fill=0.0, base=0,
                                     pattern=[[-LS, NSEQ]], channel_multiplier=1))
        link(nc.gpsimd.affine_select(out=bmask[:], in_=bmask[:], compare_op=ALU.is_ge, fill=0.0, base=LS - 1,
                                     pattern=[[LS, NSEQ]], channel_multiplier=-1))
        nc.gpsimd.tensor_copy(r8[:].rearrange("p (b t) -> p b t", t=LS),
                              ident[0:LS, 0:LS].unsqueeze(1).broadcast_to([LS, NSEQ, LS])).then_inc(consts_ready, 1)

        def load_s0(L, hd):
            pool.dma_start(s0[hd][:], A["state_hgrn"][L, :, hd].rearrange("b p v -> p b v")).then_inc(s0_in[hd], 16)

        def spread_values(L, hd):
            values = V[0:64, PAIRS, 128 * hd:128 * hd + 128]
            nc.gpsimd.tensor_tensor(vex[:], values.unsqueeze(1).broadcast_to([64, NSEQ, 128]),
                                    bmask[:].unsqueeze(2).broadcast_to([64, NSEQ, 128]), ALU.mult).then_inc(vex_ready, 1)

        layer_params(0)
        pool.dma_start(rw[:], A["router_w"][0].rearrange("(k p) e -> p k e", p=128)).then_inc(router_in, 16)
        pool.wait_ge(consts_ready, 1)
        for L in range(LAYERS):
            pool.wait_ge(layer_in, 64 * (L + 1))
            for j, (_, sz) in enumerate(TOK):
                pool.wait_ge(vn_scaled, NT * L + j + 1)
                link(nc.gpsimd.tensor_tensor(vn[0:sz, j, :], vn[0:sz, j, :], lng[0:sz], ALU.mult))
                nc.gpsimd.tensor_tensor(vn[0:sz, j, :], vn[0:sz, j, :], lnb[0:sz], ALU.add).then_inc(vn_ready, 1)
            pool.wait_ge(vn_ready, NT * (L + 1))
            pool.dma_start(OUT["v_rows"][L].rearrange("b j c -> (b j) c"), vn[0:64, PAIRS, :]).then_inc(vrow_out, 16)
            pool.wait_ge(lev_diff, NLEV * (L + 1))
            load_s0(L, 0)
            pool.wait_ge(lev_prod, NLEV * (L + 1))
            pool.wait_ge(score_psum, score_count(L, 1))
            pool.wait_ge(act_emptied, tile[(L, "value", NT - 1)][3])
            spread_values(L, 0)
            pool.wait_ge(mix_psum, H * (L + 1))
            pool.wait_ge(vrow_out, 16 * (L + 1))
            load_s0(L, 1)
            pool.wait_ge(state_ready, NPC * (L + 1))
            pool.dma_start(OUT["prompt_state"][L, 0].rearrange("h p v -> p h v"), S34[:, 1]).then_inc(pstate_out, 16)
            pool.wait_ge(o_psum, H * (L + 1))
            load_s0(L, 2)
            load_s0(L, 3)
            for hd in range(H):
                if hd + 1 < H:
                    pool.wait_ge(su_psum, H * L + hd + 1)
                    spread_values(L, hd + 1)
                pool.wait_ge(s0_ready, H * L + hd + 1)
                pool.dma_start(OUT["sample_state"][L, :, hd].rearrange("b p v -> p b v"), s0[hd][:]).then_inc(
                    s0_out[hd], 16)
            if L + 1 < LAYERS:
                pool.wait_ge(a_ready, H * (L + 1))
                layer_params(L + 1)
        for q in s0_out:
            pool.wait_ge(q, 16 * LAYERS)
        pool.wait_ge(vrow_out, 16 * LAYERS)
        pool.wait_ge(pstate_out, 16 * LAYERS)
        pool.dma_start(gfin[:], A["final_norm_g"].partition_broadcast(128)).then_inc(gfin_in, 16)

    @block.scalar
    def _(act):
        links = [0]
        fn = nc.scalar.activation

        def link(ins):
            links[0] += 1
            ins.then_inc(act_link, 1)
            act.wait_ge(act_link, links[0])

        def split_high(c, half):
            n = piece_width(c)
            p = 2 * c + half
            act.wait_ge(raw_full[p % RING], 16 * (p // RING + 1))
            if p >= RING:
                act.wait_ge(pe_mark, mark_after[p - RING])
            fn(whi[:, p % RING, 0:n], raw[:, p % RING, 0:n], ACT.Copy).then_inc(high_done, 1)

        def square(n, j):
            if n == 0:
                act.wait_ge(h_ready, j + 1)
            else:
                L, sec = (n - 1) // 2, ("w_out", "down")[(n - 1) % 2]
                act.wait_ge(dve_emptied, tile[(L, sec, j)][3])
            if 8 * n + j >= 2:
                act.wait_ge(summed, KD * n + j - 1)
            fn(sq[:, j % 2, :], h[:, j, :], ACT.Square).then_inc(squared, 1)

        def norm(n, parts=True):
            act.wait_ge(stat_psum, n + 1)
            if n:
                act.wait_ge(xn_ready, KD * n)
            fn(rcol[:], bank[4][:, 0:NT], ACT.Sqrt, bias=eps_t[:], scale=1.0 / D).then_inc(root_ready, 1)
            if parts:
                for j in range(KD):
                    act.wait_ge(xn_ready, KD * n + j + 1)
                    fn(xh[:, j, :], xn[:, j, :], ACT.Copy).then_inc(xh_ready, 1)

        def empties(L, sec, j, out, f, psz=128, cols=T, scale=1.0):
            b, mark = tile[(L, sec, j)][0:2]
            act.wait_ge(pe_mark, mark)
            fn(out, bank[b][0:psz, 0:cols], f, scale=scale).then_inc(act_emptied, 1)

        nc.scalar.preload_act_table(ACT.Sqrt)
        act.wait_ge(first_ready, 3)
        for j in range(KD):
            square(0, j)
        split_high(0, 0)
        split_high(0, 1)
        norm(0)
        for c in range(1, AHEAD):
            split_high(c, 0)
            split_high(c, 1)
        act.wait_ge(lb_ready, 1)
        link(fn(lbt[:, 3], lbt[:, 0], ACT.Abs))
        link(fn(lbt[:, 3], lbt[:, 3], ACT.Exp, scale=-1.0))
        fn(lbt[:, 4], lbt[:, 3], ACT.Ln, bias=1.0).then_inc(lb_exp, 1)

        for L in range(LAYERS):
            if L:
                norm(2 * L)
            for i, (sec, part) in enumerate(MIX):
                c = base(L) + i
                split_high(c + AHEAD, 0)
                if SAMPLE_AT < i <= SAMPLE_AT + H:
                    hd = i - SAMPLE_AT - 1
                    act.wait_ge(s0_ready, H * L + hd + 1)
                    if hd >= 2:
                        act.wait_ge(ostat_psum, H * L + hd - 1)
                    fn(sq[:, hd % 2, :], Q[:, hd], ACT.Square).then_inc(osq_ready, 1)
                if i == B_AT:
                    for hd in range(H):
                        act.wait_ge(b_ready, H * L + hd + 1)
                        fn(bhi[:, hd], Q[:, hd], ACT.Copy).then_inc(b_high, 1)
                if sec == "forget":
                    for j in (2 * part, 2 * part + 1):
                        empties(L, sec, j, G[:, j, :], ACT.Copy)
                elif sec == "q":
                    for j in (2 * part, 2 * part + 1):
                        empties(L, sec, j, Q[:, j, :], ACT.Silu)
                elif sec == "value" and part == 1:
                    for j, (_, sz) in enumerate(TOK):
                        empties(L, sec, j, V[0:sz, j, :], ACT.Copy, sz, DA)
                elif sec == "v" and part == 1:
                    if L:
                        act.wait_ge(vrow_out, 16 * L)
                        act.wait_ge(s0_out[1], 16 * L)
                    for j, (_, sz) in enumerate(TOK):
                        empties(L, sec, j, vn[0:sz, j, :], ACT.Gelu, sz, DA)
                elif sec == "u":
                    for j in (2 * part, 2 * part + 1):
                        empties(L, sec, j, u[:, j, :], ACT.Gelu)
                elif sec == "gate_a":
                    for j in (2 * part, 2 * part + 1):
                        empties(L, sec, j, xn[:, j, :], ACT.Tanh, scale=0.5)
                elif sec == "out_gate":
                    if part == 0:
                        act.wait_ge(a_ready, H * (L + 1))
                    for j in (2 * part, 2 * part + 1):
                        empties(L, sec, j, u[:, j, :], ACT.Silu)
                elif sec == "gate_b":
                    for j in (2 * part, 2 * part + 1):
                        empties(L, sec, j, gb[:, j, :], ACT.Tanh, scale=0.5)
                if i == DECAYS_AT:
                    act.wait_ge(cum_ready, H * (L + 1))
                    act.wait_ge(key_ready, L + 1)
                    fn(E[:], G[:], ACT.Exp).then_inc(expg_ready, 1)
                    act.wait_ge(gap_ready, L + 1)
                    fn(Z[:], Z[:], ACT.Exp).then_inc(gap_exp, 1)
                if i == LN_AT:
                    for j, (_, sz) in enumerate(TOK):
                        act.wait_ge(var_ready, NT * L + j + 1)
                        fn(bag[0:sz, j, 1:2], bag[0:sz, j, 1:2], ACT.Sqrt, bias=eps_t[0:sz]).then_inc(dev_ready, 1)
                if sec == "w_out":
                    for j in (2 * part, 2 * part + 1):
                        square(2 * L + 1, j)
                split_high(c + AHEAD, 1)
                if i == GATES_AT:
                    act.wait_ge(act_emptied, tile[(L, "forget", H - 1)][3])
                    if L:
                        act.wait_ge(b_low, H * L)
                        act.wait_ge(pstate_out, 16 * L)
                        for q in s0_out:
                            act.wait_ge(q, 16 * L)
                    link(fn(Z[:], G[:], ACT.Abs))
                    link(fn(Z[:], Z[:], ACT.Exp, scale=-1.0))
                    fn(E[:], Z[:], ACT.Ln, bias=1.0).then_inc(softplus_a, 1)
                if i == KEYS_AT:
                    act.wait_ge(logsig_ready, L + 1)
                    if L == 0:
                        fn(K[:], E[:], ACT.Exp).then_inc(key_ready, 1)
                    else:
                        act.wait_ge(lb_ready, 2)
                        for j in range(H):
                            ins = fn(K[:, j], E[:, j], ACT.Exp, bias=lbt[:, 2, j:j + 1])
                        ins.then_inc(key_ready, 1)
                        act.wait_ge(bound_arg, L)
                        link(fn(QE[:], Z[:], ACT.Abs))
                        link(fn(QE[:], QE[:], ACT.Exp, scale=-1.0))
                        fn(QE[:], QE[:], ACT.Ln, bias=1.0).then_inc(softplus_b, 1)
                if i == TURN_AT:
                    for j, (_, sz) in enumerate(TOK):
                        act.wait_ge(kdt_psum, NT * L + j + 1)
                        fn(kdt[0:sz, j, :], bank[4 + j][0:sz, :], ACT.Copy).then_inc(kdt_ready, 1)
                if SCORES_AT <= i + 1 < SCORES_AT + NLEV:
                    li = i + 1 - SCORES_AT
                    n = tokens_of(LEVELS[li])
                    act.wait_ge(lev_diff, NLEV * L + li + 1)
                    fn(E[:, :, 0:n], E[:, :, 0:n], ACT.Exp).then_inc(lev_exp, 1)
                if MIX_AT <= i < MIX_AT + H:
                    g = i - MIX_AT
                    act.wait_ge(a_ready, H * L + g + 1)
                    fn(ahi[:, g], u[:, g], ACT.Copy).then_inc(a_high, 1)
                if i == OUT_AT:
                    for hd in range(H):
                        act.wait_ge(o_psum, H * L + hd + 1)
                        fn(Q[:, hd, :], bank[4 + hd][:, 0:T], ACT.Copy).then_inc(o_ready, 1)
                if i == ONORM_AT:
                    act.wait_ge(ostat_psum, H * (L + 1))
                    sums = bank[7][:, 0:H * NT].rearrange("p (h t) -> p h t", t=NT)
                    fn(orc[:], sums, ACT.Sqrt, bias=eps_t[:], scale=1.0 / 128).then_inc(oroot_ready, 1)
                if sec == "branch_b":
                    for j in range(4 * part, 4 * part + 4):
                        act.wait_ge(merged_ready, KD * L + j + 1)
                        fn(xh[:, j, :], xn[:, j, :], ACT.Copy, scale=0.5).then_inc(merged_high, 1)
            if L % 2 == 0:
                norm(2 * L + 1)
                act.wait_ge(pstate_out, 16 * (L + 1))
                act.wait_ge(vrow_out, 16 * (L + 1))
                for q in s0_out:
                    act.wait_ge(q, 16 * (L + 1))
                for i, (sec, part) in enumerate(FFN):
                    c = first_chunk[(L, "gate")] + i
                    split_high(c + AHEAD, 0)
                    if sec == "gate":
                        if part:
                            act.wait_ge(dve_emptied, tile[(L, "up", 2 * part - 1)][3])
                        for j in (0, 1):
                            empties(L, sec, 2 * part + j, sg[:, j, :], ACT.Silu)
                    if sec == "down" and part % 3 == 2:
                        for j in (0, 1):
                            square(2 * L + 2, 2 * (part // 3) + j)
                    split_high(c + AHEAD, 1)
                    if sec == "up":
                        for j in (0, 1):
                            act.wait_ge(dve_emptied, tile[(L, "up", 2 * part + j)][3])
                            fn(fh[:, 2 * part + j, :], hf[:, j, :], ACT.Copy).then_inc(hid_high, 1)

        norm(2 * LAYERS - 1, parts=False)
        act.wait_ge(pstate_out, 16 * LAYERS)
        act.wait_ge(vrow_out, 16 * LAYERS)
        for q in s0_out:
            act.wait_ge(q, 16 * LAYERS)
        for n, (t, hf_) in enumerate(OUTS):
            act.wait_ge(sum_psum, n + 1)
            fn(acc[0:TOK[t][1], t, 512 * hf_:512 * hf_ + 512], bank[ROW_BANK[n]][0:TOK[t][1], :], ACT.Copy).then_inc(
                sum_done, 1)
        act.wait_ge(lgt_psum, 1)
        fn(lgt[:], bank[7][0:NE, 0:T], ACT.Copy).then_inc(lgt_ready, 1)
        for n, (t, hf_) in enumerate(OUTS):
            act.wait_ge(hn_psum, n + 1)
            fn(hn[0:TOK[t][1], t, 512 * hf_:512 * hf_ + 512], bank[ROW_BANK[n]][0:TOK[t][1], :], ACT.Copy).then_inc(
                y_ready, 1)
        act.wait_ge(top_ready, 1)
        fn(g1[:, 0], g1[:, 0], ACT.Exp).then_inc(gap_top, 1)

        def expert_in_high(item):
            for hh in range(2):
                act.wait_ge(xg_psum, 2 * item + hh + 1)
                fn(xeh[:, 4 * hh:4 * hh + 4, :], bank[6 + hh][:], ACT.Copy).then_inc(xg_high, 1)

        def hidden_high(item, j):
            ts = group_tiles(j)
            act.wait_ge(het_psum, NG * item + j + 1)
            fn(heh[:, ts[0]:ts[-1] + 1, :], bank[4 + j % 2][:, 0:128 * len(ts)], ACT.Copy).then_inc(heh_ready, 1)

        def high_of(item, i, half):
            n = piece_width(NDENSE + i % NEC)
            p = 2 * i + half
            act.wait_ge(raw_full[p % RING], 16 * (2 * NEC // RING) * item + 16 * (2 * NDENSE // RING + p // RING + 1))
            act.wait_ge(pe_mark, 2 * NEC * item + (MB + p - RING + 1))
            fn(whi[:, p % RING, 0:n], raw[:, p % RING, 0:n], ACT.Copy).then_inc(high_done, 1)

        def chunk(item, i, last, ahead):
            if i + AHEAD < last:
                high_of(item, i + AHEAD, 0)
            if i >= NEC:
                item, i, last = item + 1, i - NEC, last - NEC
            kind, j, cols = ECH[i][0], ECH[i][1], ECH[i][6]
            closed = i == closing.get((kind, j))
            if kind == "gate" and closed:
                act.wait_ge(pe_mark, 2 * NEC * item + (MB + 2 * i + 2))
                if j >= 2:
                    act.wait_ge(he_ready, NG * item + (j - 1))
                fn(sge[:, j % 2, 0:cols], bank[2 * (j % 2)][:, 0:cols], ACT.Silu).then_inc(gate_emptied, 1)
            if i + AHEAD < last:
                high_of(item, i + AHEAD, 1)
            if kind == "up" and closed:
                if j == 1:
                    act.wait_ge(pickt_psum, item + 1)
                    act.wait_ge(sum_psum, NO * item + NO)
                    fn(pickt[:], bank[5][:, 0:T], ACT.Copy).then_inc(pickt_ready, 1)
                if j:
                    hidden_high(item, j - 1)
                if j == NG - 1:
                    if ahead:
                        expert_in_high(item + 1)
                    hidden_high(item, j)
            if i == NEC - 1:
                act.wait_ge(pe_mark, 2 * NEC * item + (MB + 2 * NEC))
                act.wait_ge(sum_psum, NO * item + NO)
                for hh in range(2):
                    fn(Yh[:, 512 * hh:512 * hh + 512], bank[down_bank(ahead) + hh][:], ACT.Copy).then_inc(y_ready, 1)

        def extra(item, n):
            for i in range(AHEAD):
                for half in range(2):
                    high_of(item, i, half)
            expert_in_high(item)
            for i in range(NEC):
                chunk(item, i, NEC, False)

        expert_in_high(0)
        for i in range(HEAD):
            chunk(0, i, 2 * NEC, True)
        with act.Fori(0, NE - 1) as e:
            for i in range(HEAD, HEAD + NEC):
                chunk(e, i, 2 * NEC, True)
        for i in range(HEAD, NEC):
            chunk(NE - 1, i, NEC, False)
        extra_blocks(act, extra)
        for t, (_, sz) in enumerate(TOK):
            act.wait_ge(fsq_ready, t + 1)
            fn(rf[0:sz, t:t + 1], ssf[0:sz, t:t + 1], ACT.Sqrt, bias=eps_t[0:sz], scale=1.0 / D).then_inc(froot_ready, 1)

    @block.vector
    def _(dve):
        links = [0]
        v = nc.vector

        def link(ins):
            links[0] += 1
            ins.then_inc(dve_link, 1)
            dve.wait_ge(dve_link, links[0])

        def split_low(c, half):
            n = piece_width(c)
            p = 2 * c + half
            dve.wait_ge(high_done, p + 1)
            v.tensor_tensor(wlo[:, p % RING, 0:n], raw[:, p % RING, 0:n],
                            whi[:, p % RING, 0:n].bitcast(F), ALU.subtract).then_inc(low_done, 1)

        def add_square(n, j):
            dve.wait_ge(squared, KD * n + j + 1)
            if j == 0:
                if n:
                    dve.wait_ge(stat_psum, n)
                v.tensor_copy(ssum[:], sq[:, 0, :]).then_inc(summed, 1)
            else:
                dve.wait_ge(summed, KD * n + j)
                v.tensor_tensor(ssum[:], ssum[:], sq[:, j % 2, :], ALU.add).then_inc(summed, 1)

        def norm(n, parts=True):
            col = (P_FFN if n % 2 else P_MIX) + KD * (n // 2)
            dve.wait_ge(root_ready, n + 1)
            v.reciprocal(rcol[:], rcol[:]).then_inc(rinv_ready, 1)
            dve.wait_ge(spread_psum, n + 1)
            for j in range(KD + 1):
                if j < KD:
                    v.scalar_tensor_tensor(out=xn[:, j, :], in0=h[:, j, :], scalar=prm[:, col + j:col + j + 1],
                                           in1=bank[4][:, 0:T], op0=ALU.mult, op1=ALU.mult).then_inc(xn_ready, 1)
                if j and parts:
                    dve.wait_ge(xh_ready, KD * n + j)
                    v.tensor_tensor(xl[:, j - 1, :], xn[:, j - 1, :], xh[:, j - 1, :].bitcast(F),
                                    ALU.subtract).then_inc(xl_ready, 1)

        def waits_tile(L, sec, j):
            b, mark, _, _, _ = tile[(L, sec, j)]
            dve.wait_ge(pe_mark, mark)
            return bank[b]

        def add_residual(L, sec, j):
            b = waits_tile(L, sec, j)
            v.tensor_tensor(h[:, j, :], h[:, j, :], b[:, 0:T], ALU.add).then_inc(dve_emptied, 1)

        dve.wait_ge(prm_psum, 1)
        v.tensor_copy(prm[:], bank[7][:, 0:NROW]).then_inc(prm_ready, 1)
        for j in range(KD):
            dve.wait_ge(xt_psum, j + 1)
            v.tensor_copy(h[:, j, :], bank[j % 4][:, 0:T]).then_inc(h_ready, 1)
            if j:
                add_square(0, j - 1)
        add_square(0, KD - 1)
        split_low(0, 0)
        split_low(0, 1)
        dve.wait_ge(prm_ready, 1)
        v.tensor_tensor(lbt[:, 0], prm[:, P_LB + H:P_LB + 2 * H], prm[:, P_LB:P_LB + H], ALU.subtract).then_inc(lb_ready, 1)
        norm(0)
        for c in range(1, AHEAD):
            split_low(c, 0)
            split_low(c, 1)
        dve.wait_ge(lb_exp, 1)
        dve.wait_ge(lb_ready, 1)
        link(v.scalar_tensor_tensor(out=lbt[:, 1], in0=lbt[:, 0], scalar=0.0, in1=lbt[:, 4], op0=ALU.min,
                                    op1=ALU.subtract))
        v.tensor_tensor(lbt[:, 2], lbt[:, 1], lbt[:, 0], ALU.subtract).then_inc(lb_ready, 1)

        for L in range(LAYERS):
            if L:
                norm(2 * L)

            def b_low_part(hd, L=L):
                dve.wait_ge(b_high, H * L + hd + 1)
                v.tensor_tensor(blo[:, hd], Q[:, hd], bhi[:, hd].bitcast(F), ALU.subtract).then_inc(b_low, 1)

            def merged_low_part(j, L=L):
                dve.wait_ge(merged_high, KD * L + j + 1)
                v.scalar_tensor_tensor(out=xl[:, j, :], in0=xn[:, j, :], scalar=0.5, in1=xh[:, j, :].bitcast(F),
                                       op0=ALU.mult, op1=ALU.subtract).then_inc(merged_low, 1)

            for i, (sec, part) in enumerate(MIX):
                c = base(L) + i
                split_low(c + AHEAD, 0)
                if sec == "branch_a":
                    for j in range(4 * part, 4 * part + 4):
                        b = waits_tile(L, sec, j)
                        dve.wait_ge(act_emptied, tile[(L, "gate_a", j)][3])
                        v.scalar_tensor_tensor(out=xn[:, j, :], in0=xn[:, j, :], scalar=1.0, in1=b[:, 0:T], op0=ALU.add,
                                               op1=ALU.mult).then_inc(dve_emptied, 1)
                if sec == "branch_b":
                    for j in range(4 * part, 4 * part + 4):
                        b = waits_tile(L, sec, j)
                        dve.wait_ge(act_emptied, tile[(L, "gate_b", j)][3])
                        v.scalar_tensor_tensor(out=tmp[:, j % 2, :], in0=gb[:, j, :], scalar=1.0, in1=b[:, 0:T], op0=ALU.add,
                                               op1=ALU.mult).then_inc(dve_emptied, 1)
                        dve.wait_ge(dve_emptied, tile[(L, sec, j)][3])
                        v.tensor_tensor(xn[:, j, :], xn[:, j, :], tmp[:, j % 2, :], ALU.add).then_inc(merged_ready, 1)
                        if j:
                            merged_low_part(j - 1)
                    if part == 1:
                        merged_low_part(KD - 1)
                if sec == "w_out":
                    for j in (2 * part, 2 * part + 1):
                        add_residual(L, sec, j)
                if i == KEYS_AT:
                    dve.wait_ge(softplus_a, L + 1)
                    link(v.scalar_tensor_tensor(out=Z[:], in0=G[:], scalar=0.0, in1=E[:], op0=ALU.min, op1=ALU.subtract))
                    v.tensor_tensor(E[:], Z[:], G[:], ALU.subtract).then_inc(logsig_ready, 1)
                    dve.wait_ge(logsig_ready, L + 1)
                    if L:
                        for j in range(H):
                            ins = v.tensor_scalar(Z[:, j], Z[:, j], lbt[:, 0, j:j + 1], None, ALU.subtract)
                        ins.then_inc(bound_arg, 1)
                if i == SUMS_AT:
                    dve.wait_ge(logsig_ready, L + 1)
                    if L:
                        dve.wait_ge(softplus_b, L)
                        dve.wait_ge(bound_arg, L)
                        link(v.scalar_tensor_tensor(out=Z[:], in0=Z[:], scalar=0.0, in1=QE[:], op0=ALU.max, op1=ALU.add))
                        for j in range(H):
                            link(v.tensor_scalar(Z[:, j], Z[:, j], lbt[:, 1, j:j + 1], None, ALU.add))
                    for j in range(H):
                        v.tensor_tensor_scan(G[:, j], smask[:], Z[:, j], 0.0, ALU.mult, ALU.add).then_inc(cum_ready, 1)
                if i == DECAYS_AT:
                    dve.wait_ge(cum_ready, H * (L + 1))
                    link(v.tensor_tensor(Z[:, :, 0:TP].rearrange("p h (c t) -> p h c t", t=CH),
                                         G[:, :, CH - 1:TP:CH].unsqueeze(3).broadcast_to([128, H, NPC, CH]),
                                         G[:, :, 0:TP].rearrange("p h (c t) -> p h c t", t=CH), ALU.subtract))
                    v.tensor_tensor(Z[:, :, TP:T].rearrange("p h (c t) -> p h c t", t=LS),
                                    G[:, :, TP + LS - 1:T:LS].unsqueeze(3).broadcast_to([128, H, NSEQ, LS]),
                                    G[:, :, TP:T].rearrange("p h (c t) -> p h c t", t=LS),
                                    ALU.subtract).then_inc(gap_ready, 1)
                    dve.wait_ge(expg_ready, L + 1)
                    link(v.tensor_copy(el[:, :, 0:NPC], E[:, :, CH - 1:TP:CH]))
                    link(v.tensor_copy(el[:, :, NPC:], E[:, :, TP + LS - 1:T:LS]))
                    dve.wait_ge(act_emptied, tile[(L, "q", H - 1)][3])
                    v.tensor_tensor(QE[:], Q[:], E[:], ALU.mult).then_inc(qdec_ready, 1)
                    dve.wait_ge(gap_exp, L + 1)
                    dve.wait_ge(key_ready, L + 1)
                    v.tensor_tensor(Z[:], Z[:], K[:], ALU.mult).then_inc(kdec_ready, 1)
                    if L:
                        dve.wait_ge(s0_out[3], 16 * L)
                    link(v.memset(sc[:], 0.0))
                    link(v.memset(scs[:], 0.0))
                if i == LN_AT:
                    for j, (_, sz) in enumerate(TOK):
                        dve.wait_ge(act_emptied, tile[(L, "v", j)][3])
                        link(v.bn_stats(bst[0:sz, j, :], vn[0:sz, j, :]))
                        v.bn_aggr(bag[0:sz, j, :], bst[0:sz, j, :]).then_inc(var_ready, 1)
                    for j, (_, sz) in enumerate(TOK):
                        dve.wait_ge(dev_ready, NT * L + j + 1)
                        link(v.reciprocal(bag[0:sz, j, 1:2], bag[0:sz, j, 1:2]))
                        v.tensor_scalar(vn[0:sz, j, :], vn[0:sz, j, :], bag[0:sz, j, 0:1], bag[0:sz, j, 1:2],
                                        ALU.subtract, ALU.mult).then_inc(vn_scaled, 1)
                if i == B_AT:
                    dve.wait_ge(s0_out[0], 16 * (L + 1))
                    for hd in range(H):
                        dve.wait_ge(ospread_psum, H * L + hd + 1)
                        link(v.tensor_tensor(Q[:, hd], Q[:, hd], bank[4 + hd][:, 0:T], ALU.mult))
                        dve.wait_ge(act_emptied, tile[(L, "out_gate", hd)][3])
                        v.scalar_tensor_tensor(out=Q[:, hd], in0=Q[:, hd],
                                               scalar=prm[:, P_HG + H * L + hd:P_HG + H * L + hd + 1],
                                               in1=u[:, hd], op0=ALU.mult, op1=ALU.mult).then_inc(b_ready, 1)
                        if hd:
                            b_low_part(hd - 1)
                    b_low_part(H - 1)
                if sec == "w_out":
                    for j in (2 * part, 2 * part + 1):
                        add_square(2 * L + 1, j)
                split_low(c + AHEAD, 1)
                if i == 0:
                    dve.wait_ge(wst_psum, L + 1)
                    dve.wait_ge(consts_ready, 1)
                    v.tensor_tensor(wst[:], bank[7][:].rearrange("p (g t) -> p g t", g=H),
                                    upper[:].unsqueeze(1).broadcast_to([128, H, 128]), ALU.mult).then_inc(wst_ready, 1)
                if i == 1:
                    dve.wait_ge(wsd_psum, L + 1)
                    for g in range(H):
                        ins = v.tensor_tensor(wsd[:, g].rearrange("p (b t) -> p b t", t=LS),
                                              bank[7][0:64, 64 * g:64 * g + 64].rearrange("p (b t) -> p b t", t=LS),
                                              bmask[:].unsqueeze(2).broadcast_to([64, NSEQ, LS]), ALU.mult)
                        ins.then_inc(wsd_ready, 1)
                if SCORES_AT <= i < SCORES_AT + NLEV:
                    li = i - SCORES_AT
                    n = tokens_of(LEVELS[li])
                    ea, eb, _ = halves(E, LEVELS[li], n)
                    za, zb, _ = halves(Z, LEVELS[li], n)
                    ka, _, _ = halves(K, LEVELS[li], n)
                    _, qb, _ = halves(Q, LEVELS[li], n)
                    dve.wait_ge(lev_exp, NLEV * L + li + 1)
                    if li == 0:
                        dve.wait_ge(kdt_psum, NT * (L + 1))
                    else:
                        dve.wait_ge(score_psum, score_count(L, li + 1))
                    v.tensor_tensor(za, ka, ea, ALU.mult)
                    v.tensor_tensor(zb, qb, eb, ALU.mult).then_inc(lev_prod, 1)
                if SCORES_AT <= i + 1 < SCORES_AT + NLEV:
                    li = i + 1 - SCORES_AT
                    n = tokens_of(LEVELS[li])
                    ga, gb2, ref = halves(G, LEVELS[li], n)
                    ea, eb, _ = halves(E, LEVELS[li], n)
                    if li == 0:
                        dve.wait_ge(qdec_ready, L + 1)
                    else:
                        dve.wait_ge(lev_prod, NLEV * L + li)
                    v.tensor_tensor(ea, ref, ga, ALU.subtract)
                    v.tensor_tensor(eb, gb2, ref, ALU.subtract).then_inc(lev_diff, 1)
                if i == DIAGONAL_AT or SCORES_AT < i <= SCORES_AT + NLEV:
                    li = max(0, i - SCORES_AT)
                    k = score_count(L, li)
                    lv = ([0] + LEVELS)[li]
                    for p in range(SCORES if lv <= LS // 2 else PAIRS):
                        dve.wait_ge(score_psum, k + p + 1)
                        if li:
                            dve.wait_ge(score_ready, score_count(L, li))
                        if p < PAIRS:
                            v.copy_predicated(sc[:, p], lmask[:, li, :].unsqueeze(1).broadcast_to([128, H, 128]),
                                              bank[4 + p][:].rearrange("p (h t) -> p h t", h=H)).then_inc(score_ready, 1)
                        else:
                            v.copy_predicated(scs[:], lmask[0:64, li, 0:64].unsqueeze(1).broadcast_to([64, H, 64]),
                                              bank[6][0:64, 0:64 * H].rearrange("p (h t) -> p h t", h=H)).then_inc(
                                                  score_ready, 1)
                if MIX_AT <= i < MIX_AT + H:
                    g = i - MIX_AT
                    dve.wait_ge(mix_psum, H * L + g + 1)
                    dve.wait_ge(act_emptied, tile[(L, "u", H - 1)][3])
                    b = bank[7]
                    t1 = tmp[:, g % 2, :]
                    link(v.tensor_tensor(t1[:, 0:TP].rearrange("p (c t) -> p c t", t=128),
                                         b[:, 0:TP].rearrange("p (c t) -> p c t", t=128),
                                         bsp[:, g].unsqueeze(1).broadcast_to([128, PAIRS, 128]), ALU.add))
                    link(v.tensor_tensor(t1[:, TP:T].rearrange("p (c t) -> p c t", t=LS),
                                         b[:, TP:T].rearrange("p (c t) -> p c t", t=LS),
                                         bsp[:, g, 0:LS].unsqueeze(1).broadcast_to([128, NSEQ, LS]), ALU.add))
                    v.tensor_tensor(u[:, g], u[:, g], t1, ALU.mult).then_inc(a_ready, 1)
                    dve.wait_ge(a_high, H * L + g + 1)
                    v.tensor_tensor(alo[:, g], u[:, g], ahi[:, g].bitcast(F), ALU.subtract).then_inc(a_low, 1)
                if i == STATES_AT:
                    for n in range(NPC):
                        dve.wait_ge(upd_psum, NPC * L + n + 1)
                        dst = (S12 if n < 2 else S34)[:, n % 2]
                        if n == 0:
                            v.tensor_copy(dst, bank[4][:].rearrange("p (h v) -> p h v", h=H)).then_inc(state_ready, 1)
                            continue
                        dve.wait_ge(state_ready, NPC * L + n)
                        src = (S12 if n - 1 < 2 else S34)[:, (n - 1) % 2]
                        for hd in range(H):
                            ins = v.scalar_tensor_tensor(out=dst[:, hd], in0=src[:, hd], scalar=el[:, hd, n:n + 1],
                                                         in1=bank[4 + n][:, 128 * hd:128 * hd + 128],
                                                         op0=ALU.mult, op1=ALU.add)
                        ins.then_inc(state_ready, 1)
                if SAMPLE_AT <= i < SAMPLE_AT + H:
                    hd = i - SAMPLE_AT
                    dve.wait_ge(so_psum, H * L + hd + 1)
                    dve.wait_ge(o_ready, H * L + hd + 1)
                    link(v.tensor_tensor(Q[:, hd, TP:T], Q[:, hd, TP:T], bank[6][:, 0:64], ALU.add))
                    dve.wait_ge(su_psum, H * L + hd + 1)
                    st = s0[hd]
                    for b in range(NSEQ):
                        ins = v.scalar_tensor_tensor(out=st[:, b], in0=st[:, b], scalar=el[:, hd, NPC + b:NPC + b + 1],
                                                     in1=bank[4 + b // 4][:, 128 * (b % 4):128 * (b % 4) + 128],
                                                     op0=ALU.mult, op1=ALU.add)
                    ins.then_inc(s0_ready, 1)
                if i == ONORM_AT:
                    dve.wait_ge(oroot_ready, L + 1)
                    v.reciprocal(orc[:], orc[:]).then_inc(orinv_ready, 1)
            if L % 2 == 0:
                norm(2 * L + 1)
                for i, (sec, part) in enumerate(FFN):
                    c = first_chunk[(L, "gate")] + i
                    split_low(c + AHEAD, 0)
                    if sec == "up":
                        for j in (0, 1):
                            b = waits_tile(L, sec, 2 * part + j)
                            dve.wait_ge(act_emptied, tile[(L, "gate", 2 * part + j)][3])
                            if part:
                                dve.wait_ge(hid_low, 2 * part)
                            v.tensor_tensor(hf[:, j, :], b[:, 0:T], sg[:, j, :], ALU.mult).then_inc(dve_emptied, 1)
                    if sec == "down" and part % 3 == 2:
                        for j in (0, 1):
                            add_residual(L, sec, 2 * (part // 3) + j)
                        for j in (0, 1):
                            add_square(2 * L + 2, 2 * (part // 3) + j)
                    split_low(c + AHEAD, 1)
                    if sec == "up":
                        for j in (0, 1):
                            dve.wait_ge(hid_high, 2 * part + j + 1)
                            v.tensor_tensor(fl[:, 2 * part + j, :], hf[:, j, :], fh[:, 2 * part + j, :].bitcast(F),
                                            ALU.subtract).then_inc(hid_low, 1)

        norm(2 * LAYERS - 1, parts=False)
        link(v.memset(lg[:], 0.0))
        dve.wait_ge(logit_psum, 1)
        link(v.tensor_copy(lg[:, 0:PAIRS], bank[7][:, 0:PAIRS * NE].rearrange("p (t e) -> p t e", e=NE)))
        v.tensor_copy(lg[0:64, PAIRS], bank[7][0:64, PAIRS * NE:NT * NE]).then_inc(lg_ready, 1)
        dve.wait_ge(lg_ready, 1)
        for t in range(NT):
            ins = v.max(top[:, t], lg[:, t])
        link(ins)
        for t in range(NT):
            ins = v.max_index(topi[:, t], top[:, t], lg[:, t])
        link(ins)
        link(v.tensor_copy(topf[:], topi[:]))
        v.tensor_tensor(g1[:, 0], top[:, :, 1], top[:, :, 0], ALU.subtract).then_inc(top_ready, 1)
        row = iota[:, 0:NE].unsqueeze(1).broadcast_to([128, NT, NE])
        link(v.tensor_tensor(m1[:], row, topf[:, :, 0:1].broadcast_to([128, NT, NE]), ALU.is_equal))
        link(v.tensor_tensor(m2[:], row, topf[:, :, 1:2].broadcast_to([128, NT, NE]), ALU.is_equal))
        v.tensor_tensor(mk[:], m1[:], m2[:], ALU.add).then_inc(chosen_ready, 1)
        link(v.memset(slot[:], -1.0))
        dve.wait_ge(rank_psum, 1)
        dve.wait_ge(chosen_ready, 1)
        link(v.tensor_tensor(slot[:, 0:PAIRS], bank[7][:, 0:PAIRS * NE].rearrange("p (t e) -> p t e", e=NE),
                             mk[:, 0:PAIRS], ALU.mult))
        link(v.tensor_tensor(slot[0:64, PAIRS], bank[7][0:64, PAIRS * NE:NT * NE], mk[0:64, PAIRS], ALU.mult))
        link(v.tensor_copy(fullf[:, 0, 0:NE], bank[7][:, NT * NE:(NT + 1) * NE]))
        link(v.tensor_scalar(slot[:, 0:PAIRS], slot[:, 0:PAIRS], -1.0, None, ALU.add))
        v.tensor_scalar(slot[0:64, PAIRS], slot[0:64, PAIRS], -1.0, None, ALU.add).then_inc(shift_done, 1)

        def choose(item, e, shifts=1):
            dve.wait_ge(shift_done, shifts)
            v.tensor_copy(cslot[:], slot[:, :, bass.ds(e, 1)]).then_inc(columns_ready, 1)
            dve.wait_ge(columns_ready, item + 1)
            if not isinstance(item, int) or item:
                dve.wait_ge(xg_psum, 2 * item)
                dve.wait_ge(pickt_psum, item)
            for t, (_, sz) in enumerate(TOK):
                ins = v.tensor_scalar(pick[0:sz, t], iota[0:sz], cslot[0:sz, t:t + 1], None, ALU.is_equal)
            ins.then_inc(pick_ready, 1)

        def expert_in_low(item):
            for hh in range(2):
                dve.wait_ge(xg_high, 2 * item + hh + 1)
                v.tensor_tensor(xel[:, 4 * hh:4 * hh + 4, :].rearrange("p k s -> p (k s)"), bank[6 + hh][:],
                                xeh[:, 4 * hh:4 * hh + 4, :].rearrange("p k s -> p (k s)").bitcast(F),
                                ALU.subtract).then_inc(xg_low, 1)

        def hidden_low(item, j):
            ts = group_tiles(j)
            dve.wait_ge(heh_ready, NG * item + j + 1)
            v.tensor_tensor(hel[:, ts[0]:ts[-1] + 1, :].rearrange("p k s -> p (k s)"), bank[4 + j % 2][:, 0:128 * len(ts)],
                            heh[:, ts[0]:ts[-1] + 1, :].rearrange("p k s -> p (k s)").bitcast(F),
                            ALU.subtract).then_inc(hel_ready, 1)

        def low_of(item, i, half):
            n = piece_width(NDENSE + i % NEC)
            p = 2 * i + half
            dve.wait_ge(high_done, 2 * NEC * item + (2 * NDENSE + p + 1))
            v.tensor_tensor(wlo[:, p % RING, 0:n], raw[:, p % RING, 0:n],
                            whi[:, p % RING, 0:n].bitcast(F), ALU.subtract).then_inc(low_done, 1)

        def chunk(item, i, last, ahead, e=None):
            if i + AHEAD < last:
                low_of(item, i + AHEAD, 0)
            if i >= NEC:
                item, i, last = item + 1, i - NEC, last - NEC
            kind, j, c0, cols = ECH[i][0], ECH[i][1], ECH[i][5], ECH[i][6]
            closed = i == closing.get((kind, j))
            if kind == "up" and closed:
                dve.wait_ge(pe_mark, 2 * NEC * item + (MB + 2 * i + 2))
                dve.wait_ge(gate_emptied, NG * item + (j + 1))
                v.tensor_tensor(He[:, c0:c0 + cols], bank[1 + 2 * (j % 2)][:, 0:cols], sge[:, j % 2, 0:cols],
                                ALU.mult).then_inc(he_ready, 1)
            if i + AHEAD < last:
                low_of(item, i + AHEAD, 1)
            if kind == "up" and closed:
                if j:
                    hidden_low(item, j - 1)
                if j == NG - 3 and ahead:
                    choose(item + 1, item + 1)
                if j == NG - 1:
                    if ahead:
                        expert_in_low(item + 1)
                    hidden_low(item, j)
            if i == NEC - 1:
                dve.wait_ge(sum_psum, NO * item + NO)
                for hh in range(2):
                    dve.wait_ge(y_ready, 2 * item + (NO + hh + 1))
                    v.tensor_tensor(Yl[:, 512 * hh:512 * hh + 512], bank[down_bank(ahead) + hh][:],
                                    Yh[:, 512 * hh:512 * hh + 512].bitcast(F), ALU.subtract).then_inc(y_low, 1)

        def add_sums(item, e):
            dve.wait_ge(sum_done, NO * item + NO)
            v.tensor_copy(cgate[:], cmb[:, :, bass.ds(e, 1)]).then_inc(gates_ready, 1)
            dve.wait_ge(gates_ready, item + 1)
            for n, (t, hf_) in enumerate(OUTS):
                sz = TOK[t][1]
                part = acc[0:sz, t, 512 * hf_:512 * hf_ + 512]
                dve.wait_ge(sum_psum, NO * item + (NO + n + 1))
                v.scalar_tensor_tensor(out=part, in0=bank[SUM_BANK[n]][0:sz, :], scalar=cgate[0:sz, t:t + 1], in1=part,
                                       op0=ALU.mult, op1=ALU.add).then_inc(sum_done, 1)

        choose(0, 0)
        dve.wait_ge(gap_top, 1)
        link(v.tensor_scalar(g1[:, 1], g1[:, 0], 1.0, None, ALU.add))
        link(v.reciprocal(g1[:, 2], g1[:, 1]))
        link(v.tensor_tensor(g1[:, 3], g1[:, 0], g1[:, 2], ALU.mult))
        link(v.tensor_tensor(m1[:], m1[:], g1[:, 2].unsqueeze(2).broadcast_to([128, NT, NE]), ALU.mult))
        link(v.tensor_tensor(m2[:], m2[:], g1[:, 3].unsqueeze(2).broadcast_to([128, NT, NE]), ALU.mult))
        link(v.tensor_tensor(cmb[:], m1[:], m2[:], ALU.add))
        expert_in_low(0)
        for n in range(1, BLOCKS - 1):
            link(v.tensor_scalar(fullf[:, 0, NE * n:NE * n + NE], fullf[:, 0, 0:NE], -float(CAP * n), None, ALU.add))
        link(v.tensor_scalar(fullf[:, 1], fullf[:, 0], float(CAP), None, ALU.is_gt))
        link(v.memset(fullf[:, 0], 1.0))
        link(v.tensor_tensor_scan(fullf[:, 2], fullf[:, 0], fullf[:, 1], 0.0, ALU.mult, ALU.add))
        link(v.tensor_tensor(fullf[:, 2], fullf[:, 2], fullf[:, 1], ALU.subtract))
        link(v.tensor_copy(full[:, 0:NMORE], fullf[:, 1]))
        link(v.tensor_copy(items[:], fullf[:, 2]))
        v.tensor_reduce(full[:, NMORE:NMORE + 1], fullf[:, 1], mybir.AxisListType.X, ALU.max).then_inc(table_ready, 1)
        for i in range(HEAD):
            chunk(0, i, 2 * NEC, True)
        with dve.Fori(0, NE - 1) as e:
            for i in range(HEAD, HEAD + NEC):
                chunk(e, i, 2 * NEC, True)
            add_sums(e, e)
        for i in range(HEAD, NEC):
            chunk(NE - 1, i, NEC, False)
        add_sums(NE - 1, NE - 1)

        with dve.If(any_extra(dve)):
            with dve.Fori(1, BLOCKS) as b:
                dve.wait_ge(pick_ready, NE)
                dve.wait_ge(shift_done, b)
                v.tensor_scalar(slot[:], slot[:], -float(CAP), None, ALU.add).then_inc(shift_done, 1)
                with dve.Fori(0, NE) as e:
                    more, item = extra_block(dve, b * NE + e - NE)
                    with dve.If(more):
                        choose(item, e, b + 1)
                        for i in range(AHEAD):
                            for half in range(2):
                                low_of(item, i, half)
                        expert_in_low(item)
                        for i in range(NEC):
                            chunk(item, i, NEC, False)
                        add_sums(item, e)
                        dve.wait_ge(sum_done, NO * item + 2 * NO)
                        v.memset(cgate[:], 0.0)
        dve.wait_ge(sum_done, NO * (NE + 1))
        dve.wait_ge(gfin_in, 16)
        def square_rows(t, sz):
            v.tensor_tensor_reduce(out=He[0:sz, 0:D], in0=acc[0:sz, t], in1=acc[0:sz, t], scale=1.0, scalar=0.0,
                                   op0=ALU.mult, op1=ALU.add, accum_out=ssf[0:sz, t:t + 1]).then_inc(fsq_ready, 1)

        square_rows(0, TOK[0][1])
        for t, (_, sz) in enumerate(TOK):
            if t + 1 < NT:
                dve.wait_ge(fsq_ready, t + 1)
                square_rows(t + 1, TOK[t + 1][1])
            dve.wait_ge(froot_ready, t + 1)
            link(v.reciprocal(rf[0:sz, t:t + 1], rf[0:sz, t:t + 1]))
            v.scalar_tensor_tensor(out=acc[0:sz, t], in0=acc[0:sz, t], scalar=rf[0:sz, t:t + 1], in1=gfin[0:sz],
                                   op0=ALU.mult, op1=ALU.mult).then_inc(fout_ready, 1)

    @block.tensor
    def _(pe):
        mm = nc.tensor.matmul

        def opens(L, sec, t):
            b, _, _, _, prev = tile[(L, sec, t)]
            if prev:
                pe.wait_ge(emptied_sem(tile[prev][2]), tile[prev][3])
            return bank[b]

        def products(L, sec, c, tiles, first, last, mh, ml, k0=0, ready=None, between=None):
            _, kt, cols = chunks[c]
            for half in range(2):
                p = 2 * c + half
                if half and between:
                    between()
                pe.wait_ge(low_done, p + 1)
                for n, t in enumerate(tiles):
                    b = opens(L, sec, t) if first and half == 0 else bank[tile[(L, sec, t)][0]]
                    for q in range(kt // 2):
                        k = half * (kt // 2) + q
                        if ready and n == 0:
                            ready(k)
                        w = slice(q * cols + 128 * n, q * cols + 128 * n + 128)
                        ends = half == 1 and q == kt // 2 - 1
                        mm(b[:, 0:T], whi[:, p % RING, w], mh[:, k0 + k, :], start=first and k == 0, stop=False)
                        mm(b[:, 0:T], whi[:, p % RING, w], ml[:, k0 + k, :], start=False, stop=False)
                        ins = mm(b[:, 0:T], wlo[:, p % RING, w], mh[:, k0 + k, :], start=False, stop=last and ends)
                    if last and half or n == len(tiles) - 1:
                        ins.then_inc(pe_mark, 1)

        def row_products(L, sec, c, part):
            for half in range(2):
                p = 2 * c + half
                pe.wait_ge(low_done, p + 1)
                for t, (t0, sz) in enumerate(TOK):
                    b = opens(L, sec, t) if part == 0 and half == 0 else bank[tile[(L, sec, t)][0]]
                    for q in range(2):
                        w = slice(q * DA, (q + 1) * DA)
                        kk = 4 * part + 2 * half + q
                        mm(b[0:sz, :], xh[:, kk, t0:t0 + sz], whi[:, p % RING, w], start=kk == 0, stop=False)
                        mm(b[0:sz, :], xh[:, kk, t0:t0 + sz], wlo[:, p % RING, w], start=False, stop=False)
                        ins = mm(b[0:sz, :], xl[:, kk, t0:t0 + sz], whi[:, p % RING, w], start=False, stop=kk == KD - 1)
                    if part == 1 and half or t == NT - 1:
                        ins.then_inc(pe_mark, 1)

        def mean_square(n, meanwhile=None):
            pe.wait_ge(summed, KD * (n + 1))
            for t, (s0_, _) in enumerate(STAT):
                ins = mm(bank[4][:, t:t + 1], ssum[:, s0_:s0_ + 128], ones[:, 0:1], start=True, stop=True)
            ins.then_inc(stat_psum, 1)
            if meanwhile:
                meanwhile()
            pe.wait_ge(rinv_ready, n + 1)
            for t, (t0, sz) in enumerate(TOK):
                r = slice(STAT[t][1], 128)
                ins = mm(bank[4][:, t0:t0 + sz], rcol[r, t:t + 1].broadcast_to([sz, 128]), ident[r, r],
                         start=True, stop=True)
            ins.then_inc(spread_psum, 1)

        pe.wait_ge(first_ready, 3)
        pe.wait_ge(rows_in, 64)
        nc.tensor.transpose(bank[7][:, 0:NROW], prow[:], ident[0:NROW, 0:NROW]).then_inc(prm_psum, 1)
        pe.wait_ge(x_in[0], 16)
        pe.wait_ge(x_in[1], 16)
        for j in range(KD):
            if j >= 4:
                pe.wait_ge(h_ready, j - 3)
            for t, (t0, sz) in enumerate(TOK):
                ins = nc.tensor.transpose(bank[j % 4][:, t0:t0 + sz], xt[0:sz, t, 128 * j:128 * j + 128],
                                          ident[0:sz, 0:sz])
            ins.then_inc(xt_psum, 1)
        mean_square(0)
        pe.wait_ge(h_ready, KD)

        for L in range(LAYERS):
            if L:
                mean_square(2 * L)
            ns = 2 * L

            def normed(k, ns=ns):
                pe.wait_ge(xh_ready, KD * ns + k + 1)
                pe.wait_ge(xl_ready, KD * ns + k + 1)

            def spread_out(L=L):
                pe.wait_ge(orinv_ready, L + 1)
                for hd in range(H):
                    for t, (t0, sz) in enumerate(TOK):
                        r = slice(STAT[t][1], 128)
                        ins = mm(bank[4 + hd][:, t0:t0 + sz], orc[r, hd, t:t + 1].broadcast_to([sz, 128]),
                                 ident[r, r], start=True, stop=True)
                    ins.then_inc(ospread_psum, 1)

            for i, (sec, part) in enumerate(MIX):
                c = base(L) + i
                if sec in ("value", "v"):
                    row_products(L, sec, c, part)
                elif sec == "branch_a":
                    products(L, sec, c, range(4 * part, 4 * part + 4), True, True, ahi, alo,
                             ready=lambda k: (pe.wait_ge(a_low, H * L + k + 1)))
                elif sec == "branch_b":
                    products(L, sec, c, range(4 * part, 4 * part + 4), True, True, bhi, blo,
                             ready=lambda k: (pe.wait_ge(b_low, H * L + k + 1)))
                elif sec == "w_out":
                    products(L, sec, c, (2 * part, 2 * part + 1), True, True, xh, xl,
                             ready=lambda k: (pe.wait_ge(merged_low, KD * L + k + 1)))
                else:
                    products(L, sec, c, (2 * part, 2 * part + 1), True, True, xh, xl,
                             ready=normed if i == 0 else None, between=spread_out if i == B_AT else None)
                if i == 0:
                    pe.wait_ge(layer_in, 64 * (L + 1))
                    pe.wait_ge(prm_ready, 1)
                    if L:
                        pe.wait_ge(b_ready, H * L)
                    for g in range(H):
                        ins = nc.tensor.transpose(bank[7][:, 128 * g:128 * g + 128], wsp[:, g, :], ident[:])
                    ins.then_inc(wst_psum, 1)
                if i == 1:
                    pe.wait_ge(wst_ready, L + 1)
                    pe.wait_ge(consts_ready, 1)
                    for g in range(H):
                        ins = mm(bank[7][0:64, 64 * g:64 * g + 64], r8[:],
                                 wst[0:LS, g, 0:LS].unsqueeze(1).broadcast_to([LS, NSEQ, LS]), start=True, stop=True)
                    ins.then_inc(wsd_psum, 1)
                if i == TURN_AT:
                    pe.wait_ge(kdec_ready, L + 1)
                    pe.wait_ge(score_ready, score_count(L, 1))
                    for t, (t0, sz) in enumerate(TOK):
                        for hd in range(H):
                            ins = nc.tensor.transpose(bank[4 + t][0:sz, 128 * hd:128 * hd + 128],
                                                      Z[:, hd, t0:t0 + sz], ident[:])
                        ins.then_inc(kdt_psum, 1)
                if i == DIAGONAL_AT or SCORES_AT < i <= SCORES_AT + NLEV:
                    li = max(0, i - SCORES_AT)
                    if li == 0:
                        pe.wait_ge(qdec_ready, L + 1)
                        pe.wait_ge(key_ready, L + 1)
                        lhs, rhs = K, Q
                    else:
                        pe.wait_ge(kdt_ready, NT * (L + 1))
                        pe.wait_ge(lev_prod, NLEV * L + li)
                        pe.wait_ge(score_ready, score_count(L, li))
                        lhs, rhs = Z, Z
                    lv = ([0] + LEVELS)[li]
                    for p in range(SCORES if lv <= LS // 2 else PAIRS):
                        t0, sz = TOK[p]
                        for hd in range(H):
                            ins = mm(bank[4 + p][0:sz, sz * hd:sz * hd + sz], lhs[:, hd, t0:t0 + sz],
                                     rhs[:, hd, t0:t0 + sz], start=True, stop=True)
                        ins.then_inc(score_psum, 1)
                if MIX_AT <= i < MIX_AT + H:
                    g = i - MIX_AT
                    if g == 0:
                        pe.wait_ge(vn_ready, NT * (L + 1))
                        pe.wait_ge(wsd_ready, H * (L + 1))
                    else:
                        pe.wait_ge(a_ready, H * L + g)
                    for t, (t0, sz) in enumerate(TOK):
                        w = wst[:, g, :] if t < PAIRS else wsd[:, g, :]
                        ins = mm(bank[7][:, t0:t0 + sz], vn[0:sz, t, 128 * g:128 * g + 128], w, start=True, stop=True)
                    ins.then_inc(mix_psum, 1)
                if i == STATES_AT:
                    pe.wait_ge(score_ready, NSCORE * (L + 1))
                    pe.wait_ge(a_ready, H * (L + 1))
                    for n in range(NPC):
                        p0 = CH * (n % 2)
                        for hd in range(H):
                            cs = slice(128 * hd, 128 * hd + 128)
                            ins = mm(bank[4 + n][:, cs], kdt[p0:p0 + CH, n // 2, cs], V[p0:p0 + CH, n // 2, cs],
                                     start=True, stop=True)
                        ins.then_inc(upd_psum, 1)
                if i == OUT_AT:
                    pe.wait_ge(state_ready, NPC * (L + 1))
                    for hd in range(H):
                        b = bank[4 + hd]
                        cs = slice(128 * hd, 128 * hd + 128)
                        for p in range(PAIRS):
                            mm(b[:, 128 * p:128 * p + 128], V[:, p, cs], sc[:, p, hd, :], start=p == 0, stop=False)
                        for n in range(1, NPC):
                            S = (S12 if n - 1 < 2 else S34)[:, (n - 1) % 2]
                            mm(b[:, CH * n:CH * n + CH], S[:, hd], QE[:, hd, CH * n:CH * n + CH], start=False, stop=False)
                        mm(b[:, TP:T], V[0:64, PAIRS, cs], scs[:, hd, :], start=False, stop=True).then_inc(o_psum, 1)
                if SAMPLE_AT <= i < SAMPLE_AT + H:
                    hd = i - SAMPLE_AT
                    cs = slice(128 * hd, 128 * hd + 128)
                    st = s0[hd]
                    pe.wait_ge(s0_in[hd], 16 * (L + 1))
                    if hd:
                        pe.wait_ge(s0_ready, H * L + hd)
                    else:
                        pe.wait_ge(o_ready, H * (L + 1))
                    for b in range(NSEQ):
                        ins = mm(bank[6][:, LS * b:LS * b + LS], st[:, b, :], QE[:, hd, TP + LS * b:TP + LS * b + LS],
                                 start=b == 0, stop=b == NSEQ - 1, skip_group_check=True)
                    ins.then_inc(so_psum, 1)
                    pe.wait_ge(vex_ready, H * L + hd + 1)
                    for b in (0, 1):
                        ins = mm(bank[4 + b][:], kdt[0:64, PAIRS, cs], vex[:, 4 * b:4 * b + 4, :], start=True, stop=True)
                    ins.then_inc(su_psum, 1)
                if SAMPLE_AT < i <= SAMPLE_AT + H:
                    hd = i - SAMPLE_AT - 1
                    pe.wait_ge(osq_ready, H * L + hd + 1)
                    for t, (s0_, _) in enumerate(STAT):
                        n = NT * hd + t
                        ins = mm(bank[7][:, n:n + 1], sq[:, hd % 2, s0_:s0_ + 128], ones[:, 0:1], start=True, stop=True)
                    ins.then_inc(ostat_psum, 1)
            if L % 2 == 0:
                mean_square(2 * L + 1)
                ns = 2 * L + 1

                def normed(k, ns=ns):
                    pe.wait_ge(xh_ready, KD * ns + k + 1)
                    pe.wait_ge(xl_ready, KD * ns + k + 1)

                for i, (sec, part) in enumerate(FFN):
                    c = first_chunk[(L, "gate")] + i
                    if sec == "down":
                        k0, kt = KCUT[part % 3]
                        t = 2 * (part // 3)
                        products(L, sec, c, (t, t + 1), part % 3 == 0, part % 3 == 2, fh, fl, k0=k0,
                                 ready=lambda k, k0=k0: pe.wait_ge(hid_low, k0 + k + 1))
                    else:
                        products(L, sec, c, (2 * part, 2 * part + 1), True, True, xh, xl,
                                 ready=normed if i == 0 else None)

        def turn_rows(src, psum, free):
            for n, (t, hf_) in enumerate(OUTS):
                t0, sz = TOK[t]
                if free:
                    pe.wait_ge(free, n + 1)
                for k in range(4):
                    ins = nc.tensor.transpose(bank[ROW_BANK[n]][0:sz, 128 * k:128 * k + 128],
                                              src[:, 4 * hf_ + k, t0:t0 + sz], ident[:])
                ins.then_inc(psum, 1)

        pe.wait_ge(dve_emptied, emptied["dve"])
        mean_square(2 * LAYERS - 1, meanwhile=lambda: turn_rows(h, sum_psum, None))
        pe.wait_ge(router_in, 16)
        for k in range(KD):
            pe.wait_ge(xn_ready, KD * (2 * LAYERS - 1) + k + 1)
            ins = mm(bank[7][0:NE, 0:T], rw[:, k, :], xn[:, k, :], start=k == 0, stop=k == KD - 1)
        ins.then_inc(lgt_psum, 1)
        pe.wait_ge(lgt_ready, 1)
        for t, (t0, sz) in enumerate(TOK):
            ins = nc.tensor.transpose(bank[7][0:sz, NE * t:NE * t + NE], lgt[:, t0:t0 + sz], ident[0:NE, 0:NE])
        ins.then_inc(logit_psum, 1)
        turn_rows(xn, hn_psum, sum_done)
        pe.wait_ge(chosen_ready, 1)
        for t, (_, sz) in enumerate(TOK):
            for q in range(t):
                mm(bank[7][0:sz, NE * t:NE * t + NE], ones[:, 0:sz], mk[:, q, :], start=q == 0, stop=False)
            mm(bank[7][0:sz, NE * t:NE * t + NE], upper[0:sz, 0:sz], mk[0:sz, t, :], start=t == 0, stop=True)
        for t, (_, sz) in enumerate(TOK):
            ins = mm(bank[7][:, NE * NT:NE * NT + NE], ones[0:sz, :], mk[0:sz, t, :], start=t == 0, stop=t == NT - 1)
        ins.then_inc(rank_psum, 1)

        def gather(item):
            pe.wait_ge(pick_ready, item + 1)
            for hh in range(2):
                for k in range(4):
                    for t, (_, sz) in enumerate(TOK):
                        kk = 4 * hh + k
                        ins = mm(bank[6 + hh][:, 128 * k:128 * k + 128], hn[0:sz, t, 128 * kk:128 * kk + 128],
                                 pick[0:sz, t, :], start=t == 0, stop=t == NT - 1)
                ins.then_inc(xg_psum, 1)

        def hidden_rows_turned(item, j):
            pe.wait_ge(he_ready, NG * item + (j + 1))
            if j == 1:
                pe.wait_ge(pickt_ready, item + 1)
            if j >= 2:
                pe.wait_ge(hel_ready, NG * item + (j - 1))
            for n, t in enumerate(group_tiles(j)):
                ins = nc.tensor.transpose(bank[4 + j % 2][:, 128 * n:128 * n + 128], He[:, 128 * t:128 * t + 128], ident[:])
            ins.then_inc(het_psum, 1)

        def chunk(item, i, ahead):
            if i >= NEC:
                item, i = item + 1, i - NEC
            kind, j, part, k0, kt, c0, cols = ECH[i]
            if kind == "down" and j == 0:
                pe.wait_ge(he_ready, NG * item + (NG if ahead else NG - 1))
            for half in range(2):
                p = 2 * i + half
                pe.wait_ge(low_done, 2 * NEC * item + (2 * NDENSE + p + 1))
                if kind != "down" and part == 0 and half == 0:
                    if j == 1:
                        pe.wait_ge(sum_done, NO * item + (1 if kind == "gate" else 2))
                    elif j > 1:
                        pe.wait_ge(gate_emptied if kind == "gate" else he_ready, NG * item + (j - 1))
                for q in range(kt // 2):
                    kk = k0 + half * (kt // 2) + q
                    if kind == "down":
                        if kk % 4 == 0:
                            pe.wait_ge(hel_ready, NG * item + (kk // 4 + 1))
                        for hh in range(2):
                            w = slice(q * cols + 512 * hh, q * cols + 512 * hh + 512)
                            mm(bank[down_bank(ahead) + hh][:], heh[:, kk, :], whi[:, p % RING, w], start=kk == 0, stop=False)
                            mm(bank[down_bank(ahead) + hh][:], heh[:, kk, :], wlo[:, p % RING, w], start=False, stop=False)
                            ins = mm(bank[down_bank(ahead) + hh][:], hel[:, kk, :], whi[:, p % RING, w], start=False,
                                     stop=kk == KF - 1)
                    else:
                        if j == 0 and kk % 4 == 0:
                            pe.wait_ge(xg_low, 2 * item + (kk // 4 + 1))
                        b = bank[(kind == "up") + 2 * (j % 2)]
                        w = slice(q * cols, (q + 1) * cols)
                        mm(b[:, 0:cols], xeh[:, kk, :], whi[:, p % RING, w], start=kk == 0, stop=False)
                        mm(b[:, 0:cols], xeh[:, kk, :], wlo[:, p % RING, w], start=False, stop=False)
                        ins = mm(b[:, 0:cols], xel[:, kk, :], whi[:, p % RING, w], start=False, stop=kk == KD - 1)
                ins.then_inc(pe_mark, 1)
            if kind == "up" and i == closing[(kind, j)]:
                if j == 1:
                    pe.wait_ge(sum_done, NO * item + NO)
                    for t, (t0, sz) in enumerate(TOK):
                        ins = nc.tensor.transpose(bank[5][:, t0:t0 + sz], pick[0:sz, t, :], ident[0:sz, 0:sz])
                    ins.then_inc(pickt_psum, 1)
                if j:
                    hidden_rows_turned(item, j - 1)
                if j == NG - 1:
                    if ahead:
                        gather(item + 1)
                        hidden_rows_turned(item, j)
            if kind == "down" and j == 0 and not ahead:
                hidden_rows_turned(item, NG - 1)

        def scatter(item, ahead):
            pe.wait_ge(pickt_ready, item + 1)
            pe.wait_ge(y_low, 2 * item + 2)
            pe.wait_ge(hel_ready, NG * item + NG)
            if not ahead:
                pe.wait_ge(he_ready, NG * item + NG)
            if ahead:
                pe.wait_ge(xg_low, 2 * item + 4)
            for n, (t, hf_) in enumerate(OUTS):
                t0, sz = TOK[t]
                w = slice(512 * hf_, 512 * hf_ + 512)
                mm(bank[SUM_BANK[n]][0:sz, :], pickt[:, t0:t0 + sz], Yh[:, w], start=True, stop=False)
                mm(bank[SUM_BANK[n]][0:sz, :], pickt[:, t0:t0 + sz], Yl[:, w], start=False, stop=True).then_inc(
                    sum_psum, 1)

        def extra(item, n):
            pe.wait_ge(sum_done, NO * item + NO)
            gather(item)
            for i in range(NEC):
                chunk(item, i, False)
            scatter(item, False)

        pe.wait_ge(y_ready, NO)
        pe.wait_ge(sum_done, NO)
        gather(0)
        for i in range(HEAD):
            chunk(0, i, True)
        with pe.Fori(0, NE - 1) as e:
            for i in range(HEAD, HEAD + NEC):
                chunk(e, i, True)
            scatter(e, True)
        for i in range(HEAD, NEC):
            chunk(NE - 1, i, False)
        scatter(NE - 1, False)
        extra_blocks(pe, extra)

    ctx.close()


_OUTS = {"y_prompt": (1, 256, 1024), "y_sample": (8, 8, 1024), "prompt_state": (2, 1, 4, 128, 128),
         "sample_state": (2, 8, 4, 128, 128), "v_rows": (2, 8, 8, 512)}


def kernel(**inputs):
    import numpy as np
    import concourse.bacc as bacc
    from concourse.bass_utils import run_bass_kernel_spmd

    nc = bacc.Bacc("TRN2", target_bir_lowering=False, num_devices=1)
    arrays, ins, outs = {}, {}, {}
    for name, a in inputs.items():
        arrays["in_" + name] = np.ascontiguousarray(a)
        ins[name] = nc.dram_tensor("in_" + name, a.shape, mybir.dt.float32, kind="ExternalInput").ap()
    for name, shape in _OUTS.items():
        outs[name] = nc.dram_tensor("out_" + name, shape, mybir.dt.float32, kind="ExternalOutput").ap()
    hybrid_trunk_program(nc, ins, outs)
    r = run_bass_kernel_spmd(nc, [arrays], core_ids=[0])
    return tuple(r.results[0]["out_" + name] for name in _OUTS)
```
